# Optimizing a Trainium2 kernel written in Bass

```python
import jax, jax.numpy as jnp
from jax import lax
import numpy as np

D_MODEL = 1024
BATCH = 1
SEQ = 512
DEPTH = 2

D_FF = 2816
N_MOD = 9
SSD_INNER = 1024
SSD_HEADDIM = 64
SSD_HEADS = SSD_INNER // SSD_HEADDIM
SSD_GROUPS = 2
SSD_STATE = 128
SSD_CONV = 5
SSD_CHUNK = 128
CONV_CH = SSD_INNER + 2 * SSD_GROUPS * SSD_STATE
MLA_HEADS = 8
QK_NOPE = 128
QK_ROPE = 64
V_DIM = 128
Q_LORA = 512
KV_LORA = 256
ATTN_WIDTH = MLA_HEADS * V_DIM
Q_BLOCK = 128
ROPE_THETA = 10000.0
IN_SPLITS = (SSD_INNER, CONV_CH, 2 * SSD_HEADS, Q_LORA, KV_LORA + QK_ROPE)
IN_COLS = sum(IN_SPLITS)
MIX_WIDTH = SSD_INNER + ATTN_WIDTH
EPS = 1e-6

kernel_name = 'hybrid_ssd_mla_macaron_encoder'

def rmsnorm(x, g):
    xf = x.astype(jnp.float32)
    y = xf * lax.rsqrt(jnp.mean(xf * xf, axis=-1, keepdims=True) + EPS)
    return (y * g.astype(jnp.float32)).astype(x.dtype)

def modulate(x, g, shift, scale):
    return rmsnorm(x, g) * (1.0 + scale[:, None, :]) + shift[:, None, :]

def swiglu(h, w_gate, w_up, w_down):
    return (jax.nn.silu(h @ w_gate) * (h @ w_up)) @ w_down

def dwconv_centred(u, w, b):
    k, ch = w.shape
    out = lax.conv_general_dilated(
        u, w.astype(u.dtype)[:, None, :], window_strides=(1,),
        padding=[(k // 2, k // 2)], dimension_numbers=('NWC', 'WIO', 'NWC'),
        feature_group_count=ch)
    return out + b

def rope(t, cos, sin):
    half = t.shape[-1] // 2
    t1, t2 = t[..., :half], t[..., half:]
    return jnp.concatenate([t1 * cos - t2 * sin, t2 * cos + t1 * sin], axis=-1).astype(t.dtype)

def ssd_chunked(xh, dt, a, bm, cm):
    b, s, h, p = xh.shape
    g, n = bm.shape[2], bm.shape[3]
    e = h // g
    nc, l = s // SSD_CHUNK, SSD_CHUNK
    x_dt = (xh.astype(jnp.float32) * dt[..., None]).reshape(b, nc, l, g, e, p)
    a_dt = (dt * a).reshape(b, nc, l, g, e)
    bc = bm.astype(jnp.float32).reshape(b, nc, l, g, n)
    cc = cm.astype(jnp.float32).reshape(b, nc, l, g, n)
    a_cs = jnp.cumsum(a_dt, axis=2)
    diff = a_cs[:, :, :, None] - a_cs[:, :, None, :]
    mask = jnp.tril(jnp.ones((l, l), dtype=bool))[:, :, None, None]
    decay = jnp.exp(jnp.where(mask, diff, -jnp.inf))
    cb = jnp.einsum('bclgn,bcsgn->bclsg', cc, bc)
    y_diag = jnp.einsum('bclsge,bcsgep->bclgep', cb[..., None] * decay, x_dt)
    decay_to_end = jnp.exp(a_cs[:, :, -1:] - a_cs)
    chunk_states = jnp.einsum('bclgn,bclgep->bcgepn', bc, x_dt * decay_to_end[..., None])
    chunk_decay = jnp.exp(a_cs[:, :, -1])

    def step(state, inp):
        st, dec = inp
        return dec[..., None, None] * state + st, state

    init = jnp.zeros((b, g, e, p, n), jnp.float32)
    _, states_in = lax.scan(step, init, (jnp.moveaxis(chunk_states, 1, 0), jnp.moveaxis(chunk_decay, 1, 0)))
    states_in = jnp.moveaxis(states_in, 0, 1)
    y_off = jnp.einsum('bclgn,bcgepn->bclgep', cc, states_in) * jnp.exp(a_cs)[..., None]
    return (y_diag + y_off).reshape(b, s, h, p)

def mla_attention(h_qa, h_kva, q_norm_g, w_q_b, kv_norm_g, w_kv_b, cos, sin):
    b, s, _ = h_qa.shape
    q = (rmsnorm(h_qa, q_norm_g) @ w_q_b).reshape(b, s, MLA_HEADS, QK_NOPE + QK_ROPE)
    q_nope = q[..., :QK_NOPE]
    q_rope = rope(q[..., QK_NOPE:], cos[:, :, None, :], sin[:, :, None, :])
    c_kv = rmsnorm(h_kva[..., :KV_LORA], kv_norm_g)
    k_rope = rope(h_kva[..., KV_LORA:], cos, sin)
    kv = (c_kv @ w_kv_b).reshape(b, s, MLA_HEADS, QK_NOPE + V_DIM)
    k_nope, v = kv[..., :QK_NOPE], kv[..., QK_NOPE:]
    scale = (QK_NOPE + QK_ROPE) ** -0.5
    nb = s // Q_BLOCK

    def to_blocks(t):
        return jnp.moveaxis(t.reshape(b, nb, Q_BLOCK, *t.shape[2:]), 1, 0)

    def attend(qb):
        qn, qr = qb
        sc = jnp.einsum('bqhd,bkhd->bhqk', qn, k_nope) + jnp.einsum('bqhr,bkr->bhqk', qr, k_rope)
        pr = jax.nn.softmax(sc.astype(jnp.float32) * scale, axis=-1).astype(v.dtype)
        return jnp.einsum('bhqk,bkhd->bqhd', pr, v)

    o = lax.map(attend, (to_blocks(q_nope), to_blocks(q_rope)))
    return jnp.moveaxis(o, 0, 1).reshape(b, s, ATTN_WIDTH)

def hybrid_mixer(h, w_in, conv_w, conv_b, dt_bias, a_log, d_skip, ssd_norm_g,
                 q_norm_g, w_q_b, kv_norm_g, w_kv_b, attn_norm_g, w_out, cos, sin):
    b, s, _ = h.shape
    cuts = [int(i) for i in np.cumsum(IN_SPLITS)[:-1]]
    z, xbc, dt_raw, h_qa, h_kva = jnp.split(h @ w_in, cuts, axis=-1)
    xbc = jax.nn.silu(dwconv_centred(xbc, conv_w, conv_b))
    xs, bm, cm = jnp.split(xbc, [SSD_INNER, SSD_INNER + SSD_GROUPS * SSD_STATE], axis=-1)
    xh = xs.reshape(b, s, SSD_HEADS, SSD_HEADDIM)
    bm = bm.reshape(b, s, SSD_GROUPS, SSD_STATE)
    cm = cm.reshape(b, s, SSD_GROUPS, SSD_STATE)
    dt = jax.nn.softplus(dt_raw.astype(jnp.float32).reshape(b, s, 2, SSD_HEADS) + dt_bias.astype(jnp.float32))
    a = -jnp.exp(a_log.astype(jnp.float32))
    y_fwd = ssd_chunked(xh, dt[:, :, 0], a[0], bm, cm)
    flip = lambda t: jnp.flip(t, axis=1)
    y_bwd = flip(ssd_chunked(flip(xh), flip(dt[:, :, 1]), a[1], flip(bm), flip(cm)))
    y = y_fwd + y_bwd + d_skip.astype(jnp.float32)[:, None] * xh.astype(jnp.float32)
    y = y.reshape(b, s, SSD_INNER) * jax.nn.silu(z.astype(jnp.float32))
    y = rmsnorm(y.reshape(b, s, SSD_GROUPS, SSD_INNER // SSD_GROUPS),
                ssd_norm_g.reshape(SSD_GROUPS, SSD_INNER // SSD_GROUPS))
    ssd_out = y.reshape(b, s, SSD_INNER).astype(h.dtype)
    attn_out = rmsnorm(mla_attention(h_qa, h_kva, q_norm_g, w_q_b, kv_norm_g, w_kv_b, cos, sin), attn_norm_g)
    return jnp.concatenate([ssd_out, attn_out.astype(h.dtype)], axis=-1) @ w_out

def setup_inputs(seed: int = 0) -> dict:
    key = jax.random.key(seed)
    ks = jax.random.split(key, 24)
    nrm = lambda k, shape, sc: jax.random.normal(k, shape, jnp.float32) * sc
    gain = lambda k, shape: 1.0 + 0.02 * jax.random.normal(k, shape, jnp.float32)
    x = nrm(ks[0], (BATCH, SEQ, D_MODEL), 1.0)
    c = nrm(ks[1], (BATCH, D_MODEL), 1.0)
    offset = jax.random.randint(ks[2], (BATCH, 1), 0, 1024, dtype=jnp.int32)
    positions = (offset + jnp.arange(SEQ, dtype=jnp.int32)[None, :]).astype(jnp.int32)
    ada_w = nrm(ks[3], (DEPTH, D_MODEL, N_MOD * D_MODEL), 0.5 * D_MODEL ** -0.5)
    ada_b = nrm(ks[4], (DEPTH, N_MOD * D_MODEL), 0.01)
    norm_g = gain(ks[5], (DEPTH, 3, D_MODEL))
    ffn_w_gate = nrm(ks[6], (DEPTH, 2, D_MODEL, D_FF), D_MODEL ** -0.5)
    ffn_w_up = nrm(ks[7], (DEPTH, 2, D_MODEL, D_FF), D_MODEL ** -0.5)
    ffn_w_down = nrm(ks[8], (DEPTH, 2, D_FF, D_MODEL), D_FF ** -0.5)
    w_in = nrm(ks[9], (DEPTH, D_MODEL, IN_COLS), D_MODEL ** -0.5)
    conv_w = nrm(ks[10], (DEPTH, SSD_CONV, CONV_CH), SSD_CONV ** -0.5)
    conv_b = nrm(ks[11], (DEPTH, CONV_CH), 0.01)
    dt0 = jnp.exp(jax.random.uniform(ks[12], (DEPTH, 2, SSD_HEADS), jnp.float32, np.log(1e-3), np.log(1e-1)))
    dt_bias = dt0 + jnp.log(-jnp.expm1(-dt0))
    a_log = jnp.log(jax.random.uniform(ks[13], (DEPTH, 2, SSD_HEADS), jnp.float32, 1.0, 16.0))
    d_skip = gain(ks[14], (DEPTH, SSD_HEADS))
    ssd_norm_g = gain(ks[15], (DEPTH, SSD_INNER))
    q_norm_g = gain(ks[16], (DEPTH, Q_LORA))
    w_q_b = nrm(ks[17], (DEPTH, Q_LORA, MLA_HEADS * (QK_NOPE + QK_ROPE)), Q_LORA ** -0.5)
    kv_norm_g = gain(ks[18], (DEPTH, KV_LORA))
    w_kv_b = nrm(ks[19], (DEPTH, KV_LORA, MLA_HEADS * (QK_NOPE + V_DIM)), KV_LORA ** -0.5)
    attn_norm_g = gain(ks[20], (DEPTH, ATTN_WIDTH))
    w_out = nrm(ks[21], (DEPTH, MIX_WIDTH, D_MODEL), MIX_WIDTH ** -0.5)
    final_norm_g = gain(ks[22], (D_MODEL,))
    return {'x': x, 'c': c, 'positions': positions, 'ada_w': ada_w, 'ada_b': ada_b,
            'norm_g': norm_g, 'ffn_w_gate': ffn_w_gate, 'ffn_w_up': ffn_w_up,
            'ffn_w_down': ffn_w_down, 'w_in': w_in, 'conv_w': conv_w, 'conv_b': conv_b,
            'dt_bias': dt_bias, 'a_log': a_log, 'd_skip': d_skip, 'ssd_norm_g': ssd_norm_g,
            'q_norm_g': q_norm_g, 'w_q_b': w_q_b, 'kv_norm_g': kv_norm_g, 'w_kv_b': w_kv_b,
            'attn_norm_g': attn_norm_g, 'w_out': w_out, 'final_norm_g': final_norm_g}

def reference(x, c, positions, ada_w, ada_b, norm_g, ffn_w_gate, ffn_w_up, ffn_w_down,
              w_in, conv_w, conv_b, dt_bias, a_log, d_skip, ssd_norm_g, q_norm_g, w_q_b,
              kv_norm_g, w_kv_b, attn_norm_g, w_out, final_norm_g):
    b, s, d = x.shape
    inv_freq = 1.0 / (ROPE_THETA ** (jnp.arange(0, QK_ROPE, 2, dtype=jnp.float32) / QK_ROPE))
    ang = positions.astype(jnp.float32)[..., None] * inv_freq
    cos, sin = jnp.cos(ang), jnp.sin(ang)
    c_act = jax.nn.silu(c)
    for l in range(DEPTH):
        mod = (c_act @ ada_w[l] + ada_b[l]).reshape(b, N_MOD, d)
        h = modulate(x, norm_g[l, 0], mod[:, 0], mod[:, 1])
        x = x + 0.5 * mod[:, 2][:, None, :] * swiglu(h, ffn_w_gate[l, 0], ffn_w_up[l, 0], ffn_w_down[l, 0])
        h = modulate(x, norm_g[l, 1], mod[:, 3], mod[:, 4])
        x = x + mod[:, 5][:, None, :] * hybrid_mixer(
            h, w_in[l], conv_w[l], conv_b[l], dt_bias[l], a_log[l], d_skip[l], ssd_norm_g[l],
            q_norm_g[l], w_q_b[l], kv_norm_g[l], w_kv_b[l], attn_norm_g[l], w_out[l], cos, sin)
        h = modulate(x, norm_g[l, 2], mod[:, 6], mod[:, 7])
        x = x + 0.5 * mod[:, 8][:, None, :] * swiglu(h, ffn_w_gate[l, 1], ffn_w_up[l, 1], ffn_w_down[l, 1])
    return rmsnorm(x, final_norm_g)


_drawn_inputs = setup_inputs


def setup_inputs(seed=0):
    import zlib

    import numpy as np

    out = dict(_drawn_inputs(seed))
    spreads = {}
    factors = {'ada_b': 2.959,
     'norm_g': 5.49,
     'conv_b': 8.0,
     'd_skip': 8.0,
     'ssd_norm_g': 8.0,
     'q_norm_g': 8.0,
     'kv_norm_g': 8.0,
     'attn_norm_g': 8.0,
     'final_norm_g': 2.846}
    for name, (base, spread) in spreads.items():
        noise = np.random.default_rng([zlib.crc32(name.encode()), seed]).standard_normal(out[name].shape)
        drawn = base * np.exp(spread * noise) if base else spread * noise
        out[name] = __import__('jax').numpy.asarray(drawn.astype(out[name].dtype))
    for name, factor in factors.items():
        out[name] = (out[name] * factor).astype(out[name].dtype)
    return out
```

```python
from contextlib import ExitStack

import numpy as np

import concourse.bass as bass
from concourse import mybir

F32 = mybir.dt.float32
F32R = mybir.dt.float32r
I32 = mybir.dt.int32
ACT = mybir.ActivationFunctionType
ALU = mybir.AluOpType
AXX = mybir.AxisListType.X

P = 128
DEPTH = 2
SEQ = 512
DM = 1024
DFF = 2816
KC = DM // P
FC = DFF // P
TC = SEQ // P
HEADS = 16
HD = 64
GRP = 2
NST = 128
KSZ = 5
CCH = (DM + 2 * GRP * NST) // P
MH = 8
NOPE, ROPE, VD = 128, 64, 128
QL, KVL = 512, 256
QC, KVC = QL // P, KVL // P
EPS = 1e-6
ATT_SCALE = float(NOPE + ROPE) ** -0.5
THETA = 10000.0

ITEM = 8 * P
UP_ITEMS = 2 * FC
DN_PER = 3
DN_ITEMS = KC * DN_PER
MX_ITEMS = 1 + CCH + 8 + QC + KVC + 1 + KC + 2 * 5 + KC
FF_ITEMS = UP_ITEMS + DN_ITEMS
NI = 2 * FF_ITEMS + MX_ITEMS
assert NI % 2 == 0 and FF_ITEMS % 2 == 0
TR = [0, 1] + list(range(4, CCH))
I_DT, I_CONV, I_Z = 0, 1, 1 + CCH
I_QA = I_Z + 8
I_KV = I_QA + QC
I_KR = I_KV + KVC
I_OS = I_KR + 1
I_MLA = I_OS + KC
I_OA = I_MLA + 10

P_CW = 0
P_CB = P_CW + CCH * KSZ
P_NG = P_CB + CCH
P_SG = P_NG + 3 * KC
P_QG = P_SG + KC
P_KG = P_QG + QC
P_AG = P_KG + KVC
P_AB = P_AG + KC
P_DB = P_AB + 72
P_AL = P_DB + 2 * HEADS
P_DS = P_AL + 2 * HEADS
NPAR = P_DS + HEADS

DVE_STEPS = 196
ADA_Q = 24

PRO_ANGLES = 12
TWO_PI = 2 * np.pi
C1 = 6.28125
C2 = float(np.array([np.array([TWO_PI - C1], np.float32).view(np.int32)[0] & -4096], np.int32).view(np.float32)[0])
C3 = float(TWO_PI - C1 - C2)
ROUND = 1.5 * 2.0 ** 23
PI_IN = 3.1415925


class Signal:

    def __init__(self, sem, per, first=0):
        self.sem, self.per, self.first = sem, per, first

    def at(self, layer, n):
        return layer * self.per + (self.first + n)


class Chain:

    def __init__(self, eng, sig, layer):
        self.eng, self.sig, self.layer, self.n = eng, sig, layer, 0

    def __call__(self, ins):
        ins.then_inc(self.sig.sem, 1)
        self.n += 1
        self.eng.wait_ge(self.sig.sem, self.sig.at(self.layer, self.n))


def build_trunk(nc, xT, cT, pos, invf, consts, params, finalg, w_up, w_dn, w_mx, w_ada, out):
    ctx = ExitStack()
    base = -(-nc.sbuf_base // 32) * 32
    top = [base]

    def at(name, shape, dt, off):
        return nc.alloc_sbuf_tensor_at(name, shape, dt, offset=off)

    def sb(name, shape, dt=F32):
        size = 4
        for d in shape[1:]:
            size *= d
        off = top[0]
        top[0] += -(-size // 32) * 32
        return at(name, shape, dt, off)

    x = sb("x_res", [P, KC, SEQ])
    hH = sb("h_hi", [P, KC, SEQ], F32R)
    hL = sb("h_lo", [P, KC, SEQ], F32R)
    raw = [sb(f"w_raw{j}", [P, ITEM]) for j in range(2)]
    wH = [sb(f"w_hi{j}", [P, ITEM], F32R) for j in range(2)]
    wL = [sb(f"w_lo{j}", [P, ITEM], F32R) for j in range(2)]
    cst = sb("consts_sb", [P, 5, P])
    triU, triL, ones, ident, perm = (cst[:, i, :] for i in range(5))
    cosT = sb("cosT", [P, SEQ])
    sinT = sb("sinT", [P, SEQ])
    par = sb("par", [P, NPAR])
    fing = sb("fing", [P, KC])
    mod = sb("mod", [P, 3, 3, KC])
    csil = sb("csil", [P, KC])
    cin = sb("cin", [P, KC])
    invs = sb("invs", [P, 1])
    ms = sb("ms", [P, SEQ])
    rstd = sb("rstd", [P, SEQ])
    A0 = top[0]
    ada_in = sb("ada_in", [P, 3, DM])
    acc = sb("ada_acc", [P, 3, DM])
    R0 = top[0]
    K = 1024
    assert R0 + 92 * K <= nc.sbuf_usable_end, (R0, nc.sbuf_usable_end)

    ffH = at("ff_hi", [P, FC, SEQ], F32R, R0)
    ffL = at("ff_lo", [P, FC, SEQ], F32R, R0 + 44 * K)
    sg = at("silu_gate", [P, 2, SEQ], F32, R0 + 88 * K)
    prod = [ms, rstd]
    sq = at("squares", [P, KC, SEQ], F32, R0)

    rawq = at("q_kv_raw", [P, 7, SEQ], F32, R0)
    zs = at("silu_z", [P, TC, DM], F32, R0 + 14 * K)
    xtok = at("x_tok", [P, TC, DM], F32, R0 + 30 * K)
    dec = at("decay", [P, 2, HEADS, P], F32, R0 + 46 * K)
    cbuf = at("conv_acc", [P, 2, SEQ], F32, R0 + 46 * K)
    xs = at("x_feat", [P, 2, SEQ], F32, R0 + 50 * K)
    xdt = at("x_dt", [P, 2, DM], F32, R0 + 62 * K)
    xw = at("x_w", [P, DM], F32, R0 + 70 * K)
    yb = at("y_buf", [P, DM], F32, R0 + 74 * K)
    bfm = at("b_feat", [P, GRP, SEQ], F32, R0 + 74 * K)
    btok = at("b_tok", [P, TC, GRP * NST], F32, R0 + 78 * K)
    sf = at("state_f", [P, DM], F32, R0 + 82 * K)
    yt = at("y_feat", [P, 4, P], F32, R0 + 86 * K)
    small = at("ssd_small", [P, 8, P], F32, R0 + 88 * K)
    dtt, adt, sxr, sab, sp1, sp2, uu, sea = (small[:, i, :] for i in range(8))
    cs3 = at("cs3", [P, 3, P], F32, R0 + 92 * K)
    assert R0 + 94 * K + 512 <= nc.sbuf_usable_end, (R0 + 94 * K + 512, nc.sbuf_usable_end)
    sbk = at("state_b", [P, 3, DM], F32, A0)
    cbm = at("cb_masked", [P, 2, TC, GRP, P], F32, A0 + 12 * K)
    cfm = at("c_feat", [P, GRP, SEQ], F32, A0 + 20 * K)
    csT = at("cs_rows", [HEADS, 2, SEQ], F32, R0 + 62 * K)
    ssq = at("y_ssq", [P, 8], F32, R0 + 92 * K + 1536)

    ofm = at("att_out", [P, MH, SEQ], F32, R0)
    qaH = at("qa_hi", [P, QC, SEQ], F32R, R0 + 16 * K)
    qaL = at("qa_lo", [P, QC, SEQ], F32R, R0 + 24 * K)
    ckH = at("ckv_hi", [P, KVC, SEQ], F32R, R0 + 32 * K)
    ckL = at("ckv_lo", [P, KVC, SEQ], F32R, R0 + 36 * K)
    krH = at("kr_hi", [P, SEQ], F32R, R0 + 40 * K)
    krL = at("kr_lo", [P, SEQ], F32R, R0 + 42 * K)
    kH = at("k_hi", [P, 4, SEQ], F32R, R0 + 44 * K)
    kL = at("k_lo", [P, 4, SEQ], F32R, R0 + 52 * K)
    vH = at("v_hi", [P, TC, 4 * VD], F32R, R0 + 60 * K)
    vL = at("v_lo", [P, TC, 4 * VD], F32R, R0 + 68 * K)
    qrH = at("qr_hi", [P, 2, SEQ], F32R, R0 + 76 * K)
    qrL = at("qr_lo", [P, 2, SEQ], F32R, R0 + 80 * K)
    qnH = at("qn_hi", [P, 2, SEQ], F32R, R0 + 84 * K)
    qnL = at("qn_lo", [P, 2, SEQ], F32R, R0 + 88 * K)
    asq = at("att_sq", [P, MH, SEQ], F32, R0 + 44 * K)
    ptH = at("pT_hi", [P, TC, SEQ], F32R, A0)
    ptL = at("pT_lo", [P, TC, SEQ], F32R, A0 + 8 * K)
    lsq = at("lora_sq", [P, 6, SEQ], F32, A0)
    pr = at("probs", [P, 2, SEQ], F32, A0 + 16 * K)
    rtmp = at("rope_tmp", [P, 2, SEQ], F32, A0 + 20 * K)
    sm = at("softmax_small", [P, 2, 4], F32, R0 + 92 * K)

    posi = at("pos_i", [P, SEQ], I32, R0)
    ang = at("ang", [P, SEQ], F32, R0 + 2 * K)
    kk = at("turns", [P, SEQ], F32, R0 + 4 * K)
    tmp = at("ang_tmp", [P, SEQ], F32, R0 + 6 * K)

    ps = ctx.enter_context(nc.psum_tensor("banks", [P, 8, SEQ], F32))
    cs_dram = nc.dram_tensor("cs_rows_dram", (2, HEADS, SEQ), F32, kind="Internal").ap()

    def sem(name, per=0, first=0):
        return Signal(ctx.enter_context(nc.semaphore(name)), per, first)

    go = sem("go")
    passed = {e: sem(f"passed_{e}") for e in ("gp", "dve", "pe")}
    w_land = [sem(f"w_land{j}", 16 * NI // 2) for j in range(2)]
    w_hi = sem("w_hi", NI)
    w_lo = sem("w_lo", NI, 2)
    w_used = sem("w_used", NI, 2)
    ada_land = [sem(f"ada_land{m}", 16 * ADA_Q, 16 * 8) for m in range(3)]
    ada_done = sem("ada_done", 3 * ADA_Q, ADA_Q + 3)
    acc_zero = sem("acc_zero", 3, 1)
    mod_sum = sem("mod_sum", 3)
    c_land = sem("c_land")
    x_land = sem("x_land")
    pos_land = sem("pos_land")
    par_land = sem("par_land", 16)
    csil_done = sem("csil_done")
    p_step = sem("prologue_step")
    trig_done = sem("trig_done")
    x_new = sem("x_new", 4 * KC, 2)
    sq_done = sem("sq_done", 3 * KC)
    n_sum = sem("n_sum", 3)
    ms_done = sem("ms_done", 3)
    rstd_done = sem("rstd_done", 3)
    u_done = sem("u_done", 3 * KC)
    h_hi = sem("h_hi_done", 3 * KC)
    h_lo = sem("h_lo_done", 3 * KC)
    sg_done = sem("sg_done", 2 * FC, 2)
    prod_done = sem("prod_done", 2 * FC, 2)
    ff_hi = sem("ff_hi_done", 2 * FC)
    ff_lo = sem("ff_lo_done", 2 * FC, 2)
    v_step = sem("v_step", DVE_STEPS)
    cen = sem("conv_centre", CCH)
    conv = sem("conv_done", CCH)
    csilu = sem("conv_silu", CCH)
    trx = sem("x_transposed", len(TR))
    tev = sem("x_tok_done", len(TR))
    z_ev = sem("z_done", 2 * TC)
    q_ev = sem("q_raw_done", 7)
    d_abs = sem("dt_abs", 1)
    d_exp = sem("dt_exp", 2)
    a_dt = sem("a_dt_done", 1)
    cs_mm = sem("cs_mm", 1)
    cs_cp = sem("cs_copied", 1)
    cs_out = sem("cs_stored", 32)
    cs_exp = sem("cs_exp", 1)
    u_w = sem("xw_done", 6)
    st_mm = sem("state_mm", 6)
    st_up = sem("state_done", 6)
    cb_mm = sem("cb_mm", 1)
    cb_ok = sem("cb_masked_done", 1)
    r_land = [sem(f"rows_land{d}", 16 * TC) for d in range(2)]
    d_dif = sem("dif_done", 2 * TC)
    d_ex = sem("decay_exp", 2 * TC)
    m_ok = sem("m_done", 2 * TC)
    yo_mm = sem("yoff_mm", TC)
    yd_mm = sem("ydiag_mm", TC)
    y_raw = sem("y_gated", TC)
    y_sq = sem("y_sq", 2 * TC)
    y_ms = sem("y_ms", TC)
    y_rs = sem("y_rs", TC)
    y_nm = sem("y_normed", 2 * TC)
    y_tr = sem("y_transposed", 2 * TC)
    y_f = sem("y_feat_done", 2 * TC)
    y_hi = sem("y_hi_done", 2 * TC)
    y_lo = sem("y_lo_done", 2 * TC)
    l_sq = sem("lora_sq_done", 6)
    l_sum = sem("lora_sum", 2)
    l_ms = sem("lora_ms", 2)
    l_rs = sem("lora_rstd", 2)
    l_u = sem("lora_u", 6)
    l_hi = sem("lora_hi", 6)
    l_lo = sem("lora_lo", 6)
    rp_in = sem("rope_in", 5)
    rp_mm = sem("rope_rot", 5)
    rp_out = sem("rope_out", 5)
    rp_hi = sem("rope_hi", 5)
    rp_lo = sem("rope_lo", 5)
    k_hi = sem("k_hi_done", MH)
    k_lo = sem("k_lo_done", MH)
    v_hi = sem("v_hi_done", 2 * TC)
    v_lo = sem("v_lo_done", 2 * TC)
    qn_hi = sem("qn_hi_done", MH)
    qn_lo = sem("qn_lo_done", MH)
    s_mm = sem("scores_mm", MH * TC)
    s_mx = sem("scores_max", MH * TC)
    s_ex = sem("probs_exp", MH * TC)
    s_nm = sem("probs_done", MH * TC)
    p_tr = sem("probs_T", MH * TC)
    p_hi = sem("pT_hi_done", MH * TC)
    p_lo = sem("pT_lo_done", MH * TC)
    o_mm = sem("o_mm", MH)
    o_ev = sem("o_done", MH)
    a_sq = sem("att_sq_done", MH)
    a_sum = sem("att_sum", 1)
    a_ms = sem("att_ms", 1)
    a_rs = sem("att_rstd", 1)
    a_u = sem("att_u", MH)
    a_hi = sem("att_hi", MH)
    a_lo = sem("att_lo", MH)
    f_sq = sem("f_sq")
    f_sum = sem("f_sum")
    f_ms = sem("f_ms")
    f_rs = sem("f_rs")
    f_out = sem("f_out")
    stored = sem("stored")

    block = ctx.enter_context(nc.Block())

    def rows(ap):
        return ap.rearrange("a p n -> p (a n)")

    @block.sync
    def _(sp):
        sp.dma_start(cin[:, :], cT).then_inc(c_land.sem, 16)
        sp.dma_start(cst[:, :, :], consts).then_inc(pos_land.sem, 16)

        def ada_piece(group, k, m, wait):
            sp.wait_ge(ada_done.sem, wait)
            sp.wait_ge(go.sem, 1)
            src = w_ada[bass.ds(group * ADA_Q + (k * 3 + m), 1), :, :]
            sp.dma_start(ada_in[:, m, :], rows(src)).then_inc(ada_land[m].sem, 16)

        for k in range(KC):
            for m in range(3):
                if k:
                    sp.wait_ge(ada_done.sem, 3 + 3 * (k - 1) + m + 1)
                sp.dma_start(ada_in[:, m, :], w_ada[k * 3 + m, :, :]).then_inc(ada_land[m].sem, 16)
            if k == 1:
                sp.dma_start(x[:, :, :], xT).then_inc(x_land.sem, 16)
                sp.dma_start(posi[:, :], pos.to_broadcast([P, SEQ])).then_inc(pos_land.sem, 16)
                sp.dma_start(invs[:, :], invf).then_inc(pos_land.sem, 16)
                sp.dma_start(fing[:, :], finalg).then_inc(pos_land.sem, 16)

        with sp.Fori(0, DEPTH) as l:
            sp.wait_ge(x_new.sem, x_new.at(l, 0))
            sp.wait_ge(go.sem, 1)
            sp.dma_start(par[:, :], rows(params[bass.ds(l, 1), :, :])).then_inc(par_land.sem, 16)

            def item(n, src):
                sp.wait_ge(w_lo.sem, w_lo.at(l, n - 1))
                sp.wait_ge(go.sem, 1)
                slot = n % 2 if isinstance(n, int) else item.slot
                sp.dma_start(raw[slot][:, :], rows(src)).then_inc(w_land[slot].sem, 16)

            def ffn(j, first):
                up = l * (2 * UP_ITEMS) + j * UP_ITEMS
                dn = l * (2 * DN_ITEMS) + j * DN_ITEMS

                def up_items(i):
                    for q in range(4):
                        item.slot = q % 2
                        item(i * 4 + (first + q), w_up[bass.ds(up + i * 4 + q, 1), :, :])

                group = l * 3 + 1 if j == 0 else l * -3 + 3
                with sp.Fori(0, 8) as i:
                    up_items(i)
                    if j:
                        sp.wait_ge(x_new.sem, x_new.at(l, 3 * KC))
                    for m in range(3):
                        ada_piece(group, i, m, ada_done.at(l, i * 3 + (2 * ADA_Q * j + m - 2)))
                with sp.Fori(8, 11) as i:
                    up_items(i)
                with sp.Fori(0, 4) as i:
                    for q in range(6):
                        item.slot = q % 2
                        item(i * 6 + (first + UP_ITEMS + q), w_dn[bass.ds(dn + i * 6 + q, 1), :, :])
                        if j == 0:
                            k2, m = divmod(q, 3)
                            ada_piece(l * 3 + 2, i * 2 + k2, m,
                                      ada_done.at(l, i * 6 + (ADA_Q + q - 2)))

            ffn(0, 0)
            with sp.Fori(0, MX_ITEMS // 2) as i:
                for q in range(2):
                    item.slot = q
                    item(i * 2 + (FF_ITEMS + q), w_mx[bass.ds(l * MX_ITEMS + i * 2 + q, 1), :, :])
            ffn(1, FF_ITEMS + MX_ITEMS)

        sp.wait_ge(f_out.sem, KC)
        sp.dma_start(out, sq[:, :, :]).then_inc(stored.sem, 16)
        sp.wait_ge(stored.sem, 16)

    @block.gpsimd
    def _(gp):
        gp.sem_inc(go.sem, 1)
        gp.sem_inc(w_lo.sem, 2)
        gp.memset(acc[:, :, :], 0.0).then_inc(acc_zero.sem, 1)
        with gp.Fori(0, DEPTH) as l:

            def lo(n, slot):
                gp.wait_ge(w_hi.sem, w_hi.at(l, n + 1))
                gp.tensor_tensor(wL[slot][:, :], raw[slot][:, :], wH[slot][:, :],
                                 ALU.subtract).then_inc(w_lo.sem, 1)

            def zero(n_mod, n_x):
                gp.wait_ge(mod_sum.sem, mod_sum.at(l, n_mod))
                if n_x is not None:
                    gp.wait_ge(x_new.sem, x_new.at(l, n_x))
                gp.sem_inc(passed["gp"].sem, 1)
                gp.memset(acc[:, :, :], 0.0).then_inc(acc_zero.sem, 1)

            def ffn(j, first):
                lo(first, 0)
                lo(first + 1, 1)
                if j == 0:
                    zero(1, None)
                else:
                    zero(3, 3 * KC)
                with gp.Fori(0, UP_ITEMS // 2) as i:
                    for q in range(2):
                        lo(i * 2 + (first + 2 + q), q)
                if j == 0:
                    zero(2, None)
                with gp.Fori(0, DN_ITEMS // 2 - 1) as i:
                    for q in range(2):
                        lo(i * 2 + (first + UP_ITEMS + 2 + q), q)

            ffn(0, 0)
            f = FF_ITEMS
            lo(f, 0)
            lo(f + 1, 1)
            with gp.Fori(1, MX_ITEMS // 2) as i:
                for q in range(2):
                    lo(i * 2 + (f + q), q)
            ffn(1, FF_ITEMS + MX_ITEMS)

    @block.scalar
    def _(act):
        act.sem_inc(sg_done.sem, 2)
        act.wait_ge(c_land.sem, 16)
        act.activation(csil[:, :], cin[:, :], ACT.Silu).then_inc(csil_done.sem, 1)
        act.wait_ge(p_step.sem, PRO_ANGLES)
        act.activation(sinT[:, :], ang[:, :], ACT.Sin).then_inc(trig_done.sem, 1)
        act.activation(cosT[:, :], tmp[:, :], ACT.Sin).then_inc(trig_done.sem, 1)

        with act.Fori(0, DEPTH) as l:

            def wait(sig, n):
                act.wait_ge(sig.sem, sig.at(l, n))

            def hi(n, slot, nth):
                wait(w_land[slot], nth * 16)
                wait(w_used, n - 1)
                act.activation(wH[slot][:, :], raw[slot][:, :], ACT.Copy).then_inc(w_hi.sem, 1)

            def root(dst, src, inverse, n, done):
                wait(inverse, n)
                act.activation(dst, src, ACT.Sqrt).then_inc(done.sem, 1)

            def norm(n):
                wait(x_new, [0, KC, 3 * KC][n])
                for c in range(KC):
                    act.activation(sq[:, c, :], x[:, c, :], ACT.Square).then_inc(sq_done.sem, 1)
                root(rstd[:, :], ms[:, :], ms_done, n + 1, rstd_done)
                for c in range(KC):
                    wait(u_done, n * KC + c + 1)
                    act.activation(hH[:, c, :], sq[:, c, :], ACT.Identity,
                                   bias=mod[:, n, 0, c:c + 1]).then_inc(h_hi.sem, 1)

            def ffn(j, first):
                hi(first, 0, first // 2 + 1)
                hi(first + 1, 1, first // 2 + 1)
                norm(2 * j)
                with act.Fori(0, FC // 2) as i:
                    for s in range(2):
                        n, nth = i * 4 + (first + 2 * s + 2), i * 2 + (first // 2 + s + 2)
                        hi(n, 0, nth)
                        wait(w_used, i * 4 + (first + 2 * s + 1))
                        act.activation(sg[:, s, :], ps[:, s, :], ACT.Silu).then_inc(sg_done.sem, 1)
                        hi(i * 4 + (first + 2 * s + 3), 1, nth)
                        wait(prod_done, i * 2 + (FC * j + s + 1))
                        act.wait_ge(go.sem, 1)
                        act.activation(ffH[:, bass.ds(i * 2 + s, 1), :].rearrange("p a n -> p (a n)"),
                                       prod[s][:, :], ACT.Copy).then_inc(ff_hi.sem, 1)
                with act.Fori(0, DN_ITEMS // 2 - 1) as i:
                    for q in range(2):
                        hi(i * 2 + (first + UP_ITEMS + 2 + q), q, i + ((first + UP_ITEMS) // 2 + 2))

            ffn(0, 0)

            issued = [0]

            def ahead(n):
                while issued[0] <= n:
                    m = FF_ITEMS + issued[0]
                    hi(m, m % 2, m // 2 + 1)
                    issued[0] += 1

            def used(n):
                ahead(n + 1)
                wait(w_used, FF_ITEMS + n + 1)

            ahead(1)
            norm(1)
            for s in range(CCH + 2):
                if s < CCH:
                    used(I_CONV + s)
                    if s >= 2:
                        wait(csilu, s - 1)
                    act.activation(cbuf[:, s % 2, :], ps[:, s % 2, :], ACT.Identity,
                                   bias=par[:, P_CB + s:P_CB + s + 1],
                                   scale=par[:, P_CW + s * KSZ + 2:P_CW + s * KSZ + 3]
                                   ).then_inc(cen.sem, 1)
                if s == 3:
                    wait(d_abs, 1)
                    act.activation(sab, sab, ACT.Exp, scale=-1.0).then_inc(d_exp.sem, 1)
                    act.activation(sea[:, 0:2 * HEADS], par[:, P_AL:P_AL + 2 * HEADS],
                                   ACT.Exp).then_inc(d_exp.sem, 1)
                if 1 <= s <= CCH:
                    c = s - 1
                    wait(conv, c + 1)
                    dst = bfm[:, c, :] if c < 2 else cfm[:, c - 2, :] if c < 4 else xs[:, c % 2, :]
                    act.activation(dst, cbuf[:, c % 2, :], ACT.Silu).then_inc(csilu.sem, 1)
                if s - 2 in TR:
                    c = s - 2
                    wait(trx, TR.index(c) + 1)
                    dst = (btok[:, :, c * P:(c + 1) * P] if c < 2
                           else xtok[:, :, (c - 4) * P:(c - 3) * P])
                    act.activation(dst, ps[:, 2 + c % 2, :].rearrange("p (t n) -> p t n", t=TC),
                                   ACT.Copy).then_inc(tev.sem, 1)
            ahead(I_Z + 1)
            wait(cs_cp, 1)
            for d in range(2):
                act.dma_start(cs_dram[d, :, :], csT[:, d, :]).then_inc(cs_out.sem, 16)
            act.activation(cs3[:, :, :], cs3[:, :, :], ACT.Exp).then_inc(cs_exp.sem, 1)
            wait(cs_out, 32)

            def load_rows(c):
                for d in range(2):
                    src = cs_dram[d:d + 1, :, c * P:(c + 1) * P].to_broadcast([P, HEADS, P])
                    act.dma_start(dec[:, d, :, :], src).then_inc(r_land[d].sem, 16)

            def decay_exp(c):
                for d in range(2):
                    wait(d_dif, 2 * c + d + 1)
                    act.activation(dec[:, d, :, :], dec[:, d, :, :], ACT.Exp).then_inc(d_ex.sem, 1)

            load_rows(0)
            for z in range(2):
                used(I_Z + 4 * z + 1)
                used(I_Z + 4 * z + 3)
                for t in range(TC):
                    act.activation(zs[:, t, z * SEQ:(z + 1) * SEQ], ps[:, 4 + t, :],
                                   ACT.Silu).then_inc(z_ev.sem, 1)
            for q in range(7):
                used(I_QA + q)
                act.activation(rawq[:, q, :], ps[:, q % 2, :], ACT.Copy).then_inc(q_ev.sem, 1)
            ahead(I_OS + 1)
            decay_exp(0)
            for c in range(TC):
                if c + 1 < TC:
                    wait(yd_mm, c + 1)
                    load_rows(c + 1)
                wait(y_raw, c + 1)
                for g in range(GRP):
                    act.activation(xw[:, g * SEQ:(g + 1) * SEQ], yb[:, g * SEQ:(g + 1) * SEQ],
                                   ACT.Square, accum_out=ssq[:, g:g + 1]).then_inc(y_sq.sem, 1)
                root(ssq[:, 4:6], ssq[:, 2:4], y_ms, c + 1, y_rs)
                if c + 1 < TC:
                    decay_exp(c + 1)
                for b in range(2):
                    wait(y_f, 2 * c + b + 1)
                    act.activation(hH[:, 4 * b:4 * b + 4, c * P:(c + 1) * P], yt[:, :, :],
                                   ACT.Copy).then_inc(y_hi.sem, 1)
            ahead(I_MLA + 1)
            wait(y_lo, 2 * TC)
            for c in range(6):
                act.activation(lsq[:, c, :], rawq[:, c, :], ACT.Square).then_inc(l_sq.sem, 1)
            root(rstd[:, :], ms[:, :], l_ms, 1, l_rs)
            root(rtmp[:, 1, :], rtmp[:, 0, :], l_ms, 2, l_rs)
            for c in range(6):
                wait(l_u, c + 1)
                dst = qaH[:, c, :] if c < QC else ckH[:, c - QC, :]
                act.activation(dst, rawq[:, c, :], ACT.Copy).then_inc(l_hi.sem, 1)

            def rope(r, src, dst):
                if r:
                    wait(rp_lo, r)
                act.activation(rtmp[:, 0, :], src, ACT.Copy).then_inc(rp_in.sem, 1)
                wait(rp_out, r + 1)
                act.activation(dst, rtmp[:, 0, :], ACT.Copy).then_inc(rp_hi.sem, 1)

            wait(l_lo, 6)
            rope(0, rawq[:, 6, :], krH[:, :])
            for hg in range(2):
                i0 = I_MLA + 5 * hg
                used(i0)
                for h in range(4):
                    act.activation(kH[:, h, :], ps[:, h, :], ACT.Copy).then_inc(k_hi.sem, 1)
                used(i0 + 1)
                for t in range(TC):
                    act.activation(vH[:, t, :], ps[:, 4 + t, :], ACT.Copy).then_inc(v_hi.sem, 1)
                used(i0 + 2)
                for p in range(2):
                    rope(1 + 2 * hg + p, ps[:, p, :], qrH[:, p, :])
                for p in range(2):
                    used(i0 + 3 + p)
                    for h in range(2):
                        act.activation(qnH[:, h, :], ps[:, 2 + h, :], ACT.Copy).then_inc(qn_hi.sem, 1)
                    for s in range(9):
                        n = (4 * hg + 2 * p) * TC + s
                        if s < 8:
                            wait(s_mx, n + 1)
                            if n >= 2:
                                wait(p_tr, n - 1)
                            act.activation(pr[:, n % 2, :], ps[:, 4 + n % 2, :], ACT.Exp,
                                           bias=sm[:, n % 2, 1:2], scale=ATT_SCALE,
                                           accum_out=sm[:, n % 2, 2:3]).then_inc(s_ex.sem, 1)
                        if s:
                            m = n - 1
                            t = m % TC
                            wait(p_tr, m + 1)
                            if t == 0 and m:
                                wait(o_mm, m // TC)
                            act.activation(ptH[:, :, t * P:(t + 1) * P],
                                           ps[:, 6 + m % 2, :].rearrange("p (k n) -> p k n", k=TC),
                                           ACT.Copy).then_inc(p_hi.sem, 1)
                            if t == TC - 1:
                                h = m // TC
                                wait(o_mm, h + 1)
                                act.activation(ofm[:, h, :], ps[:, h % 2, :],
                                               ACT.Copy).then_inc(o_ev.sem, 1)
            ahead(I_OA + 1)
            wait(o_ev, MH)
            for c in range(MH):
                act.activation(asq[:, c, :], ofm[:, c, :], ACT.Square).then_inc(a_sq.sem, 1)
            root(rstd[:, :], ms[:, :], a_ms, 1, a_rs)
            for c in range(MH):
                wait(a_u, c + 1)
                act.activation(hH[:, c, :], ofm[:, c, :], ACT.Copy).then_inc(a_hi.sem, 1)
            ahead(MX_ITEMS - 1)
            ffn(1, FF_ITEMS + MX_ITEMS)

        act.wait_ge(x_new.sem, x_new.at(DEPTH, 0))
        for c in range(KC):
            act.activation(sq[:, c, :], x[:, c, :], ACT.Square).then_inc(f_sq.sem, 1)
        act.wait_ge(f_ms.sem, 1)
        act.activation(rstd[:, :], ms[:, :], ACT.Sqrt).then_inc(f_rs.sem, 1)

    @block.vector
    def _(dve):
        dve.sem_inc(prod_done.sem, 2)
        dve.sem_inc(ff_lo.sem, 2)
        dve.sem_inc(ada_done.sem, 3)
        steps = [0]

        def pro(ins):
            ins.then_inc(p_step.sem, 1)
            steps[0] += 1
            dve.wait_ge(p_step.sem, steps[0])

        dve.wait_ge(csil_done.sem, 1)
        dve.wait_ge(acc_zero.sem, 1)

        def ada_piece(m, scalar, landed, own):
            for sig, n in (landed, own):
                dve.wait_ge(sig.sem, n)
            dve.scalar_tensor_tensor(acc[:, m, :], ada_in[:, m, :], scalar, acc[:, m, :],
                                     ALU.mult, ALU.add).then_inc(ada_done.sem, 1)

        for k in range(KC):
            for m in range(3):
                ada_piece(m, csil[:, k:k + 1], (ada_land[m], 16 * (k + 1)),
                          (ada_done, 3 * k + m + 1))
            if k == 1:
                dve.wait_ge(pos_land.sem, 64)
                pro(dve.tensor_copy(kk[:, :], posi[:, :]))
                pro(dve.tensor_scalar(ang[:, :], kk[:, :], invs[:, 0:1], None, ALU.mult))
                pro(dve.tensor_scalar(kk[:, :], ang[:, :], 1.0 / TWO_PI, ROUND, ALU.mult, ALU.add))
                pro(dve.tensor_scalar(kk[:, :], kk[:, :], -ROUND, None, ALU.add))
                for part in (C1, C2, C3):
                    pro(dve.scalar_tensor_tensor(ang[:, :], kk[:, :], -part, ang[:, :],
                                                 ALU.mult, ALU.add))
                pro(dve.tensor_scalar(tmp[:, :], ang[:, :], np.pi / 2, None, ALU.add))
                pro(dve.tensor_scalar(kk[:, :], tmp[:, :], np.pi, -TWO_PI, ALU.is_gt, ALU.mult))
                pro(dve.tensor_tensor(tmp[:, :], tmp[:, :], kk[:, :], ALU.add))
                pro(dve.tensor_scalar(tmp[:, :], tmp[:, :], PI_IN, -PI_IN, ALU.min, ALU.max))
                pro(dve.tensor_scalar(ang[:, :], ang[:, :], PI_IN, -PI_IN, ALU.min, ALU.max))
                assert steps[0] == PRO_ANGLES, steps[0]
        dve.wait_ge(x_land.sem, 16)
        dve.wait_ge(trig_done.sem, 2)
        dve.sem_inc(x_new.sem, 2)

        with dve.Fori(0, DEPTH) as l:
            do = Chain(dve, v_step, l)

            def wait(sig, n):
                dve.wait_ge(sig.sem, sig.at(l, n))

            def modulation(g):
                wait(mod_sum, g + 1)
                flat = mod[:, g, :, :].rearrange("p a c -> p (a c)")
                do(dve.tensor_tensor(flat, ps[:, 7, 0:ADA_Q],
                                     par[:, P_AB + g * ADA_Q:P_AB + (g + 1) * ADA_Q], ALU.add))
                do(dve.scalar_tensor_tensor(mod[:, g, 1, :], mod[:, g, 1, :], 1.0,
                                            par[:, P_NG + g * KC:P_NG + (g + 1) * KC],
                                            ALU.add, ALU.mult))
                if g != 1:
                    do(dve.tensor_scalar(mod[:, g, 2, :], mod[:, g, 2, :], 0.5, None, ALU.mult))

            def mean(dst, bank, n, done):
                do(dve.tensor_scalar(dst, ps[:, bank, :], 1.0 / n, EPS, ALU.mult, ALU.add))
                dve.reciprocal(dst, dst).then_inc(done.sem, 1)

            def norm(n):
                wait(n_sum, n + 1)
                mean(ms[:, :], 6, DM, ms_done)
                wait(rstd_done, n + 1)

                def lo(c):
                    wait(h_hi, n * KC + c + 1)
                    dve.scalar_tensor_tensor(hL[:, c, :], sq[:, c, :], mod[:, n, 0, c:c + 1],
                                             hH[:, c, :], ALU.add, ALU.subtract
                                             ).then_inc(h_lo.sem, 1)

                for c in range(KC):
                    dve.scalar_tensor_tensor(sq[:, c, :], x[:, c, :], mod[:, n, 1, c:c + 1],
                                             rstd[:, :], ALU.mult, ALU.mult).then_inc(u_done.sem, 1)
                    if c:
                        lo(c - 1)
                lo(KC - 1)

            def residual(d, gate, bank):
                dst = x[:, bass.ds(d, 1), :].rearrange("p a n -> p (a n)")
                dve.scalar_tensor_tensor(dst, ps[:, bank, :], gate, dst,
                                         ALU.mult, ALU.add).then_inc(x_new.sem, 1)

            def up_chunks(i, j, first):
                for s in range(2):
                    wait(sg_done, i * 2 + (FC * j + s + 1))
                    wait(w_used, i * 4 + (first + 2 * s + 2))
                    wait(ff_lo, i * 2 + (FC * j + s - 1))
                    dve.tensor_tensor(prod[s][:, :], sg[:, s, :], ps[:, 2 + s, :],
                                      ALU.mult).then_inc(prod_done.sem, 1)
                for s in range(2):
                    wait(ff_hi, i * 2 + (FC * j + s + 1))
                    ff = bass.ds(i * 2 + s, 1)
                    dve.tensor_tensor(ffL[:, ff, :].rearrange("p a n -> p (a n)"), prod[s][:, :],
                                      ffH[:, ff, :].rearrange("p a n -> p (a n)"),
                                      ALU.subtract).then_inc(ff_lo.sem, 1)

            def ffn(j, first):
                n = 2 * j
                if j == 0:
                    wait(par_land, 16)
                    modulation(0)
                norm(n)
                wait(acc_zero, [1, 3][j])
                dve.sem_inc(passed["dve"].sem, 1)
                off = 2 * ADA_Q * j
                with dve.Fori(0, 8) as i:
                    for m in range(3):
                        ada_piece(m, csil[:, bass.ds(i, 1)],
                                  (ada_land[m], ada_land[m].at(l, i * 16 + 16 * (16 * j + 1))),
                                  (ada_done, ada_done.at(l, i * 3 + (off + m - 2))))
                    up_chunks(i, j, first)
                with dve.Fori(8, 11) as i:
                    up_chunks(i, j, first)
                if j == 0:
                    modulation(1)
                    wait(acc_zero, 2)
                    dve.sem_inc(passed["dve"].sem, 1)
                gate = mod[:, n, 2, :]
                with dve.Fori(0, KC // 2) as i:
                    for q in range(6):
                        if j == 0:
                            k2, m = divmod(q, 3)
                            ada_piece(m, csil[:, bass.ds(i * 2 + k2, 1)],
                                      (ada_land[m], ada_land[m].at(l, i * 32 + 16 * (8 + k2 + 1))),
                                      (ada_done, ada_done.at(l, i * 6 + (ADA_Q + q - 2))))
                        if q % 3 == 2:
                            d = i * 2 + q // 3
                            wait(w_used, i * 6 + (first + UP_ITEMS + q + 1))
                            residual(d, gate[:, bass.ds(d, 1)], 4 + q // 3)

            ffn(0, 0)
            f = FF_ITEMS
            modulation(2)
            norm(1)

            def halves(t):
                return t.rearrange("p (d t h) -> p d t h", d=2, t=TC)

            dtv, adv, xrv = halves(dtt), halves(adt), halves(sxr)

            def softplus_start():
                wait(w_used, f + I_DT + 1)
                for d in range(2):
                    src = ps[:, 4, 0:P].rearrange("p (t d h) -> p d t h", d=2, t=TC)[:, d, :, :]
                    bias = par[:, P_DB + d * HEADS:P_DB + (d + 1) * HEADS]
                    do(dve.tensor_tensor(xrv[:, d, :, :], src,
                                         bias.unsqueeze(1).to_broadcast([P, TC, HEADS]), ALU.add))
                dve.scalar_tensor_tensor(sab, sxr, -1.0, sxr, ALU.mult, ALU.max).then_inc(d_abs.sem, 1)

            def softplus_end():
                wait(d_exp, 2)
                do(dve.tensor_scalar(sp1, sab, 2.0, None, ALU.add))
                do(dve.reciprocal(sp1, sp1))
                do(dve.tensor_tensor(sp1, sp1, sab, ALU.mult))
                do(dve.tensor_tensor(sp2, sp1, sp1, ALU.mult))
                do(dve.tensor_scalar(dtt, sp2, 1.0 / 15, None, ALU.mult))
                for odd in (13, 11, 9, 7, 5, 3):
                    do(dve.scalar_tensor_tensor(dtt, dtt, 1.0 / odd, sp2, ALU.add, ALU.mult))
                do(dve.scalar_tensor_tensor(dtt, dtt, 1.0, sp1, ALU.add, ALU.mult))
                do(dve.tensor_scalar(sxr, sxr, 0.0, None, ALU.max))
                do(dve.scalar_tensor_tensor(dtt, dtt, 2.0, sxr, ALU.mult, ALU.add))
                for d in range(2):
                    ea = sea[:, d * HEADS:(d + 1) * HEADS].unsqueeze(1).to_broadcast([P, TC, HEADS])
                    last = dve.scalar_tensor_tensor(adv[:, d, :, :], dtv[:, d, :, :], -1.0, ea,
                                                    ALU.mult, ALU.mult)
                    if d == 0:
                        do(last)
                last.then_inc(a_dt.sem, 1)

            for s in range(CCH):
                wait(cen, s + 1)
                for k in (0, 1, 3, 4):
                    sh = k - KSZ // 2
                    a, b = max(0, -sh), min(SEQ, SEQ - sh)
                    ins = dve.scalar_tensor_tensor(
                        cbuf[:, s % 2, a:b], ps[:, s % 2, a + sh:b + sh],
                        par[:, P_CW + s * KSZ + k:P_CW + s * KSZ + k + 1],
                        cbuf[:, s % 2, a:b], ALU.mult, ALU.add)
                    if k < 4:
                        do(ins)
                ins.then_inc(conv.sem, 1)
                if s == 2:
                    softplus_start()
                if s == 4:
                    softplus_end()

            wait(cs_mm, 1)
            do(dve.tensor_copy(cs3[:, 1:3, :], ps[:, 5, 0:2 * P].rearrange("p (a n) -> p a n", a=2)))
            do(dve.tensor_copy(sxr, cs3[:, 1, :]))
            do(dve.tensor_tensor(cs3[:, 0, :], cs3[:, 2, :], cs3[:, 1, :], ALU.subtract))
            dve.tensor_copy(csT[:, :, :], ps[0:HEADS, 6:8, :]).then_inc(cs_cp.sem, 1)
            wait(cb_mm, 1)
            for d in range(2):
                for g in range(GRP):
                    tri = (triL if d else triU).unsqueeze(1).to_broadcast([P, TC, P])
                    ins = dve.tensor_tensor(cbm[:, d, :, g, :],
                                            ps[:, 2 + g, :].rearrange("p (t n) -> p t n", t=TC),
                                            tri, ALU.mult)
                    if d + g < 2:
                        do(ins)
            ins.then_inc(cb_ok.sem, 1)
            wait(cs_exp, 1)
            to_end, vdec, cdec = (cs3[:, i, :] for i in range(3))
            do(dve.tensor_tensor(uu, dtt, to_end, ALU.mult))

            def per_head(tile, d, c):
                col = (d * TC + c) * HEADS
                return tile[:, col:col + HEADS].unsqueeze(2).to_broadcast([P, HEADS, HD])

            def heads(t):
                return t.rearrange("p (h n) -> p h n", n=HD)

            def weighted(d, c, n):
                if n:
                    wait(st_mm, n)
                dve.tensor_tensor(heads(xw[:, :]), heads(xtok[:, c, :]), per_head(uu, d, c),
                                  ALU.mult).then_inc(u_w.sem, 1)

            def bank2(b):
                return ps[:, b:b + 2, :].rearrange("p b n -> p (b n)")

            def add_state(dst, src, d, c, n):
                wait(st_mm, n + 1)
                if src is None:
                    dve.tensor_copy(dst, bank2(0)).then_inc(st_up.sem, 1)
                    return
                do(dve.tensor_tensor(heads(dst), heads(src), per_head(cdec, d, c), ALU.mult))
                dve.tensor_tensor(dst, dst, bank2(0), ALU.add).then_inc(st_up.sem, 1)

            for n, c in enumerate((3, 2, 1)):
                weighted(1, c, n)
                add_state(sbk[:, c - 1, :], sbk[:, c, :] if n else None, 1, c, n)

            def differences(c):
                for d in range(2):
                    wait(r_land[d], 16 * (c + 1))
                    col = (d * TC + c) * HEADS
                    at_s = sxr[:, col:col + HEADS].unsqueeze(2).to_broadcast([P, HEADS, P])
                    do(dve.tensor_tensor(dec[:, d, :, :], dec[:, d, :, :], at_s, ALU.subtract))
                    dve.tensor_scalar(dec[:, d, :, :], dec[:, d, :, :], 0.0, None,
                                      ALU.min).then_inc(d_dif.sem, 1)

            def masked(c):
                for d in range(2):
                    do(dve.tensor_tensor(heads(xdt[:, d, :]), heads(xtok[:, c, :]),
                                         per_head(dtt, d, c), ALU.mult))
                for d in range(2):
                    wait(d_ex, 2 * c + d + 1)
                    view = dec[:, d, :, :].rearrange("p (g h) n -> p g h n", g=GRP)
                    cb = cbm[:, d, c, :, :].unsqueeze(2).to_broadcast([P, GRP, HEADS // GRP, P])
                    dve.tensor_tensor(view, view, cb, ALU.mult).then_inc(m_ok.sem, 1)

            differences(0)
            masked(0)
            for c in range(TC):
                if c < TC - 1:
                    weighted(0, c, 3 + c)
                    add_state(sf[:, :], sf[:, :] if c else None, 0, c, 3 + c)
                wait(yd_mm, c + 1)
                do(dve.tensor_copy(yb[:, :], bank2(0)))
                for d in range(2):
                    if c == (TC - 1 if d else 0):
                        continue
                    do(dve.tensor_tensor(heads(xw[:, :]), heads(bank2(2 + 2 * d)),
                                         per_head(vdec, d, c), ALU.mult))
                    do(dve.tensor_tensor(yb[:, :], yb[:, :], xw[:, :], ALU.add))
                skip = par[:, P_DS:P_DS + HEADS].unsqueeze(2).to_broadcast([P, HEADS, HD])
                do(dve.tensor_tensor(heads(xw[:, :]), heads(xtok[:, c, :]), skip, ALU.mult))
                do(dve.tensor_tensor(yb[:, :], yb[:, :], xw[:, :], ALU.add))
                dve.tensor_tensor(yb[:, :], yb[:, :], zs[:, c, :], ALU.mult).then_inc(y_raw.sem, 1)
                if c + 1 < TC:
                    differences(c + 1)
                wait(y_sq, 2 * c + 2)
                do(dve.tensor_scalar(ssq[:, 2:4], ssq[:, 0:2], 1.0 / SEQ, EPS, ALU.mult, ALU.add))
                dve.reciprocal(ssq[:, 2:4], ssq[:, 2:4]).then_inc(y_ms.sem, 1)
                if c + 1 < TC:
                    masked(c + 1)
                wait(y_rs, c + 1)
                for g in range(GRP):
                    half = yb[:, g * SEQ:(g + 1) * SEQ]
                    dve.tensor_scalar(half, half, ssq[:, 4 + g:5 + g], None,
                                      ALU.mult).then_inc(y_nm.sem, 1)
                for b in range(2):
                    wait(y_tr, 2 * c + b + 1)
                    if 2 * c + b:
                        wait(y_lo, 2 * c + b)
                    gain = par[:, P_SG + 4 * b:P_SG + 4 * b + 4].unsqueeze(2).to_broadcast([P, 4, P])
                    dve.tensor_tensor(yt[:, :, :],
                                      ps[:, 6 + b, :].rearrange("p (k n) -> p k n", k=4), gain,
                                      ALU.mult).then_inc(y_f.sem, 1)
                    wait(y_hi, 2 * c + b + 1)
                    put = (slice(None), slice(4 * b, 4 * b + 4), slice(c * P, (c + 1) * P))
                    dve.tensor_tensor(hL[put], yt[:, :, :], hH[put],
                                      ALU.subtract).then_inc(y_lo.sem, 1)

            def mix_residual(first):
                for d in range(KC):
                    wait(w_used, f + first + d + 1)
                    dve.scalar_tensor_tensor(x[:, d, :], ps[:, 4 + d % 2, :], mod[:, 1, 2, d:d + 1],
                                             x[:, d, :], ALU.mult, ALU.add).then_inc(x_new.sem, 1)

            mix_residual(I_OS)

            def scaled(src, gain, row, n, sig_u, sig_hi, sig_lo, dsts, count):
                for c in range(n, n + count):
                    dve.scalar_tensor_tensor(src[:, c, :], src[:, c, :], gain(c), row,
                                             ALU.mult, ALU.mult).then_inc(sig_u.sem, 1)
                    wait(sig_hi, c + 1)
                    h, lo_ = dsts(c)
                    dve.tensor_tensor(lo_, src[:, c, :], h, ALU.subtract).then_inc(sig_lo.sem, 1)

            wait(l_sum, 1)
            mean(ms[:, :], 6, QL, l_ms)
            wait(l_sum, 2)
            mean(rtmp[:, 0, :], 7, KVL, l_ms)
            wait(l_rs, 1)
            scaled(rawq, lambda c: par[:, P_QG + c:P_QG + c + 1], rstd[:, :], 0, l_u, l_hi, l_lo,
                   lambda c: (qaH[:, c, :], qaL[:, c, :]), QC)
            wait(l_rs, 2)
            scaled(rawq, lambda c: par[:, P_KG + c - QC:P_KG + c - QC + 1], rtmp[:, 1, :], QC,
                   l_u, l_hi, l_lo, lambda c: (ckH[:, c - QC, :], ckL[:, c - QC, :]), KVC)

            def rope(r, dstH, dstL):
                wait(rp_mm, r + 1)
                if r:
                    wait(rp_lo, r)
                do(dve.tensor_tensor(rtmp[:, 1, :], ps[:, 2, :], sinT[:, :], ALU.mult))
                do(dve.tensor_tensor(rtmp[:, 0, :], rtmp[:, 0, :], cosT[:, :], ALU.mult))
                dve.tensor_tensor(rtmp[:, 0, :], rtmp[:, 0, :], rtmp[:, 1, :],
                                  ALU.add).then_inc(rp_out.sem, 1)
                wait(rp_hi, r + 1)
                dve.tensor_tensor(dstL, rtmp[:, 0, :], dstH, ALU.subtract).then_inc(rp_lo.sem, 1)

            rope(0, krH[:, :], krL[:, :])
            for hg in range(2):
                for h in range(4):
                    wait(k_hi, 4 * hg + h + 1)
                    dve.tensor_tensor(kL[:, h, :], ps[:, h, :], kH[:, h, :],
                                      ALU.subtract).then_inc(k_lo.sem, 1)
                for t in range(TC):
                    wait(v_hi, 4 * hg + t + 1)
                    dve.tensor_tensor(vL[:, t, :], ps[:, 4 + t, :], vH[:, t, :],
                                      ALU.subtract).then_inc(v_lo.sem, 1)
                for p in range(2):
                    rope(1 + 2 * hg + p, qrH[:, p, :], qrL[:, p, :])
                for p in range(2):
                    for h in range(2):
                        wait(qn_hi, 4 * hg + 2 * p + h + 1)
                        dve.tensor_tensor(qnL[:, h, :], ps[:, 2 + h, :], qnH[:, h, :],
                                          ALU.subtract).then_inc(qn_lo.sem, 1)
                    for s in range(9):
                        n = (4 * hg + 2 * p) * TC + s
                        if s < 8:
                            st = sm[:, n % 2, :]
                            wait(s_mm, n + 1)
                            do(dve.reduce_max(st[:, 0:1], ps[:, 4 + n % 2, :], AXX))
                            dve.tensor_scalar(st[:, 1:2], st[:, 0:1], -ATT_SCALE, None,
                                              ALU.mult).then_inc(s_mx.sem, 1)
                            wait(s_ex, n + 1)
                            do(dve.reciprocal(st[:, 3:4], st[:, 2:3]))
                            dve.tensor_scalar(pr[:, n % 2, :], pr[:, n % 2, :], st[:, 3:4], None,
                                              ALU.mult).then_inc(s_nm.sem, 1)
                        if s:
                            m = n - 1
                            t = m % TC
                            put = (slice(None), slice(None), slice(t * P, (t + 1) * P))
                            wait(p_hi, m + 1)
                            dve.tensor_tensor(ptL[put],
                                              ps[:, 6 + m % 2, :].rearrange("p (k n) -> p k n", k=TC),
                                              ptH[put], ALU.subtract).then_inc(p_lo.sem, 1)
            wait(a_sum, 1)
            mean(ms[:, :], 6, DM, a_ms)
            wait(a_rs, 1)
            scaled(ofm, lambda c: par[:, P_AG + c:P_AG + c + 1], rstd[:, :], 0, a_u, a_hi, a_lo,
                   lambda c: (hH[:, c, :], hL[:, c, :]), MH)
            mix_residual(I_OA)
            ffn(1, FF_ITEMS + MX_ITEMS)
            assert do.n == DVE_STEPS, do.n

        dve.wait_ge(f_sum.sem, 1)
        dve.tensor_scalar(ms[:, :], ps[:, 6, :], 1.0 / DM, EPS,
                          ALU.mult, ALU.add).then_inc(p_step.sem, 1)
        dve.wait_ge(p_step.sem, PRO_ANGLES + 1)
        dve.reciprocal(ms[:, :], ms[:, :]).then_inc(f_ms.sem, 1)
        dve.wait_ge(f_rs.sem, 1)
        for c in range(KC):
            dve.scalar_tensor_tensor(sq[:, c, :], x[:, c, :], fing[:, c:c + 1], rstd[:, :],
                                     ALU.mult, ALU.mult).then_inc(f_out.sem, 1)

    @block.tensor
    def _(pe):
        pe.sem_inc(w_used.sem, 2)
        pe.wait_ge(pos_land.sem, 64)

        def three(dst, aH, aL, bH, bL, first, last):
            pe.matmul(dst, aH, bH, start=first, stop=False)
            pe.matmul(dst, aH, bL, start=False, stop=False)
            return pe.matmul(dst, aL, bH, start=False, stop=last)

        with pe.Fori(0, DEPTH) as l:

            def wait(sig, n):
                pe.wait_ge(sig.sem, sig.at(l, n))

            def mod_vectors(g):
                wait(ada_done, ADA_Q * g)
                for q in range(3 * KC):
                    m, c = divmod(q, KC)
                    last = pe.matmul(ps[:, 7, q:q + 1], acc[:, m, c * P:(c + 1) * P],
                                     ones[:, 0:1], start=True, stop=True)
                last.then_inc(mod_sum.sem, 1)

            def sum_features(bank, src, n, sig, base, done):
                for c in range(n):
                    wait(sig, base + c + 1)
                    last = pe.matmul(ps[:, bank, :], ones, src[:, c, :],
                                     start=(c == 0), stop=(c == n - 1))
                last.then_inc(done.sem, 1)

            def blocks(dst, slot, n, rhsH, rhsL, k0=0, last=KC, width=P, off=0):
                for b in range(n):
                    w = slice(b * width + off, b * width + off + P)
                    k = k0 + b
                    end = three(dst, wH[slot][:, w], wL[slot][:, w], rhsH[:, k, :], rhsL[:, k, :],
                                k == 0, k == last - 1)
                return end

            def ffn(j, first):
                if j == 0:
                    mod_vectors(0)
                sum_features(6, sq, KC, sq_done, 2 * j * KC, n_sum)
                wait(h_lo, (2 * j + 1) * KC)
                pe.sem_inc(passed["pe"].sem, 1)
                with pe.Fori(0, FC // 2) as i:
                    for s in range(2):
                        for q in range(2):
                            free = sg_done if q == 0 else prod_done
                            wait(free, i * 2 + (FC * j + s - 1))
                            wait(w_lo, i * 4 + (first + 2 * s + q + 1))
                            blocks(ps[:, 2 * q + s, :], q, KC, hH, hL).then_inc(w_used.sem, 1)
                if j == 0:
                    mod_vectors(1)
                wait(ff_lo, FC * (j + 1))
                pe.sem_inc(passed["pe"].sem, 1)
                with pe.Fori(0, KC // 2) as i:
                    for q in range(6):
                        s, part = divmod(q, DN_PER)
                        if part == 0:
                            wait(x_new, i * 2 + (3 * KC * j + s - 1))
                        wait(w_lo, i * 6 + (first + UP_ITEMS + q + 1))
                        n = min(8, FC - 8 * part)
                        blocks(ps[:, 4 + s, :], q % 2, n, ffH, ffL, 8 * part,
                               FC).then_inc(w_used.sem, 1)

            ffn(0, 0)
            f = FF_ITEMS

            def ready(n):
                wait(w_lo, f + n + 1)
                return n % 2

            mod_vectors(2)
            sum_features(6, sq, KC, sq_done, KC, n_sum)
            wait(h_lo, 2 * KC)
            slot = ready(I_DT)
            for t in range(TC):
                for k in range(KC):
                    w = slice(k * 32, k * 32 + 32)
                    tok = slice(t * P, (t + 1) * P)
                    last = three(ps[:, 4, t * 32:(t + 1) * 32], hH[:, k, tok], hL[:, k, tok],
                                 wH[slot][:, w], wL[slot][:, w], k == 0, k == KC - 1)
            last.then_inc(w_used.sem, 1)
            for s in range(CCH + 2):
                if s < CCH:
                    if s >= 2:
                        wait(conv, s - 1)
                    slot = ready(I_CONV + s)
                    blocks(ps[:, s % 2, :], slot, KC, hH, hL).then_inc(w_used.sem, 1)
                if s - 2 in TR:
                    c = s - 2
                    n = TR.index(c)
                    wait(csilu, c + 1)
                    if n >= 2:
                        wait(tev, n - 1)
                    src = bfm[:, c, :] if c < 2 else xs[:, c % 2, :]
                    for t in range(TC):
                        last = pe.transpose(ps[:, 2 + c % 2, t * P:(t + 1) * P],
                                            src[:, t * P:(t + 1) * P], ident)
                    last.then_inc(trx.sem, 1)
            wait(a_dt, 1)
            half = HEADS * TC
            for d, tri in ((0, triU), (1, triL)):
                col = slice(d * half, (d + 1) * half)
                pe.matmul(ps[:, 5, d * half:(d + 1) * half], tri, adt[:, col], start=True, stop=True)
                pe.matmul(ps[:, 5, P + d * half:P + (d + 1) * half], ones, adt[:, col],
                          start=True, stop=True)
            for d, tri in ((0, triU), (1, triL)):
                for t in range(TC):
                    col = (d * TC + t) * HEADS
                    last = pe.matmul(ps[0:HEADS, 6 + d, t * P:(t + 1) * P],
                                     adt[:, col:col + HEADS], tri, start=True, stop=True)
            last.then_inc(cs_mm.sem, 1)
            wait(tev, len(TR))
            for g in range(GRP):
                for t in range(TC):
                    tok = slice(t * P, (t + 1) * P)
                    last = pe.matmul(ps[:, 2 + g, tok], bfm[:, g, tok], cfm[:, g, tok],
                                     start=True, stop=True)
            last.then_inc(cb_mm.sem, 1)

            def state(c, n):
                wait(u_w, n + 1)
                for g in range(GRP):
                    last = pe.matmul(ps[:, g, :], btok[:, c, g * NST:(g + 1) * NST],
                                     xw[:, g * SEQ:(g + 1) * SEQ], start=True, stop=True)
                last.then_inc(st_mm.sem, 1)

            wait(cs_cp, 1)
            for z in range(2):
                if z:
                    wait(z_ev, TC)
                for q in range(4):
                    slot = ready(I_Z + 4 * z + q)
                    for t in range(TC):
                        tok = slice(t * P, (t + 1) * P)
                        for b in range(2):
                            k = 2 * q + b
                            w = slice(b * SEQ, (b + 1) * SEQ)
                            last = three(ps[:, 4 + t, :], hH[:, k, tok], hL[:, k, tok],
                                         wH[slot][:, w], wL[slot][:, w], k == 0, k == KC - 1)
                    last.then_inc(w_used.sem, 1)
                    n = 4 * z + q - 2
                    if n in (0, 2, 4):
                        if n:
                            wait(st_up, n // 2)
                        state(3 - n // 2, n // 2)
            wait(st_up, 3)
            for q in range(7):
                if q >= 2:
                    wait(q_ev, q - 1)
                slot = ready(I_QA + q)
                blocks(ps[:, q % 2, :], slot, KC, hH, hL).then_inc(w_used.sem, 1)
            wait(z_ev, 2 * TC)
            wait(q_ev, 7)
            wait(cb_ok, 1)
            for c in range(TC):
                tok = slice(c * P, (c + 1) * P)
                if c:
                    wait(y_raw, c)
                for d in range(2):
                    if c == (TC - 1 if d else 0):
                        continue
                    src = sbk[:, c, :] if d else sf[:, :]
                    if not d:
                        wait(st_up, 3 + c)
                    for g in range(GRP):
                        last = pe.matmul(ps[:, 2 + 2 * d + g, :], cfm[:, g, tok],
                                         src[:, g * SEQ:(g + 1) * SEQ], start=True, stop=True)
                if c < TC - 1:
                    state(c, 3 + c)
                    wait(st_up, 4 + c)
                wait(m_ok, 2 * c + 2)
                for h in range(HEADS):
                    g, col = divmod(h * HD, SEQ)
                    for d in range(2):
                        last = pe.matmul(ps[:, g, col:col + HD], dec[:, d, h, :],
                                         xdt[:, d, h * HD:(h + 1) * HD],
                                         start=(d == 0), stop=(d == 1))
                last.then_inc(yd_mm.sem, 1)
                wait(y_nm, 2 * c + 2)
                if c:
                    wait(y_lo, 2 * c)
                for b in range(2):
                    for k in range(4):
                        col = (4 * b + k) * P
                        last = pe.transpose(ps[:, 6 + b, k * P:(k + 1) * P], yb[:, col:col + P],
                                            ident)
                    last.then_inc(y_tr.sem, 1)

            def out_half(first, new):
                for d in range(KC):
                    wait(x_new, new + d - 1)
                    slot = ready(first + d)
                    blocks(ps[:, 4 + d % 2, :], slot, KC, hH, hL).then_inc(w_used.sem, 1)

            wait(y_lo, 2 * TC)
            out_half(I_OS, KC)

            for c in range(6):
                wait(l_sq, c + 1)
                bank, k, n = (6, c, QC) if c < QC else (7, c - QC, KVC)
                last = pe.matmul(ps[:, bank, :], ones, lsq[:, c, :], start=(k == 0), stop=(k == n - 1))
                if k == n - 1:
                    last.then_inc(l_sum.sem, 1)

            def rotate(r):
                wait(rp_in, r + 1)
                pe.matmul(ps[:, 2, :], perm, rtmp[:, 0, :], start=True, stop=True
                          ).then_inc(rp_mm.sem, 1)

            rotate(0)
            wait(l_lo, 6)
            wait(rp_lo, 1)
            for hg in range(2):
                i0 = I_MLA + 5 * hg
                if hg:
                    wait(o_ev, 4)
                    wait(p_lo, 4 * TC)
                slot = ready(i0)
                for h in range(4):
                    for k in range(KVC):
                        w = slice((k * 4 + h) * P, (k * 4 + h + 1) * P)
                        last = three(ps[:, h, :], wH[slot][:, w], wL[slot][:, w],
                                     ckH[:, k, :], ckL[:, k, :], k == 0, k == KVC - 1)
                last.then_inc(w_used.sem, 1)
                slot = ready(i0 + 1)
                for t in range(TC):
                    tok = slice(t * P, (t + 1) * P)
                    for k in range(KVC):
                        w = slice(k * SEQ, (k + 1) * SEQ)
                        last = three(ps[:, 4 + t, :], ckH[:, k, tok], ckL[:, k, tok],
                                     wH[slot][:, w], wL[slot][:, w], k == 0, k == KVC - 1)
                last.then_inc(w_used.sem, 1)
                wait(k_lo, 4 * hg + 4)
                slot = ready(i0 + 2)
                for p in range(2):
                    last = blocks(ps[:, p, :], slot, QC, qaH, qaL, last=QC, width=2 * P, off=p * P)
                last.then_inc(w_used.sem, 1)
                for p in range(2):
                    rotate(1 + 2 * hg + p)
                    wait(rp_out, 2 + 2 * hg + p)
                wait(rp_lo, 3 + 2 * hg)
                wait(v_lo, 4 * hg + 4)
                for p in range(2):
                    slot = ready(i0 + 3 + p)
                    for h in range(2):
                        last = blocks(ps[:, 2 + h, :], slot, QC, qaH, qaL, last=QC, width=2 * P,
                                      off=h * P)
                    last.then_inc(w_used.sem, 1)
                    wait(qn_lo, 4 * hg + 2 * p + 2)
                    for s in range(9):
                        n = (4 * hg + 2 * p) * TC + s
                        if s < 8:
                            h, t = divmod(s, TC)
                            tok = slice(t * P, (t + 1) * P)
                            bank = ps[:, 4 + n % 2, :]
                            if n >= 2:
                                wait(s_ex, n - 1)
                            three(bank, qnH[:, h, tok], qnL[:, h, tok], kH[:, 2 * p + h, :],
                                  kL[:, 2 * p + h, :], True, False)
                            r = slice(h * ROPE, (h + 1) * ROPE)
                            three(bank, qrH[r, p, tok], qrL[r, p, tok], krH[r, :], krL[r, :],
                                  False, True).then_inc(s_mm.sem, 1)
                        if s:
                            m = n - 1
                            wait(s_nm, m + 1)
                            if m >= 2:
                                wait(p_lo, m - 1)
                            for k in range(TC):
                                last = pe.transpose(ps[:, 6 + m % 2, k * P:(k + 1) * P],
                                                    pr[:, m % 2, k * P:(k + 1) * P], ident)
                            last.then_inc(p_tr.sem, 1)
                            if m % TC == TC - 1:
                                h = m // TC
                                wait(p_lo, m + 1)
                                if h >= 2:
                                    wait(o_ev, h - 1)
                                col = slice((h % 4) * VD, (h % 4 + 1) * VD)
                                for k in range(TC):
                                    last = three(ps[:, h % 2, :], vH[:, k, col], vL[:, k, col],
                                                 ptH[:, k, :], ptL[:, k, :], k == 0, k == TC - 1)
                                last.then_inc(o_mm.sem, 1)
            sum_features(6, asq, MH, a_sq, 0, a_sum)
            wait(a_lo, MH)
            out_half(I_OA, 2 * KC)
            ffn(1, FF_ITEMS + MX_ITEMS)

        for c in range(KC):
            pe.wait_ge(f_sq.sem, c + 1)
            last = pe.matmul(ps[:, 6, :], ones, sq[:, c, :], start=(c == 0), stop=(c == KC - 1))
        last.then_inc(f_sum.sem, 1)



def chunks(v, n):
    return np.swapaxes(v.reshape(v.shape[:-1] + (n, P)), -1, -2)


def blocks_of(w, cols):
    w = w[:, cols]
    return np.transpose(w.reshape(-1, P, w.shape[1]), (1, 0, 2)).reshape(P, -1)


def padded(a):
    out = np.zeros((P, ITEM), a.dtype)
    out[:, :a.shape[1]] = a
    return out


def up_items(g, u):
    out = []
    for f in range(FC):
        for w in (g, u):
            out.append(blocks_of(w, slice(f * P, (f + 1) * P)))
    return out


def down_items(w):
    out = []
    for d in range(KC):
        b = blocks_of(w, slice(d * P, (d + 1) * P))
        out += [padded(b[:, q * ITEM:(q + 1) * ITEM]) for q in range(DN_PER)]
    return out


def mixer_items(w_in, w_q, w_kv, w_out):
    xbc0 = DM
    dt0 = xbc0 + DM + 2 * GRP * NST
    qa0 = dt0 + 2 * HEADS
    kv0 = qa0 + QL
    items = [padded(blocks_of(w_in, slice(dt0, dt0 + 2 * HEADS)))]
    for c in list(range(KC, CCH)) + list(range(KC)):
        items.append(blocks_of(w_in, slice(xbc0 + c * P, xbc0 + (c + 1) * P)))
    for z in range(2):
        b = blocks_of(w_in, slice(z * SEQ, (z + 1) * SEQ))
        items += [b[:, q * ITEM:(q + 1) * ITEM] for q in range(4)]
    for c in range(QC):
        items.append(blocks_of(w_in, slice(qa0 + c * P, qa0 + (c + 1) * P)))
    for c in range(KVC):
        items.append(blocks_of(w_in, slice(kv0 + c * P, kv0 + (c + 1) * P)))
    kr = np.arange(kv0 + KVL, kv0 + KVL + ROPE)
    items.append(blocks_of(w_in, np.concatenate([kr, kr])))
    for d in range(KC):
        items.append(blocks_of(w_out[:DM], slice(d * P, (d + 1) * P)))
    for hg in range(2):
        hs = range(4 * hg, 4 * hg + 4)
        k = np.concatenate([np.arange(h * 256, h * 256 + NOPE) for h in hs])
        q = np.concatenate([np.arange(h * 192, h * 192 + NOPE) for h in hs])
        r = np.concatenate([np.arange(h * 192 + NOPE, (h + 1) * 192) for h in hs])
        items.append(blocks_of(w_kv, k))
        items.append(blocks_of(w_kv, k + NOPE))
        items.append(blocks_of(w_q, r))
        items += [blocks_of(w_q, q[:2 * P]), blocks_of(w_q, q[2 * P:])]
    for d in range(KC):
        items.append(blocks_of(w_out[DM:], slice(d * P, (d + 1) * P)))
    assert len(items) == MX_ITEMS
    return items


def kernel(**inputs):
    import concourse.bacc as _bacc
    from concourse.bass_utils import run_bass_kernel_spmd as _run

    a = {k: np.asarray(v) for k, v in inputs.items()}
    row = np.arange(P)
    le = (row[:, None] <= row[None, :]).astype(np.float32)
    turn = np.zeros((P, P), np.float32)
    for m in range(P):
        first = m % ROPE < ROPE // 2
        turn[m + (ROPE // 2 if first else -(ROPE // 2)), m] = -1.0 if first else 1.0
    consts = np.stack([le, le.T, np.ones((P, P), np.float32), np.eye(P, dtype=np.float32), turn], 1)
    power = (np.arange(0, ROPE, 2, dtype=np.float32) / ROPE).astype(np.float32)
    inv = (np.float32(1.0) / np.power(np.float32(THETA), power)).astype(np.float32)
    invf = inv[row % (ROPE // 2)][:, None]

    def wide(v):
        return np.broadcast_to(v.reshape(1, -1), (P, v.size))

    params = []
    order = list(range(KC, CCH)) + list(range(KC))
    for l in range(DEPTH):
        cw = np.transpose(a["conv_w"][l].reshape(KSZ, CCH, P)[:, order], (2, 1, 0)).reshape(P, -1)
        params.append(np.concatenate([
            cw, chunks(a["conv_b"][l], CCH)[:, order],
            np.transpose(chunks(a["norm_g"][l], KC), (1, 0, 2)).reshape(P, -1),
            chunks(a["ssd_norm_g"][l], KC), chunks(a["q_norm_g"][l], QC),
            chunks(a["kv_norm_g"][l], KVC), chunks(a["attn_norm_g"][l], KC),
            chunks(a["ada_b"][l], 72),
            wide(a["dt_bias"][l]), wide(a["a_log"][l]), wide(a["d_skip"][l])], axis=1))
    w_up, w_dn, w_mx = [], [], []
    for l in range(DEPTH):
        for j in range(2):
            w_up += up_items(a["ffn_w_gate"][l, j], a["ffn_w_up"][l, j])
            w_dn += down_items(a["ffn_w_down"][l, j])
        w_mx += mixer_items(a["w_in"][l], a["w_q_b"][l], a["w_kv_b"][l], a["w_out"][l])
    ada = a["ada_w"].reshape(DEPTH, KC, P, 3, 3, DM).transpose(0, 3, 1, 4, 2, 5)
    arrays = {
        "xT": np.transpose(a["x"][0].reshape(SEQ, KC, P), (2, 1, 0)),
        "cT": chunks(a["c"][0], KC),
        "pos": a["positions"].astype(np.int32, copy=False).reshape(1, SEQ),
        "invf": invf, "consts": consts, "params": np.stack(params),
        "finalg": chunks(a["final_norm_g"], KC),
        "w_up": np.stack(w_up), "w_dn": np.stack(w_dn), "w_mx": np.stack(w_mx),
        "w_ada": ada.reshape(DEPTH * 3 * ADA_Q, P, DM),
    }
    arrays = {k: np.ascontiguousarray(v) for k, v in arrays.items()}
    nc = _bacc.Bacc("TRN2", target_bir_lowering=False, num_devices=1)
    args = [nc.dram_tensor(n, v.shape, mybir.dt.from_np(v.dtype), kind="ExternalInput").ap()
            for n, v in arrays.items()]
    out = nc.dram_tensor("out", (P, KC, SEQ), F32, kind="ExternalOutput").ap()
    build_trunk(nc, *args, out)
    r = _run(nc, [arrays], core_ids=[0])
    got = r.results[0]["out"]
    return np.ascontiguousarray(np.transpose(got, (2, 1, 0)).reshape(1, SEQ, DM))
```

```python
from contextlib import ExitStack

import numpy as np

import concourse.bass as bass
from concourse import mybir

F32 = mybir.dt.float32
F32R = mybir.dt.float32r
I32 = mybir.dt.int32
ACT = mybir.ActivationFunctionType
ALU = mybir.AluOpType
AXX = mybir.AxisListType.X

P = 128
DEPTH = 2
SEQ = 512
DM = 1024
DFF = 2816
KC = DM // P
FC = DFF // P
TC = SEQ // P
HEADS = 16
HD = 64
GRP = 2
NST = 128
KSZ = 5
CCH = (DM + 2 * GRP * NST) // P
MH = 8
NOPE, ROPE, VD = 128, 64, 128
QL, KVL = 512, 256
QC, KVC = QL // P, KVL // P
EPS = 1e-6
SOFT = 4 * TC
ATT_SCALE = float(NOPE + ROPE) ** -0.5
THETA = 10000.0

ITEM = 8 * P
UP_ITEMS = 2 * FC
DN_PER = 3
DN_ITEMS = KC * DN_PER
MX_ITEMS = 1 + CCH + 8 + QC + KVC + 1 + KC + 2 * 5 + KC
FF_ITEMS = UP_ITEMS + DN_ITEMS
NI = 2 * FF_ITEMS + MX_ITEMS
assert NI % 2 == 0 and FF_ITEMS % 2 == 0
TR = [0, 1] + list(range(4, CCH))
I_DT, I_CONV, I_Z = 0, 1, 1 + CCH
I_QA = I_Z + 8
I_KV = I_QA + QC
I_KR = I_KV + KVC
I_OS = I_KR + 1
I_MLA = I_OS + KC
I_OA = I_MLA + 10

P_CW = 0
P_CB = P_CW + CCH * KSZ
P_NG = P_CB + CCH
P_SG = P_NG + 3 * KC
P_QG = P_SG + KC
P_KG = P_QG + QC
P_AG = P_KG + KVC
P_AB = P_AG + KC
P_DB = P_AB + 72
P_AL = P_DB + 2 * HEADS
P_DS = P_AL + 2 * HEADS
NPAR = P_DS + HEADS

DVE_STEPS = 179
ADA_Q = 24

PRO_ANGLES = 12
TWO_PI = 2 * np.pi
C1 = 6.28125
C2 = float(np.array([np.array([TWO_PI - C1], np.float32).view(np.int32)[0] & -4096], np.int32).view(np.float32)[0])
C3 = float(TWO_PI - C1 - C2)
ROUND = 1.5 * 2.0 ** 23
PI_IN = 3.1415925


class Signal:

    def __init__(self, sem, per, first=0):
        self.sem, self.per, self.first = sem, per, first

    def at(self, layer, n):
        return layer * self.per + (self.first + n)


class Chain:

    def __init__(self, eng, sig, layer):
        self.eng, self.sig, self.layer, self.n = eng, sig, layer, 0

    def __call__(self, ins):
        ins.then_inc(self.sig.sem, 1)
        self.n += 1
        self.eng.wait_ge(self.sig.sem, self.sig.at(self.layer, self.n))


def build_trunk(nc, xT, cT, pos, invf, consts, params, finalg, w_up, w_dn, w_mx, w_ada, out):
    ctx = ExitStack()
    base = -(-nc.sbuf_base // 32) * 32
    top = [base]

    def at(name, shape, dt, off):
        return nc.alloc_sbuf_tensor_at(name, shape, dt, offset=off)

    def sb(name, shape, dt=F32):
        size = 4
        for d in shape[1:]:
            size *= d
        off = top[0]
        top[0] += -(-size // 32) * 32
        return at(name, shape, dt, off)

    x = sb("x_res", [P, KC, SEQ])
    H0 = top[0]
    hH = sb("h_hi", [P, KC, SEQ], F32R)
    hL = sb("h_lo", [P, KC, SEQ], F32R)
    raw = [sb(f"w_raw{j}", [P, ITEM]) for j in range(2)]
    wH = [sb(f"w_hi{j}", [P, ITEM], F32R) for j in range(2)]
    wL = [sb(f"w_lo{j}", [P, ITEM], F32R) for j in range(2)]
    cst = sb("consts_sb", [P, 5, P])
    triU, triL, ones, ident, perm = (cst[:, i, :] for i in range(5))
    cosT = sb("cosT", [P, SEQ])
    sinT = sb("sinT", [P, SEQ])
    par = sb("par", [P, NPAR])
    fing = sb("fing", [P, KC])
    mod = sb("mod", [P, 3, 3, KC])
    csil = sb("csil", [P, KC])
    cin = sb("cin", [P, KC])
    invs = sb("invs", [P, 1])
    MS0 = top[0]
    ms = sb("ms", [P, SEQ])
    rstd = sb("rstd", [P, SEQ])
    A0 = top[0]
    ada_in = sb("ada_in", [P, 3, DM])
    acc = sb("ada_acc", [P, 3, DM])
    R0 = top[0]
    K = 1024
    assert R0 + 92 * K <= nc.sbuf_usable_end, (R0, nc.sbuf_usable_end)

    ffH = at("ff_hi", [P, FC, SEQ], F32R, R0)
    ffL = at("ff_lo", [P, FC, SEQ], F32R, R0 + 44 * K)
    sg = at("silu_gate", [P, 2, SEQ], F32, R0 + 88 * K)
    sqs = at("sq_sum", [P, SEQ], F32, R0 + 90 * K)
    prod = [ms, rstd]
    sq = at("scaled", [P, KC, SEQ], F32, R0)

    rawq = at("q_kv_raw", [P, 7, SEQ], F32, R0)
    zs = at("silu_z", [P, TC, DM], F32, R0 + 14 * K)
    xtok = at("x_tok", [P, TC, DM], F32, R0 + 30 * K)
    dec = at("decay", [P, 2, HEADS, P], F32, R0 + 46 * K)
    cbuf = at("conv_acc", [P, 2, SEQ], F32, R0 + 46 * K)
    xs = at("x_feat", [P, 2, SEQ], F32, R0 + 50 * K)
    xdt = at("x_dt", [P, 2, DM], F32, R0 + 62 * K)
    xw = at("x_w", [P, DM], F32, R0 + 70 * K)
    yb = at("y_buf", [P, DM], F32, R0 + 74 * K)
    bfm = at("b_feat", [P, GRP, SEQ], F32, R0 + 74 * K)
    btok = at("b_tok", [P, TC, GRP * NST], F32, R0 + 78 * K)
    sf = [at("state_f1", [P, DM], F32, R0 + 82 * K), at("state_f2", [P, DM], F32, MS0),
          at("state_f3", [P, DM], F32, R0 + 78 * K)]
    yt = at("y_feat", [P, 4, P], F32, R0 + 86 * K)
    small = at("ssd_small", [P, 8, P], F32, R0 + 88 * K)
    dtt, adt, sxr, sab, sp1, sp2, uu, sea = (small[:, i, :] for i in range(8))
    cs3 = at("cs3", [P, 3, P], F32, R0 + 92 * K)
    assert R0 + 94 * K + 512 <= nc.sbuf_usable_end, (R0 + 94 * K + 512, nc.sbuf_usable_end)
    sbk = at("state_b", [P, 3, DM], F32, A0)
    cbm = at("cb_masked", [P, 2, TC, GRP, P], F32, A0 + 12 * K)
    cfm = at("c_feat", [P, GRP, SEQ], F32, A0 + 20 * K)
    csT = at("cs_rows", [HEADS, 2, SEQ], F32, R0 + 62 * K)
    dtf = at("dt_feat", [2 * HEADS, SEQ], F32, R0 + 62 * K)
    yt2 = at("y_part", [P, DM], F32, R0 + 94 * K + 512)
    assert R0 + 98 * K + 512 <= nc.sbuf_usable_end, (R0 / K, nc.sbuf_usable_end)
    ssq = at("y_ssq", [P, 8], F32, R0 + 92 * K + 1536)

    ofm = at("att_out", [P, MH, SEQ], F32, R0)
    qaH = at("qa_hi", [P, QC, SEQ], F32R, R0 + 16 * K)
    qaL = at("qa_lo", [P, QC, SEQ], F32R, R0 + 24 * K)
    ckH = at("ckv_hi", [P, KVC, SEQ], F32R, R0 + 32 * K)
    ckL = at("ckv_lo", [P, KVC, SEQ], F32R, R0 + 36 * K)
    krH = at("kr_hi", [P, SEQ], F32R, R0 + 40 * K)
    krL = at("kr_lo", [P, SEQ], F32R, R0 + 42 * K)
    kH = at("k_hi", [P, 4, SEQ], F32R, H0)
    kL = at("k_lo", [P, 4, SEQ], F32R, H0 + 8 * K)
    vH = at("v_hi", [P, TC, 4 * VD], F32R, H0 + 16 * K)
    vL = at("v_lo", [P, TC, 4 * VD], F32R, H0 + 24 * K)
    qnH = at("qn_hi", [P, 4, SEQ], F32R, R0 + 60 * K)
    qnL = at("qn_lo", [P, 4, SEQ], F32R, R0 + 68 * K)
    qrH = at("qr_hi", [P, 2, SEQ], F32R, R0 + 76 * K)
    qrL = at("qr_lo", [P, 2, SEQ], F32R, R0 + 80 * K)
    asq = at("att_sq", [P, SEQ], F32, R0 + 44 * K)
    asum = at("att_sq_sum", [P, SEQ], F32, R0 + 46 * K)
    ptH = at("pT_hi", [P, TC, SEQ], F32R, A0)
    ptL = at("pT_lo", [P, TC, SEQ], F32R, A0 + 8 * K)
    lsq = at("lora_sq", [P, 6, SEQ], F32, A0)
    pr = at("probs", [P, 3, SEQ], F32, A0 + 16 * K)
    ms2, rstd2 = pr[:, 0, :], pr[:, 1, :]
    rt = [ms, rstd]
    sm = at("softmax_small", [P, 3, 4], F32, R0 + 92 * K)

    posi = at("pos_i", [P, SEQ], I32, R0)
    ang = at("ang", [P, SEQ], F32, R0 + 2 * K)
    kk = at("turns", [P, SEQ], F32, R0 + 4 * K)
    tmp = at("ang_tmp", [P, SEQ], F32, R0 + 6 * K)
    pro_in = at("ada_in_more", [P, 3, DM], F32, R0 + 16 * K)

    ps = ctx.enter_context(nc.psum_tensor("banks", [P, 8, SEQ], F32))
    cs_dram = nc.dram_tensor("cs_rows_dram", (2, HEADS, SEQ), F32, kind="Internal").ap()

    def sem(name, per=0, first=0):
        return Signal(ctx.enter_context(nc.semaphore(name)), per, first)

    go = sem("go")
    passed = {e: sem(f"passed_{e}") for e in ("gp", "dve", "pe")}
    w_land = [sem(f"w_land{j}", 16 * NI // 2) for j in range(2)]
    w_hi = sem("w_hi", NI)
    w_lo = sem("w_lo", NI, 2)
    w_used = sem("w_used", NI, 2)
    ada_land = [sem(f"ada_land{m}", 16 * ADA_Q, 16 * 4) for m in range(3)]
    pro_land = [sem(f"ada_more_land{m}") for m in range(3)]
    ada_done = sem("ada_done", 3 * ADA_Q, ADA_Q + 3)
    acc_zero = sem("acc_zero", 3, 1)
    mod_sum = sem("mod_sum", 3)
    c_land = sem("c_land")
    x_land = sem("x_land")
    x_sq = sem("x_squared")
    pos_land = sem("pos_land")
    par_land = sem("par_land", 16)
    csil_done = sem("csil_done")
    p_step = sem("prologue_step")
    trig_done = sem("trig_done")
    x_new = sem("x_new", 4 * KC, 2)
    sq_mul = sem("sq_mul", 3 * KC)
    sq_add = sem("sq_added", 3 * KC, KC + 1)
    n_sum = sem("n_sum", 3)
    ms_done = sem("ms_done", 3)
    rstd_done = sem("rstd_done", 3)
    u_done = sem("u_done", 3 * KC)
    h_hi = sem("h_hi_done", 3 * KC)
    h_lo = sem("h_lo_done", 3 * KC)
    sg_done = sem("sg_done", 2 * FC, 2)
    prod_done = sem("prod_done", 2 * FC, 2)
    ff_hi = sem("ff_hi_done", 2 * FC)
    ff_lo = sem("ff_lo_done", 2 * FC, 2)
    v_step = sem("v_step", DVE_STEPS)
    cen = sem("conv_centre", CCH)
    conv = sem("conv_done", CCH)
    csilu = sem("conv_silu", CCH)
    trx = sem("x_transposed", len(TR))
    tev = sem("x_tok_done", len(TR))
    z_ev = sem("z_done", 2 * TC)
    q_ev = sem("q_raw_done", 7)
    dt_cp = sem("dt_copied", 1)
    dt_tr = sem("dt_transposed", 1)
    d_abs = sem("dt_abs", 1)
    d_exp = sem("dt_exp", 2)
    a_dt = sem("a_dt_done", 1)
    cs_mm = sem("cs_mm", 1)
    cs_cp = sem("cs_copied", 1)
    cs_out = sem("cs_stored", 32)
    cs_exp = sem("cs_exp", 1)
    u_w = sem("xw_done", 6)
    st_mm = sem("state_mm", 6)
    st_up = sem("state_done", 6)
    cb_mm = sem("cb_mm", 1)
    cb_ok = sem("cb_masked_done", 1)
    r_land = [sem(f"rows_land{d}", 16 * TC) for d in range(2)]
    d_dif = sem("dif_done", 2 * TC)
    d_ex = sem("decay_exp", 2 * TC)
    m_ok = sem("m_done", 2 * TC)
    skip_x = sem("skip_x_done", TC)
    x_dt = sem("x_dt_done", 2 * TC)
    yd_mm = sem("ydiag_mm", TC)
    y_raw = sem("y_gated", TC)
    y_sq = sem("y_sq", 2 * TC)
    y_ms = sem("y_ms", TC)
    y_rs = sem("y_rs", TC)
    y_nm = sem("y_normed", 2 * TC)
    y_tr = sem("y_transposed", 2 * TC)
    y_f = sem("y_feat_done", 2 * TC)
    y_hi = sem("y_hi_done", 2 * TC)
    y_lo = sem("y_lo_done", 2 * TC)
    l_sq = sem("lora_sq_done", 6)
    l_sum = sem("lora_sum", 2)
    l_ms = sem("lora_ms", 2)
    l_rs = sem("lora_rstd", 2)
    l_u = sem("lora_u", 6)
    l_hi = sem("lora_hi", 6)
    l_lo = sem("lora_lo", 6)
    rp_in = sem("rope_in", 5)
    rp_mm = sem("rope_rot", 5)
    rp_out = sem("rope_out", 5)
    rp_hi = sem("rope_hi", 5)
    rp_lo = sem("rope_lo", 5)
    k_hi = sem("k_hi_done", MH)
    k_lo = sem("k_lo_done", MH)
    v_hi = sem("v_hi_done", 2 * TC)
    v_lo = sem("v_lo_done", 2 * TC)
    qn_hi = sem("qn_hi_done", MH)
    qn_lo = sem("qn_lo_done", MH)
    s_mm = sem("scores_mm", MH * TC)
    s_mx = sem("scores_max", MH * TC)
    s_ex = sem("probs_exp", MH * TC)
    s_nm = sem("probs_done", MH * TC)
    p_tr = sem("probs_T", MH * TC)
    p_hi = sem("pT_hi_done", MH * TC)
    p_lo = sem("pT_lo_done", MH * TC)
    o_mm = sem("o_mm", MH)
    o_ev = sem("o_done", MH)
    a_sq = sem("att_sq_done", MH)
    a_add = sem("att_sq_added", MH - 1)
    a_sum = sem("att_sum", 1)
    a_ms = sem("att_ms", 1)
    a_rs = sem("att_rstd", 1)
    a_u = sem("att_u", MH)
    a_hi = sem("att_hi", MH)
    a_lo = sem("att_lo", MH)
    f_sum = sem("f_sum")
    f_ms = sem("f_ms")
    f_rs = sem("f_rs")
    f_out = sem("f_out")
    stored = sem("stored")

    block = ctx.enter_context(nc.Block())

    def rows(ap):
        return ap.rearrange("a p n -> p (a n)")

    def per_head(tile, d, c):
        col = (d * TC + c) * HEADS
        return tile[:, col:col + HEADS].unsqueeze(2).to_broadcast([P, HEADS, HD])

    def heads(t):
        return t.rearrange("p (h n) -> p h n", n=HD)

    @block.sync
    def _(sp):
        sp.dma_start(cin[:, :], cT).then_inc(c_land.sem, 16)
        sp.dma_start(cst[:, :, :], consts).then_inc(pos_land.sem, 16)

        def ada_piece(group, k, m, wait):
            sp.wait_ge(ada_done.sem, wait)
            sp.wait_ge(go.sem, 1)
            src = w_ada[bass.ds(group * ADA_Q + (k * 3 + m), 1), :, :]
            sp.dma_start(ada_in[:, m, :], rows(src)).then_inc(ada_land[m].sem, 16)

        for k in range(KC):
            for m in range(3):
                if k > 1:
                    sp.wait_ge(ada_done.sem, 3 + 3 * (k - 2) + m + 1)
                dst, land = (pro_in, pro_land) if k % 2 else (ada_in, ada_land)
                sp.dma_start(dst[:, m, :], w_ada[k * 3 + m, :, :]).then_inc(land[m].sem, 16)
            if k == 0:
                sp.dma_start(x[:, :, :], xT).then_inc(x_land.sem, 16)
            if k == 1:
                sp.dma_start(posi[:, :], pos.to_broadcast([P, SEQ])).then_inc(pos_land.sem, 16)
                sp.dma_start(invs[:, :], invf).then_inc(pos_land.sem, 16)
                sp.dma_start(fing[:, :], finalg).then_inc(pos_land.sem, 16)

        with sp.Fori(0, DEPTH) as l:
            sp.wait_ge(x_new.sem, x_new.at(l, 0))
            sp.wait_ge(go.sem, 1)
            sp.dma_start(par[:, :], rows(params[bass.ds(l, 1), :, :])).then_inc(par_land.sem, 16)

            def item(n, src):
                sp.wait_ge(w_lo.sem, w_lo.at(l, n - 1))
                sp.wait_ge(go.sem, 1)
                slot = n % 2 if isinstance(n, int) else item.slot
                sp.dma_start(raw[slot][:, :], rows(src)).then_inc(w_land[slot].sem, 16)

            def ffn(j, first):
                up = l * (2 * UP_ITEMS) + j * UP_ITEMS
                dn = l * (2 * DN_ITEMS) + j * DN_ITEMS

                def up_items(i):
                    for q in range(4):
                        item.slot = q % 2
                        item(i * 4 + (first + q), w_up[bass.ds(up + i * 4 + q, 1), :, :])

                group = l * 3 + 1 if j == 0 else l * -3 + 3
                with sp.Fori(0, 8) as i:
                    up_items(i)
                    if j:
                        sp.wait_ge(x_new.sem, x_new.at(l, 3 * KC))
                    for m in range(3):
                        ada_piece(group, i, m, ada_done.at(l, i * 3 + (2 * ADA_Q * j + m - 2)))
                with sp.Fori(8, 11) as i:
                    up_items(i)
                with sp.Fori(0, 4) as i:
                    for q in range(6):
                        item.slot = q % 2
                        item(i * 6 + (first + UP_ITEMS + q), w_dn[bass.ds(dn + i * 6 + q, 1), :, :])
                        if j == 0:
                            k2, m = divmod(q, 3)
                            ada_piece(l * 3 + 2, i * 2 + k2, m,
                                      ada_done.at(l, i * 6 + (ADA_Q + q - 2)))

            ffn(0, 0)
            with sp.Fori(0, MX_ITEMS // 2) as i:
                for q in range(2):
                    item.slot = q
                    item(i * 2 + (FF_ITEMS + q), w_mx[bass.ds(l * MX_ITEMS + i * 2 + q, 1), :, :])
            ffn(1, FF_ITEMS + MX_ITEMS)

        sp.wait_ge(f_out.sem, KC)
        sp.dma_start(out, sq[:, :, :]).then_inc(stored.sem, 16)
        sp.wait_ge(stored.sem, 16)

    @block.gpsimd
    def _(gp):
        gp.sem_inc(go.sem, 1)
        gp.sem_inc(w_lo.sem, 2)
        gp.memset(acc[:, :, :], 0.0).then_inc(acc_zero.sem, 1)
        gp.wait_ge(x_land.sem, 16)
        gp.tensor_tensor(sqs[:, :], x[:, 0, :], x[:, 0, :], ALU.mult).then_inc(sq_add.sem, 2)
        for c in range(1, KC):
            gp.wait_ge(sq_add.sem, c + 1)
            gp.tensor_tensor(ms[:, :], x[:, c, :], x[:, c, :], ALU.mult).then_inc(x_sq.sem, 1)
            gp.wait_ge(x_sq.sem, c)
            gp.tensor_tensor(sqs[:, :], sqs[:, :], ms[:, :], ALU.add).then_inc(sq_add.sem, 1)
        with gp.Fori(0, DEPTH) as l:

            def lo(n, slot):
                gp.wait_ge(w_hi.sem, w_hi.at(l, n + 1))
                gp.tensor_tensor(wL[slot][:, :], raw[slot][:, :], wH[slot][:, :],
                                 ALU.subtract).then_inc(w_lo.sem, 1)

            def zero(n_mod, n_x):
                gp.wait_ge(mod_sum.sem, mod_sum.at(l, n_mod))
                if n_x is not None:
                    gp.wait_ge(x_new.sem, x_new.at(l, n_x))
                gp.sem_inc(passed["gp"].sem, 1)
                gp.memset(acc[:, :, :], 0.0).then_inc(acc_zero.sem, 1)

            def ffn(j, first):
                lo(first, 0)
                lo(first + 1, 1)
                if j == 0:
                    zero(1, None)
                else:
                    zero(3, 3 * KC)
                with gp.Fori(0, UP_ITEMS // 2) as i:
                    for q in range(2):
                        lo(i * 2 + (first + 2 + q), q)
                if j == 0:
                    zero(2, None)
                with gp.Fori(0, DN_ITEMS // 2 - 1) as i:
                    for q in range(2):
                        lo(i * 2 + (first + UP_ITEMS + 2 + q), q)

            ffn(0, 0)
            f = FF_ITEMS
            lo(f, 0)
            lo(f + 1, 1)
            with gp.Fori(1, (I_QA + 5) // 2) as i:
                for q in range(2):
                    lo(i * 2 + (f + q), q)

            def wait(sig, n):
                gp.wait_ge(sig.sem, sig.at(l, n))

            def skip(c):
                gain = par[:, P_DS:P_DS + HEADS].unsqueeze(2).to_broadcast([P, HEADS, HD])
                gp.tensor_tensor(heads(xw[:, :]), heads(xtok[:, c, :]), gain,
                                 ALU.mult).then_inc(skip_x.sem, 1)

            wait(st_mm, 6)
            skip(0)
            lo(f + I_QA + 5, (I_QA + 5) % 2)
            lo(f + I_QA + 6, (I_QA + 6) % 2)
            for c in range(1, TC):
                wait(yd_mm, c)
                skip(c)
                for d in range(2):
                    gp.tensor_tensor(heads(xdt[:, d, :]), heads(xtok[:, c, :]),
                                     per_head(dtt, d, c), ALU.mult).then_inc(x_dt.sem, 1)
                if c == 1:
                    lo(f + I_OS, I_OS % 2)
                    lo(f + I_OS + 1, (I_OS + 1) % 2)
            with gp.Fori(I_OS // 2 + 1, I_MLA // 2 + 3) as i:
                for q in range(2):
                    lo(i * 2 + (f + q), q)

            def square_heads(hg):
                for h in range(4 * hg, 4 * hg + 4):
                    wait(o_ev, h + 1)
                    first = asum if h == 0 else asq
                    gp.tensor_tensor(first[:, :], ofm[:, h, :], ofm[:, h, :],
                                     ALU.mult).then_inc(a_sq.sem, 1)
                    wait(a_sq, h + 1)
                    if h:
                        gp.tensor_tensor(asum[:, :], asum[:, :], asq[:, :],
                                         ALU.add).then_inc(a_add.sem, 1)
                        wait(a_add, h)

            lo(f + I_MLA + 6, 0)
            square_heads(0)
            for n in range(I_MLA + 7, I_OA + 2):
                lo(f + n, n % 2)
            square_heads(1)
            gp.sem_inc(passed["gp"].sem, 1)
            with gp.Fori(I_OA // 2 + 1, MX_ITEMS // 2) as i:
                for q in range(2):
                    lo(i * 2 + (f + q), q)
            ffn(1, FF_ITEMS + MX_ITEMS)

    @block.scalar
    def _(act):
        act.sem_inc(sg_done.sem, 2)
        act.wait_ge(c_land.sem, 16)
        act.activation(csil[:, :], cin[:, :], ACT.Silu).then_inc(csil_done.sem, 1)
        act.wait_ge(p_step.sem, PRO_ANGLES)
        act.activation(sinT[:, :], ang[:, :], ACT.Sin).then_inc(trig_done.sem, 1)
        act.activation(cosT[:, :], tmp[:, :], ACT.Sin).then_inc(trig_done.sem, 1)

        with act.Fori(0, DEPTH) as l:

            def wait(sig, n):
                act.wait_ge(sig.sem, sig.at(l, n))

            def hi(n, slot, nth):
                wait(w_land[slot], nth * 16)
                wait(w_used, n - 1)
                act.activation(wH[slot][:, :], raw[slot][:, :], ACT.Copy).then_inc(w_hi.sem, 1)

            def root(dst, src, inverse, n, done):
                wait(inverse, n)
                act.activation(dst, src, ACT.Sqrt).then_inc(done.sem, 1)

            def norm(n):
                root(rstd[:, :], ms[:, :], ms_done, n + 1, rstd_done)
                for c in range(KC):
                    wait(u_done, n * KC + c + 1)
                    act.activation(hH[:, c, :], sq[:, c, :], ACT.Identity,
                                   bias=mod[:, n, 0, c:c + 1]).then_inc(h_hi.sem, 1)

            def ffn(j, first):
                hi(first, 0, first // 2 + 1)
                hi(first + 1, 1, first // 2 + 1)
                norm(2 * j)
                with act.Fori(0, FC // 2) as i:
                    for s in range(2):
                        n, nth = i * 4 + (first + 2 * s + 2), i * 2 + (first // 2 + s + 2)
                        hi(n, 0, nth)
                        wait(w_used, i * 4 + (first + 2 * s + 1))
                        act.activation(sg[:, s, :], ps[:, s, :], ACT.Silu).then_inc(sg_done.sem, 1)
                        hi(i * 4 + (first + 2 * s + 3), 1, nth)
                        wait(prod_done, i * 2 + (FC * j + s + 1))
                        act.wait_ge(go.sem, 1)
                        act.activation(ffH[:, bass.ds(i * 2 + s, 1), :].rearrange("p a n -> p (a n)"),
                                       prod[s][:, :], ACT.Copy).then_inc(ff_hi.sem, 1)
                with act.Fori(0, DN_ITEMS // 2 - 1) as i:
                    for q in range(2):
                        hi(i * 2 + (first + UP_ITEMS + 2 + q), q, i + ((first + UP_ITEMS) // 2 + 2))

            ffn(0, 0)

            issued = [0]

            def ahead(n):
                while issued[0] <= n:
                    m = FF_ITEMS + issued[0]
                    hi(m, m % 2, m // 2 + 1)
                    issued[0] += 1

            def used(n):
                ahead(n + 1)
                wait(w_used, FF_ITEMS + n + 1)

            ahead(1)
            norm(1)
            used(I_DT)
            act.activation(dtf[:, :], ps[0:2 * HEADS, 4, :], ACT.Copy).then_inc(dt_cp.sem, 1)
            for s in range(CCH + 2):
                if s < CCH:
                    used(I_CONV + s)
                    if s >= 2:
                        wait(csilu, s - 1)
                    act.activation(cbuf[:, s % 2, :], ps[:, s % 2, :], ACT.Identity,
                                   bias=par[:, P_CB + s:P_CB + s + 1],
                                   scale=par[:, P_CW + s * KSZ + 2:P_CW + s * KSZ + 3]
                                   ).then_inc(cen.sem, 1)
                if s == 3:
                    wait(d_abs, 1)
                    act.activation(sab, sab, ACT.Exp, scale=-1.0).then_inc(d_exp.sem, 1)
                    act.activation(sea[:, 0:2 * HEADS], par[:, P_AL:P_AL + 2 * HEADS],
                                   ACT.Exp).then_inc(d_exp.sem, 1)
                if 1 <= s <= CCH:
                    c = s - 1
                    wait(conv, c + 1)
                    dst = bfm[:, c, :] if c < 2 else cfm[:, c - 2, :] if c < 4 else xs[:, c % 2, :]
                    act.activation(dst, cbuf[:, c % 2, :], ACT.Silu).then_inc(csilu.sem, 1)
                if s - 2 in TR:
                    c = s - 2
                    wait(trx, TR.index(c) + 1)
                    dst = (btok[:, :, c * P:(c + 1) * P] if c < 2
                           else xtok[:, :, (c - 4) * P:(c - 3) * P])
                    act.activation(dst, ps[:, 2 + c % 2, :].rearrange("p (t n) -> p t n", t=TC),
                                   ACT.Copy).then_inc(tev.sem, 1)
            ahead(I_Z + 1)
            wait(cs_cp, 1)
            for d in range(2):
                act.dma_start(cs_dram[d, :, :], csT[:, d, :]).then_inc(cs_out.sem, 16)
            act.activation(cs3[:, :, :], cs3[:, :, :], ACT.Exp).then_inc(cs_exp.sem, 1)
            wait(cs_out, 32)

            def load_rows(c):
                for d in range(2):
                    src = cs_dram[d:d + 1, :, c * P:(c + 1) * P].to_broadcast([P, HEADS, P])
                    act.dma_start(dec[:, d, :, :], src).then_inc(r_land[d].sem, 16)

            def decay_exp(c):
                for d in range(2):
                    wait(d_dif, 2 * c + d + 1)
                    act.activation(dec[:, d, :, :], dec[:, d, :, :], ACT.Exp).then_inc(d_ex.sem, 1)

            load_rows(0)
            for z in range(2):
                used(I_Z + 4 * z + 1)
                used(I_Z + 4 * z + 3)
                for t in range(TC):
                    act.activation(zs[:, t, z * SEQ:(z + 1) * SEQ], ps[:, 4 + t, :],
                                   ACT.Silu).then_inc(z_ev.sem, 1)
            decay_exp(0)
            for q in range(7):
                if q == 5:
                    ahead(I_QA + q + 1)
                    wait(yd_mm, 1)
                    load_rows(1)
                used(I_QA + q)
                act.activation(rawq[:, q, :], ps[:, 2 + q % 2, :], ACT.Copy).then_inc(q_ev.sem, 1)
            ahead(I_OS + 1)
            for c in range(TC):
                if 1 <= c < TC - 1:
                    wait(yd_mm, c + 1)
                    load_rows(c + 1)
                if c == TC - 2:
                    for q in range(6):
                        act.activation(lsq[:, q, :], rawq[:, q, :], ACT.Square
                                       ).then_inc(l_sq.sem, 1)
                wait(y_raw, c + 1)
                for g in range(GRP):
                    act.activation(yt2[:, g * SEQ:(g + 1) * SEQ], yb[:, g * SEQ:(g + 1) * SEQ],
                                   ACT.Square, accum_out=ssq[:, g:g + 1]).then_inc(y_sq.sem, 1)
                if c + 1 < TC:
                    decay_exp(c + 1)
                root(ssq[:, 4:6], ssq[:, 2:4], y_ms, c + 1, y_rs)
                if c == TC - 1:
                    root(rstd[:, :], ms[:, :], l_ms, 1, l_rs)
                    root(rstd2, ms2, l_ms, 2, l_rs)
                for b in range(2):
                    wait(y_f, 2 * c + b + 1)
                    act.activation(hH[:, 4 * b:4 * b + 4, c * P:(c + 1) * P], yt[:, :, :],
                                   ACT.Copy).then_inc(y_hi.sem, 1)
            def rope(r, src, dst, item):
                if r:
                    wait(rp_lo, r)
                act.activation(rt[0][:, :], src, ACT.Copy).then_inc(rp_in.sem, 1)
                ahead(item)
                wait(rp_out, r + 1)
                act.activation(dst, rt[0][:, :], ACT.Copy).then_inc(rp_hi.sem, 1)

            for c in range(6):
                if c % 2 == 0:
                    ahead(I_OS + 2 + c // 2)
                wait(l_u, c + 1)
                dst = qaH[:, c, :] if c < QC else ckH[:, c - QC, :]
                act.activation(dst, rawq[:, c, :], ACT.Copy).then_inc(l_hi.sem, 1)
            ahead(I_OS + 5)
            wait(l_lo, 6)
            rope(0, rawq[:, 6, :], krH[:, :], I_OS + 6)
            for hg in range(2):
                i0 = I_MLA + 5 * hg
                used(i0)
                for h in range(4):
                    act.activation(kH[:, h, :], ps[:, h, :], ACT.Copy).then_inc(k_hi.sem, 1)
                used(i0 + 1)
                for t in range(TC):
                    act.activation(vH[:, t, :], ps[:, 4 + t, :], ACT.Copy).then_inc(v_hi.sem, 1)
                used(i0 + 2)
                for p in range(2):
                    rope(1 + 2 * hg + p, ps[:, p, :], qrH[:, p, :], i0 + 3)
                for p in range(2):
                    used(i0 + 3 + p)
                    for h in range(2):
                        act.activation(qnH[:, 2 * p + h, :], ps[:, 3 + 2 * p + h, :],
                                       ACT.Copy).then_inc(qn_hi.sem, 1)
                ahead(i0 + 6)
                for s in range(SOFT + 3):
                    n = SOFT * hg + s
                    if s < SOFT:
                        wait(s_mx, n + 1)
                        if n >= 3:
                            wait(p_tr, n - 2)
                        act.activation(pr[:, n % 3, :], ps[:, 3 + n % 3, :], ACT.Exp,
                                       bias=sm[:, n % 3, 1:2], scale=ATT_SCALE,
                                       accum_out=sm[:, n % 3, 2:3]).then_inc(s_ex.sem, 1)
                    if 3 <= s and (s - 3) % TC == TC - 1:
                        h = (n - 3) // TC
                        wait(o_mm, h + 1)
                        act.activation(ofm[:, h, :], ps[:, 2, :], ACT.Copy).then_inc(o_ev.sem, 1)
                    if 2 <= s < SOFT + 2:
                        m = n - 2
                        t = m % TC
                        wait(p_tr, m + 1)
                        act.activation(ptH[:, :, t * P:(t + 1) * P],
                                       ps[:, 6 + m % 2, :].rearrange("p (k n) -> p k n", k=TC),
                                       ACT.Copy).then_inc(p_hi.sem, 1)
            root(rstd[:, :], ms[:, :], a_ms, 1, a_rs)
            for c in range(MH):
                wait(a_u, c + 1)
                act.activation(hH[:, c, :], ofm[:, c, :], ACT.Copy).then_inc(a_hi.sem, 1)
            ahead(MX_ITEMS - 1)
            ffn(1, FF_ITEMS + MX_ITEMS)

        act.wait_ge(f_ms.sem, 1)
        act.activation(rstd[:, :], ms[:, :], ACT.Sqrt).then_inc(f_rs.sem, 1)

    @block.vector
    def _(dve):
        dve.sem_inc(prod_done.sem, 2)
        dve.sem_inc(ff_lo.sem, 2)
        dve.sem_inc(ada_done.sem, 3)
        steps = [0]

        def pro(ins):
            ins.then_inc(p_step.sem, 1)
            steps[0] += 1
            dve.wait_ge(p_step.sem, steps[0])

        dve.wait_ge(csil_done.sem, 1)
        dve.wait_ge(acc_zero.sem, 1)

        def ada_piece(m, scalar, landed, own, piece=ada_in):
            for sig, n in (landed, own):
                dve.wait_ge(sig.sem, n)
            dve.scalar_tensor_tensor(acc[:, m, :], piece[:, m, :], scalar, acc[:, m, :],
                                     ALU.mult, ALU.add).then_inc(ada_done.sem, 1)

        for k in range(KC):
            for m in range(3):
                ada_piece(m, csil[:, k:k + 1],
                          ((pro_land if k % 2 else ada_land)[m], 16 * (k // 2 + 1)),
                          (ada_done, 3 * k + m + 1), pro_in if k % 2 else ada_in)
            if k == 1:
                dve.wait_ge(pos_land.sem, 64)
                pro(dve.tensor_copy(kk[:, :], posi[:, :]))
                pro(dve.tensor_scalar(ang[:, :], kk[:, :], invs[:, 0:1], None, ALU.mult))
                pro(dve.tensor_scalar(kk[:, :], ang[:, :], 1.0 / TWO_PI, ROUND, ALU.mult, ALU.add))
                pro(dve.tensor_scalar(kk[:, :], kk[:, :], -ROUND, None, ALU.add))
                for part in (C1, C2, C3):
                    pro(dve.scalar_tensor_tensor(ang[:, :], kk[:, :], -part, ang[:, :],
                                                 ALU.mult, ALU.add))
                pro(dve.tensor_scalar(tmp[:, :], ang[:, :], np.pi / 2, None, ALU.add))
                pro(dve.tensor_scalar(kk[:, :], tmp[:, :], np.pi, -TWO_PI, ALU.is_gt, ALU.mult))
                pro(dve.tensor_tensor(tmp[:, :], tmp[:, :], kk[:, :], ALU.add))
                pro(dve.tensor_scalar(tmp[:, :], tmp[:, :], PI_IN, -PI_IN, ALU.min, ALU.max))
                pro(dve.tensor_scalar(ang[:, :], ang[:, :], PI_IN, -PI_IN, ALU.min, ALU.max))
                assert steps[0] == PRO_ANGLES, steps[0]
        dve.wait_ge(trig_done.sem, 2)
        dve.sem_inc(x_new.sem, 2)

        with dve.Fori(0, DEPTH) as l:
            do = Chain(dve, v_step, l)

            def wait(sig, n):
                dve.wait_ge(sig.sem, sig.at(l, n))

            def modulation(g):
                wait(mod_sum, g + 1)
                flat = mod[:, g, :, :].rearrange("p a c -> p (a c)")
                do(dve.tensor_tensor(flat, ps[:, 7, 0:ADA_Q],
                                     par[:, P_AB + g * ADA_Q:P_AB + (g + 1) * ADA_Q], ALU.add))
                do(dve.scalar_tensor_tensor(mod[:, g, 1, :], mod[:, g, 1, :], 1.0,
                                            par[:, P_NG + g * KC:P_NG + (g + 1) * KC],
                                            ALU.add, ALU.mult))
                if g != 1:
                    do(dve.tensor_scalar(mod[:, g, 2, :], mod[:, g, 2, :], 0.5, None, ALU.mult))

            def mean(dst, bank, n, done):
                do(dve.tensor_scalar(dst, ps[:, bank, :], 1.0 / n, EPS, ALU.mult, ALU.add))
                dve.reciprocal(dst, dst).then_inc(done.sem, 1)

            def norm(n):
                wait(n_sum, n + 1)
                mean(ms[:, :], 6, DM, ms_done)
                wait(rstd_done, n + 1)

                def lo(c):
                    wait(h_hi, n * KC + c + 1)
                    dve.scalar_tensor_tensor(hL[:, c, :], sq[:, c, :], mod[:, n, 0, c:c + 1],
                                             hH[:, c, :], ALU.add, ALU.subtract
                                             ).then_inc(h_lo.sem, 1)

                for c in range(KC):
                    dve.scalar_tensor_tensor(sq[:, c, :], x[:, c, :], mod[:, n, 1, c:c + 1],
                                             rstd[:, :], ALU.mult, ALU.mult).then_inc(u_done.sem, 1)
                    if c:
                        lo(c - 1)
                lo(KC - 1)

            def residual(d, gate, bank):
                dst = x[:, bass.ds(d, 1), :].rearrange("p a n -> p (a n)")
                dve.scalar_tensor_tensor(dst, ps[:, bank, :], gate, dst,
                                         ALU.mult, ALU.add).then_inc(x_new.sem, 1)

            def square(d, n, new):
                src = x[:, bass.ds(d, 1), :].rearrange("p a n -> p (a n)")
                wait(x_new, new)
                wait(sq_add, d + n * KC)
                dve.tensor_tensor(ms[:, :], src, src, ALU.mult).then_inc(sq_mul.sem, 1)
                wait(sq_mul, d + (n * KC + 1))
                dve.tensor_tensor(sqs[:, :], sqs[:, :], ms[:, :], ALU.add).then_inc(sq_add.sem, 1)

            def up_chunks(i, j, first):
                for s in range(2):
                    wait(sg_done, i * 2 + (FC * j + s + 1))
                    wait(w_used, i * 4 + (first + 2 * s + 2))
                    wait(ff_lo, i * 2 + (FC * j + s - 1))
                    dve.tensor_tensor(prod[s][:, :], sg[:, s, :], ps[:, 2 + s, :],
                                      ALU.mult).then_inc(prod_done.sem, 1)
                for s in range(2):
                    wait(ff_hi, i * 2 + (FC * j + s + 1))
                    ff = bass.ds(i * 2 + s, 1)
                    dve.tensor_tensor(ffL[:, ff, :].rearrange("p a n -> p (a n)"), prod[s][:, :],
                                      ffH[:, ff, :].rearrange("p a n -> p (a n)"),
                                      ALU.subtract).then_inc(ff_lo.sem, 1)

            def ffn(j, first):
                n = 2 * j
                if j == 0:
                    wait(par_land, 16)
                    modulation(0)
                norm(n)
                wait(acc_zero, [1, 3][j])
                dve.sem_inc(passed["dve"].sem, 1)
                off = 2 * ADA_Q * j
                with dve.Fori(0, 8) as i:
                    for m in range(3):
                        ada_piece(m, csil[:, bass.ds(i, 1)],
                                  (ada_land[m], ada_land[m].at(l, i * 16 + 16 * (16 * j + 1))),
                                  (ada_done, ada_done.at(l, i * 3 + (off + m - 2))))
                    up_chunks(i, j, first)
                with dve.Fori(8, 11) as i:
                    up_chunks(i, j, first)
                if j == 0:
                    modulation(1)
                    wait(acc_zero, 2)
                    dve.sem_inc(passed["dve"].sem, 1)
                gate = mod[:, n, 2, :]
                do(dve.memset(sqs[:, :], 0.0))
                dve.sem_inc(passed["dve"].sem, 1)
                with dve.Fori(0, KC // 2) as i:
                    for q in range(6):
                        if j == 0:
                            k2, m = divmod(q, 3)
                            ada_piece(m, csil[:, bass.ds(i * 2 + k2, 1)],
                                      (ada_land[m], ada_land[m].at(l, i * 32 + 16 * (8 + k2 + 1))),
                                      (ada_done, ada_done.at(l, i * 6 + (ADA_Q + q - 2))))
                        if q % 3 == 2:
                            d = i * 2 + q // 3
                            wait(w_used, i * 6 + (first + UP_ITEMS + q + 1))
                            residual(d, gate[:, bass.ds(d, 1)], 4 + q // 3)
                            square(d, n, d + (3 * KC * j + 1))

            ffn(0, 0)
            f = FF_ITEMS
            modulation(2)
            norm(1)

            def halves(t):
                return t.rearrange("p (d t h) -> p d t h", d=2, t=TC)

            dtv, adv, xrv = halves(dtt), halves(adt), halves(sxr)

            def softplus_start():
                wait(dt_tr, 1)
                for d in range(2):
                    src = ps[:, 5, 0:P].rearrange("p (t d h) -> p d t h", d=2, t=TC)[:, d, :, :]
                    bias = par[:, P_DB + d * HEADS:P_DB + (d + 1) * HEADS]
                    do(dve.tensor_tensor(xrv[:, d, :, :], src,
                                         bias.unsqueeze(1).to_broadcast([P, TC, HEADS]), ALU.add))
                dve.scalar_tensor_tensor(sab, sxr, -1.0, sxr, ALU.mult, ALU.max).then_inc(d_abs.sem, 1)

            def softplus_end():
                wait(d_exp, 2)
                do(dve.tensor_scalar(sp1, sab, 2.0, None, ALU.add))
                do(dve.reciprocal(sp1, sp1))
                do(dve.tensor_tensor(sp1, sp1, sab, ALU.mult))
                do(dve.tensor_tensor(sp2, sp1, sp1, ALU.mult))
                do(dve.tensor_scalar(dtt, sp2, 1.0 / 15, None, ALU.mult))
                for odd in (13, 11, 9, 7, 5, 3):
                    do(dve.scalar_tensor_tensor(dtt, dtt, 1.0 / odd, sp2, ALU.add, ALU.mult))
                do(dve.scalar_tensor_tensor(dtt, dtt, 1.0, sp1, ALU.add, ALU.mult))
                do(dve.tensor_scalar(sxr, sxr, 0.0, None, ALU.max))
                do(dve.scalar_tensor_tensor(dtt, dtt, 2.0, sxr, ALU.mult, ALU.add))
                for d in range(2):
                    ea = sea[:, d * HEADS:(d + 1) * HEADS].unsqueeze(1).to_broadcast([P, TC, HEADS])
                    last = dve.scalar_tensor_tensor(adv[:, d, :, :], dtv[:, d, :, :], -1.0, ea,
                                                    ALU.mult, ALU.mult)
                    if d == 0:
                        do(last)
                last.then_inc(a_dt.sem, 1)

            for s in range(CCH):
                wait(cen, s + 1)
                for k in (0, 1, 3, 4):
                    sh = k - KSZ // 2
                    a, b = max(0, -sh), min(SEQ, SEQ - sh)
                    ins = dve.scalar_tensor_tensor(
                        cbuf[:, s % 2, a:b], ps[:, s % 2, a + sh:b + sh],
                        par[:, P_CW + s * KSZ + k:P_CW + s * KSZ + k + 1],
                        cbuf[:, s % 2, a:b], ALU.mult, ALU.add)
                    if k < 4:
                        do(ins)
                ins.then_inc(conv.sem, 1)
                if s == 2:
                    softplus_start()
                if s == 4:
                    softplus_end()

            wait(cs_mm, 1)
            do(dve.tensor_copy(cs3[:, 1:3, :], ps[:, 5, 0:2 * P].rearrange("p (a n) -> p a n", a=2)))
            do(dve.tensor_copy(sxr, cs3[:, 1, :]))
            do(dve.tensor_tensor(cs3[:, 0, :], cs3[:, 2, :], cs3[:, 1, :], ALU.subtract))
            dve.tensor_copy(csT[:, :, :], ps[0:HEADS, 6:8, :]).then_inc(cs_cp.sem, 1)
            wait(cb_mm, 1)
            for d in range(2):
                for g in range(GRP):
                    tri = (triL if d else triU).unsqueeze(1).to_broadcast([P, TC, P])
                    ins = dve.tensor_tensor(cbm[:, d, :, g, :],
                                            ps[:, 2 + g, :].rearrange("p (t n) -> p t n", t=TC),
                                            tri, ALU.mult)
                    if d + g < 2:
                        do(ins)
            ins.then_inc(cb_ok.sem, 1)
            wait(cs_exp, 1)
            to_end, vdec, cdec = (cs3[:, i, :] for i in range(3))
            do(dve.tensor_tensor(uu, dtt, to_end, ALU.mult))

            def weighted(d, c, n):
                if n:
                    wait(st_mm, n)
                dve.tensor_tensor(heads(xw[:, :]), heads(xtok[:, c, :]), per_head(uu, d, c),
                                  ALU.mult).then_inc(u_w.sem, 1)

            def bank2(b):
                return ps[:, b:b + 2, :].rearrange("p b n -> p (b n)")

            def add_state(dst, src, d, c, n):
                wait(st_mm, n + 1)
                if src is None:
                    dve.tensor_copy(dst, bank2(0)).then_inc(st_up.sem, 1)
                    return
                do(dve.tensor_tensor(heads(dst), heads(src), per_head(cdec, d, c), ALU.mult))
                dve.tensor_tensor(dst, dst, bank2(0), ALU.add).then_inc(st_up.sem, 1)

            for n, c in enumerate((3, 2, 1)):
                weighted(1, c, n)
                add_state(sbk[:, c - 1, :], sbk[:, c, :] if n else None, 1, c, n)

            def differences(c):
                for d in range(2):
                    wait(r_land[d], 16 * (c + 1))
                    col = (d * TC + c) * HEADS
                    at_s = sxr[:, col:col + HEADS].unsqueeze(2).to_broadcast([P, HEADS, P])
                    do(dve.tensor_tensor(dec[:, d, :, :], dec[:, d, :, :], at_s, ALU.subtract))
                    dve.tensor_scalar(dec[:, d, :, :], dec[:, d, :, :], 0.0, None,
                                      ALU.min).then_inc(d_dif.sem, 1)

            def masked(c, d):
                wait(d_ex, 2 * c + d + 1)
                view = dec[:, d, :, :].rearrange("p (g h) n -> p g h n", g=GRP)
                cb = cbm[:, d, c, :, :].unsqueeze(2).to_broadcast([P, GRP, HEADS // GRP, P])
                dve.tensor_tensor(view, view, cb, ALU.mult).then_inc(m_ok.sem, 1)

            differences(0)
            for d in range(2):
                dve.tensor_tensor(heads(xdt[:, d, :]), heads(xtok[:, 0, :]), per_head(dtt, d, 0),
                                  ALU.mult).then_inc(x_dt.sem, 1)
            weighted(0, 0, 3)
            for d in range(2):
                masked(0, d)
            for c in range(TC - 1):
                if c:
                    weighted(0, c, 3 + c)
                add_state(sf[c][:, :], sf[c - 1][:, :] if c else None, 0, c, 3 + c)
            for c in range(TC):
                wait(yd_mm, c + 1)
                part = bank2(0)
                for d in range(2):
                    if c == (TC - 1 if d else 0):
                        continue
                    do(dve.tensor_tensor(heads(yt2[:, :]), heads(bank2(2 + 2 * d)),
                                         per_head(vdec, d, c), ALU.mult))
                    do(dve.tensor_tensor(yb[:, :], yt2[:, :], part, ALU.add))
                    part = yb[:, :]
                dve.tensor_tensor(yb[:, :], yb[:, :], zs[:, c, :], ALU.mult).then_inc(y_raw.sem, 1)
                if c + 1 < TC:
                    differences(c + 1)
                wait(y_sq, 2 * c + 2)
                do(dve.tensor_scalar(ssq[:, 2:4], ssq[:, 0:2], 1.0 / SEQ, EPS, ALU.mult, ALU.add))
                dve.reciprocal(ssq[:, 2:4], ssq[:, 2:4]).then_inc(y_ms.sem, 1)
                if c + 1 < TC:
                    masked(c + 1, 0)
                else:
                    wait(l_sum, 1)
                    mean(ms[:, :], 4, QL, l_ms)
                    wait(l_sum, 2)
                    mean(ms2, 5, KVL, l_ms)
                wait(y_rs, c + 1)
                for g in range(GRP):
                    half = yb[:, g * SEQ:(g + 1) * SEQ]
                    dve.tensor_scalar(half, half, ssq[:, 4 + g:5 + g], None,
                                      ALU.mult).then_inc(y_nm.sem, 1)
                if c + 1 < TC:
                    masked(c + 1, 1)
                for b in range(2):
                    wait(y_tr, 2 * c + b + 1)
                    if 2 * c + b:
                        wait(y_lo, 2 * c + b)
                    gain = par[:, P_SG + 4 * b:P_SG + 4 * b + 4].unsqueeze(2).to_broadcast([P, 4, P])
                    dve.tensor_tensor(yt[:, :, :],
                                      ps[:, 6 + b, :].rearrange("p (k n) -> p k n", k=4), gain,
                                      ALU.mult).then_inc(y_f.sem, 1)
                    wait(y_hi, 2 * c + b + 1)
                    put = (slice(None), slice(4 * b, 4 * b + 4), slice(c * P, (c + 1) * P))
                    dve.tensor_tensor(hL[put], yt[:, :, :], hH[put],
                                      ALU.subtract).then_inc(y_lo.sem, 1)

            def mix_residual(first, d, bank):
                wait(w_used, f + first + d + 1)
                dve.scalar_tensor_tensor(x[:, d, :], ps[:, bank + d % 2, :], mod[:, 1, 2, d:d + 1],
                                         x[:, d, :], ALU.mult, ALU.add).then_inc(x_new.sem, 1)

            def scaled(src, gain, row, n, sig_u, sig_hi, sig_lo, dsts, count):
                def lo(c):
                    wait(sig_hi, c + 1)
                    h, lo_ = dsts(c)
                    dve.tensor_tensor(lo_, src[:, c, :], h, ALU.subtract).then_inc(sig_lo.sem, 1)

                for c in range(n, n + count):
                    dve.scalar_tensor_tensor(src[:, c, :], src[:, c, :], gain(c), row,
                                             ALU.mult, ALU.mult).then_inc(sig_u.sem, 1)
                    if c > n:
                        lo(c - 1)
                lo(n + count - 1)

            def rope(r, dstH, dstL):
                wait(rp_mm, r + 1)
                if r:
                    wait(rp_lo, r)
                do(dve.tensor_tensor(rt[1][:, :], ps[:, 2, :], sinT[:, :], ALU.mult))
                do(dve.tensor_tensor(rt[0][:, :], rt[0][:, :], cosT[:, :], ALU.mult))
                dve.tensor_tensor(rt[0][:, :], rt[0][:, :], rt[1][:, :],
                                  ALU.add).then_inc(rp_out.sem, 1)
                wait(rp_hi, r + 1)
                dve.tensor_tensor(dstL, rt[0][:, :], dstH, ALU.subtract).then_inc(rp_lo.sem, 1)

            for d in range(KC):
                mix_residual(I_OS, d, 6)
                if d < 2:
                    wait(l_rs, 1)
                    scaled(rawq, lambda c: par[:, P_QG + c:P_QG + c + 1], rstd[:, :], 2 * d,
                           l_u, l_hi, l_lo, lambda c: (qaH[:, c, :], qaL[:, c, :]), 2)
                if d == 2:
                    wait(l_rs, 2)
                    scaled(rawq, lambda c: par[:, P_KG + c - QC:P_KG + c - QC + 1], rstd2, QC,
                           l_u, l_hi, l_lo, lambda c: (ckH[:, c - QC, :], ckL[:, c - QC, :]), KVC)
                if d == 4:
                    rope(0, krH[:, :], krL[:, :])
            for hg in range(2):
                for h in range(4):
                    wait(k_hi, 4 * hg + h + 1)
                    dve.tensor_tensor(kL[:, h, :], ps[:, h, :], kH[:, h, :],
                                      ALU.subtract).then_inc(k_lo.sem, 1)
                for t in range(TC):
                    wait(v_hi, 4 * hg + t + 1)
                    dve.tensor_tensor(vL[:, t, :], ps[:, 4 + t, :], vH[:, t, :],
                                      ALU.subtract).then_inc(v_lo.sem, 1)
                for p in range(2):
                    rope(1 + 2 * hg + p, qrH[:, p, :], qrL[:, p, :])
                for h in range(4):
                    wait(qn_hi, 4 * hg + h + 1)
                    dve.tensor_tensor(qnL[:, h, :], ps[:, 3 + h, :], qnH[:, h, :],
                                      ALU.subtract).then_inc(qn_lo.sem, 1)
                for s in range(SOFT + 2):
                    n = SOFT * hg + s
                    if s < SOFT:
                        st = sm[:, n % 3, :]
                        wait(s_mm, n + 1)
                        if n >= 3:
                            wait(s_nm, n - 2)
                        do(dve.reduce_max(st[:, 0:1], ps[:, 3 + n % 3, :], AXX))
                        dve.tensor_scalar(st[:, 1:2], st[:, 0:1], -ATT_SCALE, None,
                                          ALU.mult).then_inc(s_mx.sem, 1)
                    if 1 <= s < SOFT + 1:
                        m = n - 1
                        st = sm[:, m % 3, :]
                        wait(s_ex, m + 1)
                        do(dve.reciprocal(st[:, 3:4], st[:, 2:3]))
                        dve.tensor_scalar(pr[:, m % 3, :], pr[:, m % 3, :], st[:, 3:4], None,
                                          ALU.mult).then_inc(s_nm.sem, 1)
                    if s >= 2:
                        m = n - 2
                        t = m % TC
                        put = (slice(None), slice(None), slice(t * P, (t + 1) * P))
                        wait(p_hi, m + 1)
                        dve.tensor_tensor(ptL[put],
                                          ps[:, 6 + m % 2, :].rearrange("p (k n) -> p k n", k=TC),
                                          ptH[put], ALU.subtract).then_inc(p_lo.sem, 1)
            wait(a_sum, 1)
            mean(ms[:, :], 6, DM, a_ms)
            wait(a_rs, 1)
            scaled(ofm, lambda c: par[:, P_AG + c:P_AG + c + 1], rstd[:, :], 0, a_u, a_hi, a_lo,
                   lambda c: (hH[:, c, :], hL[:, c, :]), MH)
            do(dve.memset(sqs[:, :], 0.0))
            for d in range(KC):
                mix_residual(I_OA, d, 4)
                square(d, 1, 2 * KC + d + 1)
            ffn(1, FF_ITEMS + MX_ITEMS)
            assert do.n == DVE_STEPS, do.n

        dve.wait_ge(f_sum.sem, 1)
        dve.tensor_scalar(ms[:, :], ps[:, 6, :], 1.0 / DM, EPS,
                          ALU.mult, ALU.add).then_inc(p_step.sem, 1)
        dve.wait_ge(p_step.sem, PRO_ANGLES + 1)
        dve.reciprocal(ms[:, :], ms[:, :]).then_inc(f_ms.sem, 1)
        dve.wait_ge(f_rs.sem, 1)
        for c in range(KC):
            dve.scalar_tensor_tensor(sq[:, c, :], x[:, c, :], fing[:, c:c + 1], rstd[:, :],
                                     ALU.mult, ALU.mult).then_inc(f_out.sem, 1)

    @block.tensor
    def _(pe):
        pe.sem_inc(w_used.sem, 2)
        pe.wait_ge(pos_land.sem, 64)

        def three(dst, aH, aL, bH, bL, first, last):
            pe.matmul(dst, aH, bH, start=first, stop=False)
            pe.matmul(dst, aH, bL, start=False, stop=False)
            return pe.matmul(dst, aL, bH, start=False, stop=last)

        with pe.Fori(0, DEPTH) as l:

            def wait(sig, n):
                pe.wait_ge(sig.sem, sig.at(l, n))

            def mod_vectors(g):
                wait(ada_done, ADA_Q * g)
                for q in range(3 * KC):
                    m, c = divmod(q, KC)
                    last = pe.matmul(ps[:, 7, q:q + 1], acc[:, m, c * P:(c + 1) * P],
                                     ones[:, 0:1], start=True, stop=True)
                last.then_inc(mod_sum.sem, 1)

            def sum_squares(n):
                wait(sq_add, n * KC)
                pe.matmul(ps[:, 6, :], ones, sqs[:, :], start=True, stop=True
                          ).then_inc(n_sum.sem, 1)

            def blocks(dst, slot, n, rhsH, rhsL, k0=0, last=KC, width=P, off=0,
                       arrive=None):
                for b in range(n):
                    if arrive is not None:
                        wait(arrive[0], arrive[1] + b + 1)
                    w = slice(b * width + off, b * width + off + P)
                    k = k0 + b
                    end = three(dst, wH[slot][:, w], wL[slot][:, w], rhsH[:, k, :], rhsL[:, k, :],
                                k == 0, k == last - 1)
                return end

            def ffn(j, first):
                if j == 0:
                    mod_vectors(0)
                sum_squares(2 * j)
                pe.sem_inc(passed["pe"].sem, 1)
                with pe.Fori(0, FC // 2) as i:
                    for s in range(2):
                        for q in range(2):
                            free = sg_done if q == 0 else prod_done
                            wait(free, i * 2 + (FC * j + s - 1))
                            wait(w_lo, i * 4 + (first + 2 * s + q + 1))
                            blocks(ps[:, 2 * q + s, :], q, KC, hH, hL,
                                   arrive=None if s or q else (h_lo, 2 * j * KC)).then_inc(w_used.sem, 1)
                if j == 0:
                    mod_vectors(1)
                pe.sem_inc(passed["pe"].sem, 1)
                with pe.Fori(0, KC // 2) as i:
                    for q in range(6):
                        s, part = divmod(q, DN_PER)
                        if part == 0:
                            wait(x_new, i * 2 + (3 * KC * j + s - 1))
                        wait(w_lo, i * 6 + (first + UP_ITEMS + q + 1))
                        n = min(8, FC - 8 * part)
                        wait(ff_lo, FC * j + 8 * part + n)
                        blocks(ps[:, 4 + s, :], q % 2, n, ffH, ffL, 8 * part,
                               FC).then_inc(w_used.sem, 1)

            ffn(0, 0)
            f = FF_ITEMS

            def ready(n):
                wait(w_lo, f + n + 1)
                return n % 2

            mod_vectors(2)
            sum_squares(1)
            slot = ready(I_DT)
            for k in range(KC):
                wait(h_lo, KC + k + 1)
                w = slice(k * 2 * HEADS, (k + 1) * 2 * HEADS)
                last = three(ps[0:2 * HEADS, 4, :], wH[slot][:, w], wL[slot][:, w],
                             hH[:, k, :], hL[:, k, :], k == 0, k == KC - 1)
            last.then_inc(w_used.sem, 1)
            for s in range(CCH + 2):
                if s < CCH:
                    if s >= 2:
                        wait(conv, s - 1)
                    slot = ready(I_CONV + s)
                    blocks(ps[:, s % 2, :], slot, KC, hH, hL).then_inc(w_used.sem, 1)
                if s == 0:
                    wait(dt_cp, 1)
                    pe.sem_inc(passed["pe"].sem, 1)
                    for t in range(TC):
                        last = pe.transpose(ps[:, 5, t * 2 * HEADS:(t + 1) * 2 * HEADS],
                                            dtf[:, t * P:(t + 1) * P],
                                            ident[0:2 * HEADS, 0:2 * HEADS])
                    last.then_inc(dt_tr.sem, 1)
                if s - 2 in TR:
                    c = s - 2
                    n = TR.index(c)
                    wait(csilu, c + 1)
                    if n >= 2:
                        wait(tev, n - 1)
                    src = bfm[:, c, :] if c < 2 else xs[:, c % 2, :]
                    for t in range(TC):
                        last = pe.transpose(ps[:, 2 + c % 2, t * P:(t + 1) * P],
                                            src[:, t * P:(t + 1) * P], ident)
                    last.then_inc(trx.sem, 1)
            wait(a_dt, 1)
            half = HEADS * TC
            for d, tri in ((0, triU), (1, triL)):
                col = slice(d * half, (d + 1) * half)
                pe.matmul(ps[:, 5, d * half:(d + 1) * half], tri, adt[:, col], start=True, stop=True)
                pe.matmul(ps[:, 5, P + d * half:P + (d + 1) * half], ones, adt[:, col],
                          start=True, stop=True)
            for d, tri in ((0, triU), (1, triL)):
                for t in range(TC):
                    col = (d * TC + t) * HEADS
                    last = pe.matmul(ps[0:HEADS, 6 + d, t * P:(t + 1) * P],
                                     adt[:, col:col + HEADS], tri, start=True, stop=True)
            last.then_inc(cs_mm.sem, 1)
            wait(tev, len(TR))
            for g in range(GRP):
                for t in range(TC):
                    tok = slice(t * P, (t + 1) * P)
                    last = pe.matmul(ps[:, 2 + g, tok], bfm[:, g, tok], cfm[:, g, tok],
                                     start=True, stop=True)
            last.then_inc(cb_mm.sem, 1)

            def state(c, n):
                wait(u_w, n + 1)
                for g in range(GRP):
                    last = pe.matmul(ps[:, g, :], btok[:, c, g * NST:(g + 1) * NST],
                                     xw[:, g * SEQ:(g + 1) * SEQ], start=True, stop=True)
                last.then_inc(st_mm.sem, 1)

            wait(cs_cp, 1)
            for z in range(2):
                if z:
                    wait(z_ev, TC)
                for q in range(4):
                    slot = ready(I_Z + 4 * z + q)
                    for t in range(TC):
                        tok = slice(t * P, (t + 1) * P)
                        for b in range(2):
                            k = 2 * q + b
                            w = slice(b * SEQ, (b + 1) * SEQ)
                            last = three(ps[:, 4 + t, :], hH[:, k, tok], hL[:, k, tok],
                                         wH[slot][:, w], wL[slot][:, w], k == 0, k == KC - 1)
                    last.then_inc(w_used.sem, 1)
                    n = 4 * z + q - 2
                    if n in (0, 2, 4):
                        if n:
                            wait(st_up, n // 2)
                        state(3 - n // 2, n // 2)

            def off_diagonal(c):
                tok = slice(c * P, (c + 1) * P)
                if c:
                    wait(y_raw, c)
                for d in range(2):
                    if c == (TC - 1 if d else 0):
                        continue
                    src = sbk[:, c, :] if d else sf[c - 1][:, :]
                    for g in range(GRP):
                        pe.matmul(ps[:, 2 + 2 * d + g, :], cfm[:, g, tok],
                                  src[:, g * SEQ:(g + 1) * SEQ], start=True, stop=True)
                wait(skip_x, c + 1)
                for g in range(GRP):
                    pe.matmul(ps[:, g, :], ident, xw[:, g * SEQ:(g + 1) * SEQ],
                              start=True, stop=False)

            def diagonal(c):
                wait(x_dt, 2 * c + 2)
                wait(m_ok, 2 * c + 2)
                for h in range(HEADS):
                    g, col = divmod(h * HD, SEQ)
                    for d in range(2):
                        last = pe.matmul(ps[:, g, col:col + HD], dec[:, d, h, :],
                                         xdt[:, d, h * HD:(h + 1) * HD],
                                         start=False, stop=(h % 8 == 7 and d == 1))
                last.then_inc(yd_mm.sem, 1)

            def transposed(c):
                wait(y_nm, 2 * c + 2)
                if c:
                    wait(y_lo, 2 * c)
                for b in range(2):
                    for k in range(4):
                        col = (4 * b + k) * P
                        last = pe.transpose(ps[:, 6 + b, k * P:(k + 1) * P], yb[:, col:col + P],
                                            ident)
                    last.then_inc(y_tr.sem, 1)

            wait(cb_ok, 1)
            for q in range(7):
                if q >= 2:
                    wait(q_ev, q - 1)
                slot = ready(I_QA + q)
                blocks(ps[:, 2 + q % 2, :], slot, KC, hH, hL).then_inc(w_used.sem, 1)
                if q < 3:
                    wait(st_up, 3 + q)
                    state(q, 3 + q)
                if q == 4:
                    wait(st_up, 6)
                    wait(z_ev, 2 * TC)
                    off_diagonal(0)
                    diagonal(0)
            wait(q_ev, 7)
            for c in range(TC):
                if c + 1 < TC:
                    off_diagonal(c + 1)
                    transposed(c)
                    diagonal(c + 1)
                else:
                    for q in range(6):
                        wait(l_sq, q + 1)
                        bank, k, n = (4, q, QC) if q < QC else (5, q - QC, KVC)
                        last = pe.matmul(ps[:, bank, :], ones, lsq[:, q, :],
                                         start=(k == 0), stop=(k == n - 1))
                        if k == n - 1:
                            last.then_inc(l_sum.sem, 1)
                    transposed(c)

            def rotate(r):
                wait(rp_in, r + 1)
                pe.matmul(ps[:, 2, :], perm, rt[0][:, :], start=True, stop=True
                          ).then_inc(rp_mm.sem, 1)

            def out_half(first, new, bank, arrive=None):
                for d in range(KC):
                    wait(x_new, new + d - 1)
                    slot = ready(first + d)
                    blocks(ps[:, bank + d % 2, :], slot, KC, hH, hL,
                           arrive=None if d else arrive).then_inc(w_used.sem, 1)
                    if first == I_OS and d == 4:
                        rotate(0)

            wait(y_lo, 2 * TC)
            out_half(I_OS, KC, 6)

            wait(l_lo, 6)
            wait(rp_lo, 1)
            for hg in range(2):
                i0 = I_MLA + 5 * hg
                if hg:
                    wait(o_ev, 4)
                    wait(p_lo, SOFT)
                slot = ready(i0)
                for h in range(4):
                    for k in range(KVC):
                        w = slice((k * 4 + h) * P, (k * 4 + h + 1) * P)
                        last = three(ps[:, h, :], wH[slot][:, w], wL[slot][:, w],
                                     ckH[:, k, :], ckL[:, k, :], k == 0, k == KVC - 1)
                last.then_inc(w_used.sem, 1)
                slot = ready(i0 + 1)
                if hg == 0:
                    wait(x_new, 2 * KC)
                for t in range(TC):
                    tok = slice(t * P, (t + 1) * P)
                    for k in range(KVC):
                        w = slice(k * SEQ, (k + 1) * SEQ)
                        last = three(ps[:, 4 + t, :], ckH[:, k, tok], ckL[:, k, tok],
                                     wH[slot][:, w], wL[slot][:, w], k == 0, k == KVC - 1)
                last.then_inc(w_used.sem, 1)
                wait(k_lo, 4 * hg + 4)
                slot = ready(i0 + 2)
                for p in range(2):
                    last = blocks(ps[:, p, :], slot, QC, qaH, qaL, last=QC, width=2 * P, off=p * P)
                last.then_inc(w_used.sem, 1)
                for p in range(2):
                    rotate(1 + 2 * hg + p)
                    wait(rp_out, 2 + 2 * hg + p)
                wait(v_lo, 4 * hg + 4)
                for p in range(2):
                    slot = ready(i0 + 3 + p)
                    for h in range(2):
                        last = blocks(ps[:, 3 + 2 * p + h, :], slot, QC, qaH, qaL, last=QC,
                                      width=2 * P, off=h * P)
                    last.then_inc(w_used.sem, 1)
                wait(rp_lo, 3 + 2 * hg)
                wait(qn_lo, 4 * hg + 4)
                for s in range(SOFT + 3):
                    n = SOFT * hg + s
                    if s < SOFT:
                        h, t = divmod(s, TC)
                        tok = slice(t * P, (t + 1) * P)
                        bank = ps[:, 3 + n % 3, :]
                        if n >= 3:
                            wait(s_ex, n - 2)
                        three(bank, qnH[:, h, tok], qnL[:, h, tok], kH[:, h, :], kL[:, h, :],
                              True, False)
                        r = slice((h % 2) * ROPE, (h % 2 + 1) * ROPE)
                        three(bank, qrH[r, h // 2, tok], qrL[r, h // 2, tok], krH[r, :],
                              krL[r, :], False, True).then_inc(s_mm.sem, 1)
                    if s >= 3 and (s - 3) % TC == TC - 1:
                        h = (n - 3) // TC
                        wait(p_lo, n - 2)
                        if h:
                            wait(o_ev, h)
                        col = slice((h % 4) * VD, (h % 4 + 1) * VD)
                        for k in range(TC):
                            last = three(ps[:, 2, :], vH[:, k, col], vL[:, k, col],
                                         ptH[:, k, :], ptL[:, k, :], k == 0, k == TC - 1)
                        last.then_inc(o_mm.sem, 1)
                    if 2 <= s < SOFT + 2:
                        m = n - 2
                        wait(s_nm, m + 1)
                        if m >= 2:
                            wait(p_lo, m - 1)
                        for k in range(TC):
                            last = pe.transpose(ps[:, 6 + m % 2, k * P:(k + 1) * P],
                                                pr[:, m % 3, k * P:(k + 1) * P], ident)
                        last.then_inc(p_tr.sem, 1)
            wait(a_add, MH - 1)
            pe.matmul(ps[:, 6, :], ones, asum[:, :], start=True, stop=True).then_inc(a_sum.sem, 1)
            out_half(I_OA, 2 * KC, 4, (a_lo, 0))
            ffn(1, FF_ITEMS + MX_ITEMS)

        pe.wait_ge(sq_add.sem, sq_add.at(DEPTH, 0))
        pe.matmul(ps[:, 6, :], ones, sqs[:, :], start=True, stop=True).then_inc(f_sum.sem, 1)



def chunks(v, n):
    return np.swapaxes(v.reshape(v.shape[:-1] + (n, P)), -1, -2)


def blocks_of(w, cols):
    w = w[:, cols]
    return np.transpose(w.reshape(-1, P, w.shape[1]), (1, 0, 2)).reshape(P, -1)


def padded(a):
    out = np.zeros((P, ITEM), a.dtype)
    out[:, :a.shape[1]] = a
    return out


def up_items(g, u):
    out = []
    for f in range(FC):
        for w in (g, u):
            out.append(blocks_of(w, slice(f * P, (f + 1) * P)))
    return out


def down_items(w):
    out = []
    for d in range(KC):
        b = blocks_of(w, slice(d * P, (d + 1) * P))
        out += [padded(b[:, q * ITEM:(q + 1) * ITEM]) for q in range(DN_PER)]
    return out


def mixer_items(w_in, w_q, w_kv, w_out):
    xbc0 = DM
    dt0 = xbc0 + DM + 2 * GRP * NST
    qa0 = dt0 + 2 * HEADS
    kv0 = qa0 + QL
    items = [padded(blocks_of(w_in, slice(dt0, dt0 + 2 * HEADS)))]
    for c in list(range(KC, CCH)) + list(range(KC)):
        items.append(blocks_of(w_in, slice(xbc0 + c * P, xbc0 + (c + 1) * P)))
    for z in range(2):
        b = blocks_of(w_in, slice(z * SEQ, (z + 1) * SEQ))
        items += [b[:, q * ITEM:(q + 1) * ITEM] for q in range(4)]
    for c in range(QC):
        items.append(blocks_of(w_in, slice(qa0 + c * P, qa0 + (c + 1) * P)))
    for c in range(KVC):
        items.append(blocks_of(w_in, slice(kv0 + c * P, kv0 + (c + 1) * P)))
    kr = np.arange(kv0 + KVL, kv0 + KVL + ROPE)
    items.append(blocks_of(w_in, np.concatenate([kr, kr])))
    for d in range(KC):
        items.append(blocks_of(w_out[:DM], slice(d * P, (d + 1) * P)))
    for hg in range(2):
        hs = range(4 * hg, 4 * hg + 4)
        k = np.concatenate([np.arange(h * 256, h * 256 + NOPE) for h in hs])
        q = np.concatenate([np.arange(h * 192, h * 192 + NOPE) for h in hs])
        r = np.concatenate([np.arange(h * 192 + NOPE, (h + 1) * 192) for h in hs])
        items.append(blocks_of(w_kv, k))
        items.append(blocks_of(w_kv, k + NOPE))
        items.append(blocks_of(w_q, r))
        items += [blocks_of(w_q, q[:2 * P]), blocks_of(w_q, q[2 * P:])]
    for d in range(KC):
        items.append(blocks_of(w_out[DM:], slice(d * P, (d + 1) * P)))
    assert len(items) == MX_ITEMS
    return items


def kernel(**inputs):
    import concourse.bacc as _bacc
    from concourse.bass_utils import run_bass_kernel_spmd as _run

    a = {k: np.asarray(v) for k, v in inputs.items()}
    row = np.arange(P)
    le = (row[:, None] <= row[None, :]).astype(np.float32)
    turn = np.zeros((P, P), np.float32)
    for m in range(P):
        first = m % ROPE < ROPE // 2
        turn[m + (ROPE // 2 if first else -(ROPE // 2)), m] = -1.0 if first else 1.0
    consts = np.stack([le, le.T, np.ones((P, P), np.float32), np.eye(P, dtype=np.float32), turn], 1)
    power = (np.arange(0, ROPE, 2, dtype=np.float32) / ROPE).astype(np.float32)
    inv = (np.float32(1.0) / np.power(np.float32(THETA), power)).astype(np.float32)
    invf = inv[row % (ROPE // 2)][:, None]

    def wide(v):
        return np.broadcast_to(v.reshape(1, -1), (P, v.size))

    params = []
    order = list(range(KC, CCH)) + list(range(KC))
    for l in range(DEPTH):
        cw = np.transpose(a["conv_w"][l].reshape(KSZ, CCH, P)[:, order], (2, 1, 0)).reshape(P, -1)
        params.append(np.concatenate([
            cw, chunks(a["conv_b"][l], CCH)[:, order],
            np.transpose(chunks(a["norm_g"][l], KC), (1, 0, 2)).reshape(P, -1),
            chunks(a["ssd_norm_g"][l], KC), chunks(a["q_norm_g"][l], QC),
            chunks(a["kv_norm_g"][l], KVC), chunks(a["attn_norm_g"][l], KC),
            chunks(a["ada_b"][l], 72),
            wide(a["dt_bias"][l]), wide(a["a_log"][l]), wide(a["d_skip"][l])], axis=1))
    w_up, w_dn, w_mx = [], [], []
    for l in range(DEPTH):
        for j in range(2):
            w_up += up_items(a["ffn_w_gate"][l, j], a["ffn_w_up"][l, j])
            w_dn += down_items(a["ffn_w_down"][l, j])
        w_mx += mixer_items(a["w_in"][l], a["w_q_b"][l], a["w_kv_b"][l], a["w_out"][l])
    ada = a["ada_w"].reshape(DEPTH, KC, P, 3, 3, DM).transpose(0, 3, 1, 4, 2, 5)
    arrays = {
        "xT": np.transpose(a["x"][0].reshape(SEQ, KC, P), (2, 1, 0)),
        "cT": chunks(a["c"][0], KC),
        "pos": a["positions"].astype(np.int32, copy=False).reshape(1, SEQ),
        "invf": invf, "consts": consts, "params": np.stack(params),
        "finalg": chunks(a["final_norm_g"], KC),
        "w_up": np.stack(w_up), "w_dn": np.stack(w_dn), "w_mx": np.stack(w_mx),
        "w_ada": ada.reshape(DEPTH * 3 * ADA_Q, P, DM),
    }
    arrays = {k: np.ascontiguousarray(v) for k, v in arrays.items()}
    nc = _bacc.Bacc("TRN2", target_bir_lowering=False, num_devices=1)
    args = [nc.dram_tensor(n, v.shape, mybir.dt.from_np(v.dtype), kind="ExternalInput").ap()
            for n, v in arrays.items()]
    out = nc.dram_tensor("out", (P, KC, SEQ), F32, kind="ExternalOutput").ap()
    build_trunk(nc, *args, out)
    r = _run(nc, [arrays], core_ids=[0])
    got = r.results[0]["out"]
    return np.ascontiguousarray(np.transpose(got, (2, 1, 0)).reshape(1, SEQ, DM))
```

```python
from contextlib import ExitStack

import numpy as np

import concourse.bass as bass
from concourse import mybir

F32 = mybir.dt.float32
F32R = mybir.dt.float32r
I32 = mybir.dt.int32
ACT = mybir.ActivationFunctionType
ALU = mybir.AluOpType
AXX = mybir.AxisListType.X

P = 128
DEPTH = 2
SEQ = 512
DM = 1024
DFF = 2816
KC = DM // P
FC = DFF // P
TC = SEQ // P
HEADS = 16
HD = 64
GRP = 2
NST = 128
KSZ = 5
CCH = (DM + 2 * GRP * NST) // P
MH = 8
NOPE, ROPE, VD = 128, 64, 128
QL, KVL = 512, 256
QC, KVC = QL // P, KVL // P
EPS = 1e-6
SOFT = 4 * TC
ATT_SCALE = float(NOPE + ROPE) ** -0.5
THETA = 10000.0

ITEM = 8 * P
UP_ITEMS = 2 * FC
DN_PER = 3
DN_ITEMS = KC * DN_PER
MX_ITEMS = 1 + CCH + 8 + QC + KVC + 1 + KC + 2 * 5 + KC
FF_ITEMS = UP_ITEMS + DN_ITEMS
NI = 2 * FF_ITEMS + MX_ITEMS
assert NI % 2 == 0 and FF_ITEMS % 2 == 0
TR = [0, 1] + list(range(4, CCH))
I_DT, I_CONV, I_Z = 0, 1, 1 + CCH
I_QA = I_Z + 8
I_KV = I_QA + QC
I_KR = I_KV + KVC
I_OS = I_KR + 1
I_MLA = I_OS + KC
I_OA = I_MLA + 10

P_CW = 0
P_CB = P_CW + CCH * KSZ
P_NG = P_CB + CCH
P_SG = P_NG + 3 * KC
P_QG = P_SG + KC
P_KG = P_QG + QC
P_AG = P_KG + KVC
P_AB = P_AG + KC
P_DB = P_AB + 72
P_AL = P_DB + 2 * HEADS
P_DS = P_AL + 2 * HEADS
NPAR = P_DS + HEADS

DVE_STEPS = 180
ADA_Q = 24

PRO_ANGLES = 12
TWO_PI = 2 * np.pi
C1 = 6.28125
C2 = float(np.array([np.array([TWO_PI - C1], np.float32).view(np.int32)[0] & -4096], np.int32).view(np.float32)[0])
C3 = float(TWO_PI - C1 - C2)
ROUND = 1.5 * 2.0 ** 23
PI_IN = 3.1415925


class Signal:

    def __init__(self, sem, per, first=0):
        self.sem, self.per, self.first = sem, per, first

    def at(self, layer, n):
        return layer * self.per + (self.first + n)


class Chain:

    def __init__(self, eng, sig, layer):
        self.eng, self.sig, self.layer, self.n = eng, sig, layer, 0

    def __call__(self, ins):
        ins.then_inc(self.sig.sem, 1)
        self.n += 1
        self.eng.wait_ge(self.sig.sem, self.sig.at(self.layer, self.n))


def build_trunk(nc, xT, cT, pos, invf, consts, params, finalg, w_up, w_dn, w_mx, w_ada, out):
    ctx = ExitStack()
    base = -(-nc.sbuf_base // 32) * 32
    top = [base]

    def at(name, shape, dt, off):
        return nc.alloc_sbuf_tensor_at(name, shape, dt, offset=off)

    def sb(name, shape, dt=F32):
        size = 4
        for d in shape[1:]:
            size *= d
        off = top[0]
        top[0] += -(-size // 32) * 32
        return at(name, shape, dt, off)

    x = sb("x_res", [P, KC, SEQ])
    H0 = top[0]
    hH = sb("h_hi", [P, KC, SEQ], F32R)
    hL = sb("h_lo", [P, KC, SEQ], F32R)
    raw = [sb(f"w_raw{j}", [P, ITEM]) for j in range(2)]
    wH = [sb(f"w_hi{j}", [P, ITEM], F32R) for j in range(2)]
    wL = [sb(f"w_lo{j}", [P, ITEM], F32R) for j in range(2)]
    cst = sb("consts_sb", [P, 5, P])
    triU, triL, ones, ident, perm = (cst[:, i, :] for i in range(5))
    cosT = sb("cosT", [P, SEQ])
    sinT = sb("sinT", [P, SEQ])
    par = sb("par", [P, NPAR])
    fing = sb("fing", [P, KC])
    mod = sb("mod", [P, 3, 3, KC])
    csil = sb("csil", [P, KC])
    cin = sb("cin", [P, KC])
    invs = sb("invs", [P, 1])
    TMP0 = top[0]
    tmp_a = sb("tmp_a", [P, SEQ])
    tmp_b = sb("tmp_b", [P, SEQ])
    stat = sb("norm_stat", [P, 2, 2, TC])
    A0 = top[0]
    ada_in = sb("ada_in", [P, 3, DM])
    acc = sb("ada_acc", [P, 3, DM])
    R0 = top[0]
    K = 1024
    assert R0 + 92 * K <= nc.sbuf_usable_end, (R0, nc.sbuf_usable_end)

    ffH = at("ff_hi", [P, FC, SEQ], F32R, R0)
    ffL = at("ff_lo", [P, FC, SEQ], F32R, R0 + 44 * K)
    sg = at("silu_gate", [P, 2, SEQ], F32, R0 + 88 * K)
    sqs = at("sq_sum", [P, SEQ], F32, R0 + 90 * K)
    prod = [tmp_a, tmp_b]
    sq = at("scaled", [P, KC, SEQ], F32, R0)

    rawq = at("q_kv_raw", [P, 7, SEQ], F32, R0)
    zs = at("silu_z", [P, TC, DM], F32, R0 + 14 * K)
    xtok = at("x_tok", [P, TC, DM], F32, R0 + 30 * K)
    dec = at("decay", [P, 2, HEADS, P], F32, R0 + 46 * K)
    cbuf = at("conv_acc", [P, 2, SEQ], F32, R0 + 46 * K)
    xs = at("x_feat", [P, 2, SEQ], F32, R0 + 50 * K)
    xdt = at("x_dt", [P, 2, DM], F32, R0 + 62 * K)
    xw = at("x_w", [P, DM], F32, R0 + 70 * K)
    yb = at("y_buf", [P, DM], F32, R0 + 74 * K)
    bfm = at("b_feat", [P, GRP, SEQ], F32, R0 + 74 * K)
    btok = at("b_tok", [P, TC, GRP * NST], F32, R0 + 78 * K)
    sf = [at("state_f1", [P, DM], F32, R0 + 82 * K), at("state_f2", [P, DM], F32, TMP0),
          at("state_f3", [P, DM], F32, R0 + 78 * K)]
    yt = at("y_feat", [P, 4, P], F32, R0 + 86 * K)
    ytl = at("y_feat_last", [P, 4, P], F32, R0 + 70 * K)
    small = at("ssd_small", [P, 8, P], F32, R0 + 88 * K)
    dtt, adt, sxr, sab, sp1, sp2, uu, sea = (small[:, i, :] for i in range(8))
    cs3 = at("cs3", [P, 3, P], F32, R0 + 92 * K)
    assert R0 + 94 * K + 512 <= nc.sbuf_usable_end, (R0 + 94 * K + 512, nc.sbuf_usable_end)
    sbk = at("state_b", [P, 3, DM], F32, A0)
    cbm = at("cb_masked", [P, 2, TC, GRP, P], F32, A0 + 12 * K)
    cfm = at("c_feat", [P, GRP, SEQ], F32, A0 + 20 * K)
    csT = at("cs_rows", [HEADS, 2, SEQ], F32, R0 + 62 * K)
    dtf = at("dt_feat", [2 * HEADS, SEQ], F32, R0 + 62 * K)
    yt2 = at("y_part", [P, DM], F32, R0 + 94 * K + 512)
    assert R0 + 98 * K + 512 <= nc.sbuf_usable_end, (R0 / K, nc.sbuf_usable_end)
    ssq = at("y_ssq", [P, 8], F32, R0 + 92 * K + 1536)

    ofm = at("att_out", [P, MH, SEQ], F32, R0)
    qaH = at("qa_hi", [P, QC, SEQ], F32R, R0 + 16 * K)
    qaL = at("qa_lo", [P, QC, SEQ], F32R, R0 + 24 * K)
    ckH = at("ckv_hi", [P, KVC, SEQ], F32R, R0 + 32 * K)
    ckL = at("ckv_lo", [P, KVC, SEQ], F32R, R0 + 36 * K)
    krH = at("kr_hi", [P, SEQ], F32R, R0 + 40 * K)
    krL = at("kr_lo", [P, SEQ], F32R, R0 + 42 * K)
    kH = at("k_hi", [P, 4, SEQ], F32R, H0)
    kL = at("k_lo", [P, 4, SEQ], F32R, H0 + 8 * K)
    vH = at("v_hi", [P, TC, 4 * VD], F32R, H0 + 16 * K)
    vL = at("v_lo", [P, TC, 4 * VD], F32R, H0 + 24 * K)
    qnH = at("qn_hi", [P, 4, SEQ], F32R, R0 + 60 * K)
    qnL = at("qn_lo", [P, 4, SEQ], F32R, R0 + 68 * K)
    qrH = at("qr_hi", [P, 2, SEQ], F32R, R0 + 76 * K)
    qrL = at("qr_lo", [P, 2, SEQ], F32R, R0 + 80 * K)
    oH = (at("o_hi_012", [P, 3, SEQ], F32R, R0 + 48 * K),
          at("o_hi_3", [P, 1, SEQ], F32R, R0 + 84 * K),
          at("o_hi_4567", [P, 4, SEQ], F32R, R0 + 16 * K))
    oL = (at("o_lo_012", [P, 3, SEQ], F32R, R0 + 54 * K),
          at("o_lo_3", [P, 1, SEQ], F32R, R0 + 86 * K),
          at("o_lo_4567", [P, 4, SEQ], F32R, R0 + 24 * K))
    o_place = [(0, 0), (0, 1), (0, 2), (1, 0), (2, 0), (2, 1), (2, 2), (2, 3)]
    asq = at("att_sq", [P, SEQ], F32, R0 + 44 * K)
    asum = at("att_sq_sum", [P, SEQ], F32, R0 + 46 * K)
    ptH = at("pT_hi", [P, TC, SEQ], F32R, A0)
    ptL = at("pT_lo", [P, TC, SEQ], F32R, A0 + 8 * K)
    lsq = at("lora_sq", [P, 6, SEQ], F32, A0)
    pr = at("probs", [P, 4, SEQ], F32, A0 + 16 * K)
    rt = [tmp_a, tmp_b]
    sm = at("softmax_small", [P, 4, 4], F32, R0 + 92 * K)

    posi = at("pos_i", [P, SEQ], I32, R0)
    ang = at("ang", [P, SEQ], F32, R0 + 2 * K)
    kk = at("turns", [P, SEQ], F32, R0 + 4 * K)
    tmp = at("ang_tmp", [P, SEQ], F32, R0 + 6 * K)
    pro_in = at("ada_in_more", [P, 3, DM], F32, R0 + 16 * K)

    ps = ctx.enter_context(nc.psum_tensor("banks", [P, 8, SEQ], F32))
    cs_dram = nc.dram_tensor("cs_rows_dram", (2, HEADS, SEQ), F32, kind="Internal").ap()

    def sem(name, per=0, first=0):
        return Signal(ctx.enter_context(nc.semaphore(name)), per, first)

    go = sem("go")
    passed = {e: sem(f"passed_{e}") for e in ("gp", "dve", "pe")}
    w_land = [sem(f"w_land{j}", 16 * NI // 2) for j in range(2)]
    w_hi = sem("w_hi", NI)
    w_lo = sem("w_lo", NI, 2)
    w_used = sem("w_used", NI, 2)
    ada_land = [sem(f"ada_land{m}", 16 * ADA_Q, 16 * 4) for m in range(3)]
    pro_land = [sem(f"ada_more_land{m}") for m in range(3)]
    ada_done = sem("ada_done", 3 * ADA_Q, ADA_Q + 3)
    acc_zero = sem("acc_zero", 3, 1)
    mod_sum = sem("mod_sum", 3)
    c_land = sem("c_land")
    x_land = sem("x_land")
    x_sq = sem("x_squared")
    pos_land = sem("pos_land")
    par_land = sem("par_land", 16)
    csil_done = sem("csil_done")
    p_step = sem("prologue_step")
    trig_done = sem("trig_done")
    x_new = sem("x_new", 4 * KC, 2)
    sq_mul = sem("sq_mul", 3 * KC)
    sq_add = sem("sq_added", 3 * KC, KC + 1)
    n_sum = sem("n_sum", 3)
    ms_done = sem("ms_done", 3)
    rstd_done = sem("rstd_done", 3)
    n_row = sem("rstd_row", 3)
    u_done = sem("u_done", 3 * KC)
    h_hi = sem("h_hi_done", 3 * KC)
    h_lo = sem("h_lo_done", 3 * KC)
    sg_done = sem("sg_done", 2 * FC, 2)
    prod_done = sem("prod_done", 2 * FC, 2)
    ff_hi = sem("ff_hi_done", 2 * FC)
    ff_lo = sem("ff_lo_done", 2 * FC, 2)
    v_step = sem("v_step", DVE_STEPS)
    cen = sem("conv_centre", CCH)
    conv = sem("conv_done", CCH)
    csilu = sem("conv_silu", CCH)
    trx = sem("x_transposed", len(TR))
    tev = sem("x_tok_done", len(TR))
    z_ev = sem("z_done", 2 * TC)
    q_ev = sem("q_raw_done", 7)
    dt_cp = sem("dt_copied", 1)
    dt_tr = sem("dt_transposed", 1)
    d_abs = sem("dt_abs", 1)
    d_exp = sem("dt_exp", 2)
    a_dt = sem("a_dt_done", 1)
    cs_mm = sem("cs_mm", 1)
    cs_cp = sem("cs_copied", 1)
    cs_out = sem("cs_stored", 32)
    cs_exp = sem("cs_exp", 1)
    u_w = sem("xw_done", 6)
    st_mm = sem("state_mm", 6)
    st_up = sem("state_done", 6)
    cb_mm = sem("cb_mm", 1)
    cb_ok = sem("cb_masked_done", 1)
    r_land = [sem(f"rows_land{d}", 16 * TC) for d in range(2)]
    d_dif = sem("dif_done", 2 * TC)
    d_ex = sem("decay_exp", 2 * TC)
    m_ok = sem("m_done", 2 * TC)
    skip_x = sem("skip_x_done", TC)
    x_dt = sem("x_dt_done", 2 * TC)
    off_mm = sem("y_off_mm", TC)
    off_rd = sem("y_off_read", TC)
    yd_mm = sem("ydiag_mm", 2 * TC)
    part_rd = sem("ydiag_read", TC)
    y_raw = sem("y_gated", TC)
    y_sq = sem("y_sq", 2 * TC)
    y_ms = sem("y_ms", TC)
    y_rs = sem("y_rs", TC)
    y_nm = sem("y_normed", 2 * TC)
    y_tr = sem("y_transposed", 2 * TC)
    y_f = sem("y_feat_done", 2 * TC)
    y_hi = sem("y_hi_done", 2 * TC)
    y_lo = sem("y_lo_done", 2 * TC)
    l_sq = sem("lora_sq_done", 6)
    l_sum = sem("lora_sum", 2)
    l_ms = sem("lora_ms", 2)
    l_rs = sem("lora_rstd", 2)
    l_row = sem("lora_row", 2)
    l_u = sem("lora_u", 6)
    l_hi = sem("lora_hi", 6)
    l_lo = sem("lora_lo", 6)
    rp_in = sem("rope_in", 5)
    rp_mm = sem("rope_rot", 5)
    rp_out = sem("rope_out", 5)
    rp_hi = sem("rope_hi", 5)
    rp_lo = sem("rope_lo", 5)
    k_hi = sem("k_hi_done", MH)
    k_lo = sem("k_lo_done", MH)
    v_hi = sem("v_hi_done", 2 * TC)
    v_lo = sem("v_lo_done", 2 * TC)
    qn_hi = sem("qn_hi_done", MH)
    qn_lo = sem("qn_lo_done", MH)
    s_mm = sem("scores_mm", MH * TC)
    s_mx = sem("scores_max", MH * TC)
    s_ex = sem("probs_exp", MH * TC)
    s_nm = sem("probs_done", MH * TC)
    p_tr = sem("probs_T", MH * TC)
    p_hi = sem("pT_hi_done", MH * TC)
    p_lo = sem("pT_lo_done", MH * TC)
    o_mm = sem("o_mm", MH)
    o_ev = sem("o_done", MH)
    a_sq = sem("att_sq_done", MH)
    a_add = sem("att_sq_added", MH - 1)
    a_sum = sem("att_sum", 1)
    a_ms = sem("att_ms", 1)
    a_rs = sem("att_rstd", 1)
    a_row = sem("att_row", 1)
    a_u = sem("att_gained", MH - 1)
    a_hi = sem("att_hi", MH)
    a_lo = sem("att_lo", MH)
    f_sum = sem("f_sum")
    f_ms = sem("f_ms")
    f_rs = sem("f_rs")
    f_row = sem("f_row")
    f_out = sem("f_out")
    stored = sem("stored")

    block = ctx.enter_context(nc.Block())

    def rows(ap):
        return ap.rearrange("a p n -> p (a n)")

    def per_head(tile, d, c):
        col = (d * TC + c) * HEADS
        return tile[:, col:col + HEADS].unsqueeze(2).to_broadcast([P, HEADS, HD])

    def heads(t):
        return t.rearrange("p (h n) -> p h n", n=HD)

    @block.sync
    def _(sp):
        sp.dma_start(cin[:, :], cT).then_inc(c_land.sem, 16)
        sp.dma_start(cst[:, :, :], consts).then_inc(pos_land.sem, 16)

        def ada_piece(group, k, m, wait):
            sp.wait_ge(ada_done.sem, wait)
            sp.wait_ge(go.sem, 1)
            src = w_ada[bass.ds(group * ADA_Q + (k * 3 + m), 1), :, :]
            sp.dma_start(ada_in[:, m, :], rows(src)).then_inc(ada_land[m].sem, 16)

        for k in range(KC):
            for m in range(3):
                if k > 1:
                    sp.wait_ge(ada_done.sem, 3 + 3 * (k - 2) + m + 1)
                dst, land = (pro_in, pro_land) if k % 2 else (ada_in, ada_land)
                sp.dma_start(dst[:, m, :], w_ada[k * 3 + m, :, :]).then_inc(land[m].sem, 16)
            if k == 0:
                sp.dma_start(x[:, :, :], xT).then_inc(x_land.sem, 16)
            if k == 1:
                sp.dma_start(posi[:, :], pos.to_broadcast([P, SEQ])).then_inc(pos_land.sem, 16)
                sp.dma_start(invs[:, :], invf).then_inc(pos_land.sem, 16)
                sp.dma_start(fing[:, :], finalg).then_inc(pos_land.sem, 16)

        with sp.Fori(0, DEPTH) as l:
            sp.wait_ge(x_new.sem, x_new.at(l, 0))
            sp.wait_ge(go.sem, 1)
            sp.dma_start(par[:, :], rows(params[bass.ds(l, 1), :, :])).then_inc(par_land.sem, 16)

            def item(n, src):
                sp.wait_ge(w_lo.sem, w_lo.at(l, n - 1))
                sp.wait_ge(go.sem, 1)
                slot = n % 2 if isinstance(n, int) else item.slot
                sp.dma_start(raw[slot][:, :], rows(src)).then_inc(w_land[slot].sem, 16)

            def ffn(j, first):
                up = l * (2 * UP_ITEMS) + j * UP_ITEMS
                dn = l * (2 * DN_ITEMS) + j * DN_ITEMS

                def up_items(i):
                    for q in range(4):
                        item.slot = q % 2
                        item(i * 4 + (first + q), w_up[bass.ds(up + i * 4 + q, 1), :, :])

                group = l * 3 + 1 if j == 0 else l * -3 + 3
                with sp.Fori(0, 8) as i:
                    up_items(i)
                    if j:
                        sp.wait_ge(x_new.sem, x_new.at(l, 3 * KC))
                    for m in range(3):
                        ada_piece(group, i, m, ada_done.at(l, i * 3 + (2 * ADA_Q * j + m - 2)))
                with sp.Fori(8, 11) as i:
                    up_items(i)
                with sp.Fori(0, 4) as i:
                    for q in range(6):
                        item.slot = q % 2
                        item(i * 6 + (first + UP_ITEMS + q), w_dn[bass.ds(dn + i * 6 + q, 1), :, :])
                        if j == 0:
                            k2, m = divmod(q, 3)
                            ada_piece(l * 3 + 2, i * 2 + k2, m,
                                      ada_done.at(l, i * 6 + (ADA_Q + q - 2)))

            ffn(0, 0)
            with sp.Fori(0, MX_ITEMS // 2) as i:
                for q in range(2):
                    item.slot = q
                    item(i * 2 + (FF_ITEMS + q), w_mx[bass.ds(l * MX_ITEMS + i * 2 + q, 1), :, :])
            ffn(1, FF_ITEMS + MX_ITEMS)

        sp.wait_ge(f_out.sem, KC)
        sp.dma_start(out, sq[:, :, :]).then_inc(stored.sem, 16)
        sp.wait_ge(stored.sem, 16)

    @block.gpsimd
    def _(gp):
        gp.sem_inc(go.sem, 1)
        gp.sem_inc(w_lo.sem, 2)
        gp.memset(acc[:, :, :], 0.0).then_inc(acc_zero.sem, 1)
        gp.wait_ge(x_land.sem, 16)
        gp.tensor_tensor(sqs[:, :], x[:, 0, :], x[:, 0, :], ALU.mult).then_inc(sq_add.sem, 2)
        for c in range(1, KC):
            gp.wait_ge(sq_add.sem, c + 1)
            gp.tensor_tensor(tmp_a[:, :], x[:, c, :], x[:, c, :], ALU.mult).then_inc(x_sq.sem, 1)
            gp.wait_ge(x_sq.sem, c)
            gp.tensor_tensor(sqs[:, :], sqs[:, :], tmp_a[:, :], ALU.add).then_inc(sq_add.sem, 1)
        with gp.Fori(0, DEPTH) as l:

            def lo(n, slot):
                gp.wait_ge(w_hi.sem, w_hi.at(l, n + 1))
                gp.tensor_tensor(wL[slot][:, :], raw[slot][:, :], wH[slot][:, :],
                                 ALU.subtract).then_inc(w_lo.sem, 1)

            def zero(n_mod, n_x):
                gp.wait_ge(mod_sum.sem, mod_sum.at(l, n_mod))
                if n_x is not None:
                    gp.wait_ge(x_new.sem, x_new.at(l, n_x))
                gp.sem_inc(passed["gp"].sem, 1)
                gp.memset(acc[:, :, :], 0.0).then_inc(acc_zero.sem, 1)

            def ffn(j, first):
                lo(first, 0)
                lo(first + 1, 1)
                if j == 0:
                    zero(1, None)
                else:
                    zero(3, 3 * KC)
                with gp.Fori(0, UP_ITEMS // 2) as i:
                    for q in range(2):
                        lo(i * 2 + (first + 2 + q), q)
                if j == 0:
                    zero(2, None)
                with gp.Fori(0, DN_ITEMS // 2 - 1) as i:
                    for q in range(2):
                        lo(i * 2 + (first + UP_ITEMS + 2 + q), q)

            ffn(0, 0)
            f = FF_ITEMS
            lo(f, 0)
            lo(f + 1, 1)
            with gp.Fori(1, (I_QA + 5) // 2) as i:
                for q in range(2):
                    lo(i * 2 + (f + q), q)

            def skip(c):
                gain = par[:, P_DS:P_DS + HEADS].unsqueeze(2).to_broadcast([P, HEADS, HD])
                gp.tensor_tensor(heads(xw[:, :]), heads(xtok[:, c, :]), gain,
                                 ALU.mult).then_inc(skip_x.sem, 1)

            def y_lo_part(c):
                for b in range(2):
                    gp.wait_ge(y_hi.sem, y_hi.at(l, 2 * c + b + 1))
                    put = (slice(None), slice(4 * b, 4 * b + 4), slice(c * P, (c + 1) * P))
                    gp.tensor_tensor(hL[put], yt[:, :, :], hH[put],
                                     ALU.subtract).then_inc(y_lo.sem, 1)

            gp.wait_ge(st_mm.sem, st_mm.at(l, 6))
            skip(0)
            lo(f + I_QA + 5, (I_QA + 5) % 2)
            lo(f + I_QA + 6, (I_QA + 6) % 2)
            for c in range(1, TC):
                gp.wait_ge(yd_mm.sem, yd_mm.at(l, 2 * c))
                skip(c)
                for d in range(2):
                    gp.tensor_tensor(heads(xdt[:, d, :]), heads(xtok[:, c, :]),
                                     per_head(dtt, d, c), ALU.mult).then_inc(x_dt.sem, 1)
                if c == 1:
                    lo(f + I_OS, I_OS % 2)
                    lo(f + I_OS + 1, (I_OS + 1) % 2)
                y_lo_part(c - 1)
            gp.sem_inc(passed["gp"].sem, 1)
            with gp.Fori(I_OS // 2 + 1, I_MLA // 2 + 3) as i:
                for q in range(2):
                    lo(i * 2 + (f + q), q)

            def square_heads(hg):
                for h in range(4 * hg, 4 * hg + 4):
                    gp.wait_ge(o_ev.sem, o_ev.at(l, h + 1))
                    first = asum if h == 0 else asq
                    gp.tensor_tensor(first[:, :], ofm[:, h, :], ofm[:, h, :],
                                     ALU.mult).then_inc(a_sq.sem, 1)
                    gp.wait_ge(a_sq.sem, a_sq.at(l, h + 1))
                    if h:
                        gp.tensor_tensor(asum[:, :], asum[:, :], asq[:, :],
                                         ALU.add).then_inc(a_add.sem, 1)
                        gp.wait_ge(a_add.sem, a_add.at(l, h))
                    if h < MH - 1:
                        tile, i = o_place[h]
                        gain = par[:, P_AG + h:P_AG + h + 1].to_broadcast([P, SEQ])
                        gp.tensor_tensor(ofm[:, h, :], ofm[:, h, :], gain,
                                         ALU.mult).then_inc(a_u.sem, 1)
                        gp.wait_ge(a_hi.sem, a_hi.at(l, h + 1))
                        gp.wait_ge(a_u.sem, a_u.at(l, h + 1))
                        gp.tensor_tensor(oL[tile][:, i, :], ofm[:, h, :], oH[tile][:, i, :],
                                         ALU.subtract).then_inc(a_lo.sem, 1)

            lo(f + I_MLA + 6, 0)
            square_heads(0)
            for n in range(I_MLA + 7, I_OA + 2):
                lo(f + n, n % 2)
            square_heads(1)
            gp.sem_inc(passed["gp"].sem, 1)
            with gp.Fori(I_OA // 2 + 1, MX_ITEMS // 2) as i:
                for q in range(2):
                    lo(i * 2 + (f + q), q)
            ffn(1, FF_ITEMS + MX_ITEMS)

    @block.scalar
    def _(act):
        act.sem_inc(sg_done.sem, 2)
        act.wait_ge(c_land.sem, 16)
        act.activation(csil[:, :], cin[:, :], ACT.Silu).then_inc(csil_done.sem, 1)
        act.wait_ge(p_step.sem, PRO_ANGLES)
        act.activation(sinT[:, :], ang[:, :], ACT.Sin).then_inc(trig_done.sem, 1)
        act.activation(cosT[:, :], tmp[:, :], ACT.Sin).then_inc(trig_done.sem, 1)

        with act.Fori(0, DEPTH) as l:

            def hi(n, slot, nth):
                act.wait_ge(w_land[slot].sem, w_land[slot].at(l, nth * 16))
                act.wait_ge(w_used.sem, w_used.at(l, n - 1))
                act.activation(wH[slot][:, :], raw[slot][:, :], ACT.Copy).then_inc(w_hi.sem, 1)

            def root(dst, src, inverse, n, done):
                act.wait_ge(inverse.sem, inverse.at(l, n))
                act.activation(dst, src, ACT.Sqrt).then_inc(done.sem, 1)

            def norm(n):
                root(stat[:, 0, 1, :], stat[:, 0, 0, :], ms_done, n + 1, rstd_done)
                for c in range(KC):
                    act.wait_ge(u_done.sem, u_done.at(l, n * KC + c + 1))
                    act.activation(hH[:, c, :], sq[:, c, :], ACT.Identity,
                                   bias=mod[:, n, 0, c:c + 1]).then_inc(h_hi.sem, 1)

            def ffn(j, first):
                hi(first, 0, first // 2 + 1)
                hi(first + 1, 1, first // 2 + 1)
                norm(2 * j)
                with act.Fori(0, FC // 2) as i:
                    for s in range(2):
                        n, nth = i * 4 + (first + 2 * s + 2), i * 2 + (first // 2 + s + 2)
                        hi(n, 0, nth)
                        act.wait_ge(w_used.sem, w_used.at(l, i * 4 + (first + 2 * s + 1)))
                        act.activation(sg[:, s, :], ps[:, s, :], ACT.Silu).then_inc(sg_done.sem, 1)
                        hi(i * 4 + (first + 2 * s + 3), 1, nth)
                        act.wait_ge(prod_done.sem, prod_done.at(l, i * 2 + (FC * j + s + 1)))
                        act.wait_ge(go.sem, 1)
                        act.activation(ffH[:, bass.ds(i * 2 + s, 1), :].rearrange("p a n -> p (a n)"),
                                       prod[s][:, :], ACT.Copy).then_inc(ff_hi.sem, 1)
                with act.Fori(0, DN_ITEMS // 2 - 1) as i:
                    for q in range(2):
                        hi(i * 2 + (first + UP_ITEMS + 2 + q), q, i + ((first + UP_ITEMS) // 2 + 2))

            ffn(0, 0)

            issued = [0]

            def ahead(n):
                while issued[0] <= n:
                    m = FF_ITEMS + issued[0]
                    hi(m, m % 2, m // 2 + 1)
                    issued[0] += 1

            def used(n):
                ahead(n + 1)
                act.wait_ge(w_used.sem, w_used.at(l, FF_ITEMS + n + 1))

            ahead(1)
            norm(1)
            used(I_DT)
            act.activation(dtf[:, :], ps[0:2 * HEADS, 4, :], ACT.Copy).then_inc(dt_cp.sem, 1)
            for s in range(CCH + 2):
                if s < CCH:
                    used(I_CONV + s)
                    if s >= 2:
                        act.wait_ge(csilu.sem, csilu.at(l, s - 1))
                    act.activation(cbuf[:, s % 2, :], ps[:, s % 2, :], ACT.Identity,
                                   bias=par[:, P_CB + s:P_CB + s + 1],
                                   scale=par[:, P_CW + s * KSZ + 2:P_CW + s * KSZ + 3]
                                   ).then_inc(cen.sem, 1)
                if s == 3:
                    act.wait_ge(d_abs.sem, d_abs.at(l, 1))
                    act.activation(sab, sab, ACT.Exp, scale=-1.0).then_inc(d_exp.sem, 1)
                    act.activation(sea[:, 0:2 * HEADS], par[:, P_AL:P_AL + 2 * HEADS],
                                   ACT.Exp).then_inc(d_exp.sem, 1)
                if 1 <= s <= CCH:
                    c = s - 1
                    act.wait_ge(conv.sem, conv.at(l, c + 1))
                    dst = bfm[:, c, :] if c < 2 else cfm[:, c - 2, :] if c < 4 else xs[:, c % 2, :]
                    act.activation(dst, cbuf[:, c % 2, :], ACT.Silu).then_inc(csilu.sem, 1)
                if s - 2 in TR:
                    c = s - 2
                    act.wait_ge(trx.sem, trx.at(l, TR.index(c) + 1))
                    dst = (btok[:, :, c * P:(c + 1) * P] if c < 2
                           else xtok[:, :, (c - 4) * P:(c - 3) * P])
                    act.activation(dst, ps[:, 2 + c % 2, :].rearrange("p (t n) -> p t n", t=TC),
                                   ACT.Copy).then_inc(tev.sem, 1)
            ahead(I_Z + 1)
            act.wait_ge(cs_cp.sem, cs_cp.at(l, 1))
            for d in range(2):
                act.dma_start(cs_dram[d, :, :], csT[:, d, :]).then_inc(cs_out.sem, 16)
            act.activation(cs3[:, :, :], cs3[:, :, :], ACT.Exp).then_inc(cs_exp.sem, 1)
            act.wait_ge(cs_out.sem, cs_out.at(l, 32))

            def load_rows(c, d):
                if c:
                    act.wait_ge(yd_mm.sem, yd_mm.at(l, 2 * c - 1 + d))
                src = cs_dram[d:d + 1, :, c * P:(c + 1) * P].to_broadcast([P, HEADS, P])
                act.dma_start(dec[:, d, :, :], src).then_inc(r_land[d].sem, 16)

            def decay_exp(c, d):
                act.wait_ge(d_dif.sem, d_dif.at(l, 2 * c + d + 1))
                act.activation(dec[:, d, :, :], dec[:, d, :, :], ACT.Exp).then_inc(d_ex.sem, 1)

            for d in range(2):
                load_rows(0, d)
            for z in range(2):
                used(I_Z + 4 * z + 1)
                used(I_Z + 4 * z + 3)
                for t in range(TC):
                    act.activation(zs[:, t, z * SEQ:(z + 1) * SEQ], ps[:, 4 + t, :],
                                   ACT.Silu).then_inc(z_ev.sem, 1)
            for d in range(2):
                decay_exp(0, d)
            for q in range(7):
                if q == 5:
                    ahead(I_QA + q + 1)
                    load_rows(1, 0)
                used(I_QA + q)
                act.activation(rawq[:, q, :], ps[:, 2 + q % 2, :], ACT.Copy).then_inc(q_ev.sem, 1)
            ahead(I_OS + 1)
            for c in range(TC):
                if c + 1 < TC:
                    decay_exp(c + 1, 0)
                    load_rows(c + 1, 1)
                act.wait_ge(y_raw.sem, y_raw.at(l, c + 1))
                for g in range(GRP):
                    act.activation(yt2[:, g * SEQ:(g + 1) * SEQ], yb[:, g * SEQ:(g + 1) * SEQ],
                                   ACT.Square, accum_out=ssq[:, g:g + 1]).then_inc(y_sq.sem, 1)
                root(ssq[:, 4:6], ssq[:, 2:4], y_ms, c + 1, y_rs)
                act.wait_ge(y_rs.sem, y_rs.at(l, c + 1))
                for g in range(GRP):
                    half = yb[:, g * SEQ:(g + 1) * SEQ]
                    act.activation(half, half, ACT.Copy,
                                   scale=ssq[:, 4 + g:5 + g]).then_inc(y_nm.sem, 1)
                if c + 1 < TC:
                    decay_exp(c + 1, 1)
                if c == TC - 2:
                    for q in range(6):
                        act.activation(lsq[:, q, :], rawq[:, q, :], ACT.Square
                                       ).then_inc(l_sq.sem, 1)
                if c + 2 < TC:
                    load_rows(c + 2, 0)
                for b in range(2):
                    act.wait_ge(y_f.sem, y_f.at(l, 2 * c + b + 1))
                    src = ytl if c == TC - 1 and b else yt
                    act.activation(hH[:, 4 * b:4 * b + 4, c * P:(c + 1) * P], src[:, :, :],
                                   ACT.Copy).then_inc(y_hi.sem, 1)
            def rope_in(r, src):
                if r:
                    act.wait_ge(rp_lo.sem, rp_lo.at(l, r))
                act.activation(rt[0][:, :], src, ACT.Copy).then_inc(rp_in.sem, 1)

            def rope_hi(r, dst):
                act.wait_ge(rp_out.sem, rp_out.at(l, r + 1))
                act.activation(dst, rt[0][:, :], ACT.Copy).then_inc(rp_hi.sem, 1)

            def rope(r, src, dst, item):
                rope_in(r, src)
                ahead(item)
                rope_hi(r, dst)

            for q in range(2):
                root(stat[:, 1 - q, 1, :], stat[:, 1 - q, 0, :], l_ms, q + 1, l_rs)
            for c in range(6):
                if c % 2 == 0:
                    ahead(I_OS + 3 + c // 2)
                act.wait_ge(l_u.sem, l_u.at(l, c + 1))
                dst = qaH[:, c, :] if c < QC else ckH[:, c - QC, :]
                act.activation(dst, rawq[:, c, :], ACT.Copy).then_inc(l_hi.sem, 1)
            ahead(I_OS + 6)
            act.wait_ge(l_lo.sem, l_lo.at(l, 6))
            rope(0, rawq[:, 6, :], krH[:, :], I_OS + 7)
            for hg in range(2):
                i0 = I_MLA + 5 * hg
                used(i0)
                for h in range(4):
                    act.activation(kH[:, h, :], ps[:, h, :], ACT.Copy).then_inc(k_hi.sem, 1)
                used(i0 + 1)
                for t in range(TC):
                    act.activation(vH[:, t, :], ps[:, 4 + t, :], ACT.Copy).then_inc(v_hi.sem, 1)
                used(i0 + 2)
                rope(1 + 2 * hg, ps[:, 0, :], qrH[:, 0, :], i0 + 4)
                used(i0 + 3)
                for h in range(2):
                    act.activation(qnH[:, h, :], ps[:, 3 + h, :], ACT.Copy).then_inc(qn_hi.sem, 1)
                rope_in(2 + 2 * hg, ps[:, 1, :])
                used(i0 + 4)
                for h in range(2, 4):
                    act.activation(qnH[:, h, :], ps[:, 3 + h, :], ACT.Copy).then_inc(qn_hi.sem, 1)
                rope_hi(2 + 2 * hg, qrH[:, 1, :])
                ahead(i0 + 6)
                for s in range(SOFT + 4):
                    n = SOFT * hg + s
                    if s > 3 and (s - 3) % TC == 0:
                        h = (n - 3) // TC - 1
                        act.wait_ge(o_mm.sem, o_mm.at(l, h + 1))
                        act.activation(ofm[:, h, :], ps[:, 2, :], ACT.Copy).then_inc(o_ev.sem, 1)
                        tile, i = o_place[h]
                        act.activation(oH[tile][:, i, :], ps[:, 2, :], ACT.Identity,
                                       scale=par[:, P_AG + h:P_AG + h + 1]).then_inc(a_hi.sem, 1)
                    if 3 <= s < SOFT + 3:
                        m = n - 3
                        t = m % TC
                        act.wait_ge(p_tr.sem, p_tr.at(l, m + 1))
                        act.activation(ptH[:, :, t * P:(t + 1) * P],
                                       ps[:, 6 + m % 2, :].rearrange("p (k n) -> p k n", k=TC),
                                       ACT.Copy).then_inc(p_hi.sem, 1)
                    if s < SOFT:
                        act.wait_ge(s_mx.sem, s_mx.at(l, n + 1))
                        if n >= 4:
                            act.wait_ge(p_tr.sem, p_tr.at(l, n - 3))
                        act.activation(pr[:, n % 4, :], ps[:, 3 + n % 3, :], ACT.Exp,
                                       bias=sm[:, n % 4, 1:2], scale=ATT_SCALE,
                                       accum_out=sm[:, n % 4, 2:3]).then_inc(s_ex.sem, 1)
            ahead(I_OA + 2)
            root(stat[:, 0, 1, :], stat[:, 0, 0, :], a_ms, 1, a_rs)
            ahead(MX_ITEMS - 1)
            ffn(1, FF_ITEMS + MX_ITEMS)

        act.wait_ge(f_ms.sem, 1)
        act.activation(stat[:, 0, 1, :], stat[:, 0, 0, :], ACT.Sqrt).then_inc(f_rs.sem, 1)

    @block.vector
    def _(dve):
        dve.sem_inc(prod_done.sem, 2)
        dve.sem_inc(ff_lo.sem, 2)
        dve.sem_inc(ada_done.sem, 3)
        steps = [0]

        def pro(ins):
            ins.then_inc(p_step.sem, 1)
            steps[0] += 1
            dve.wait_ge(p_step.sem, steps[0])

        dve.wait_ge(csil_done.sem, 1)
        dve.wait_ge(acc_zero.sem, 1)

        def ada_piece(m, scalar, landed, own, piece=ada_in):
            for sig, n in (landed, own):
                dve.wait_ge(sig.sem, n)
            dve.scalar_tensor_tensor(acc[:, m, :], piece[:, m, :], scalar, acc[:, m, :],
                                     ALU.mult, ALU.add).then_inc(ada_done.sem, 1)

        for k in range(KC):
            for m in range(3):
                ada_piece(m, csil[:, k:k + 1],
                          ((pro_land if k % 2 else ada_land)[m], 16 * (k // 2 + 1)),
                          (ada_done, 3 * k + m + 1), pro_in if k % 2 else ada_in)
            if k == 1:
                dve.wait_ge(pos_land.sem, 64)
                pro(dve.tensor_copy(kk[:, :], posi[:, :]))
                pro(dve.tensor_scalar(ang[:, :], kk[:, :], invs[:, 0:1], None, ALU.mult))
                pro(dve.tensor_scalar(kk[:, :], ang[:, :], 1.0 / TWO_PI, ROUND, ALU.mult, ALU.add))
                pro(dve.tensor_scalar(kk[:, :], kk[:, :], -ROUND, None, ALU.add))
                for part in (C1, C2, C3):
                    pro(dve.scalar_tensor_tensor(ang[:, :], kk[:, :], -part, ang[:, :],
                                                 ALU.mult, ALU.add))
                pro(dve.tensor_scalar(tmp[:, :], ang[:, :], np.pi / 2, None, ALU.add))
                pro(dve.tensor_scalar(kk[:, :], tmp[:, :], np.pi, -TWO_PI, ALU.is_gt, ALU.mult))
                pro(dve.tensor_tensor(tmp[:, :], tmp[:, :], kk[:, :], ALU.add))
                pro(dve.tensor_scalar(tmp[:, :], tmp[:, :], PI_IN, -PI_IN, ALU.min, ALU.max))
                pro(dve.tensor_scalar(ang[:, :], ang[:, :], PI_IN, -PI_IN, ALU.min, ALU.max))
                assert steps[0] == PRO_ANGLES, steps[0]
        dve.wait_ge(trig_done.sem, 2)
        dve.sem_inc(x_new.sem, 2)

        with dve.Fori(0, DEPTH) as l:
            do = Chain(dve, v_step, l)

            def modulation(g):
                dve.wait_ge(mod_sum.sem, mod_sum.at(l, g + 1))
                flat = mod[:, g, :, :].rearrange("p a c -> p (a c)")
                do(dve.tensor_tensor(flat, ps[:, 7, 0:ADA_Q],
                                     par[:, P_AB + g * ADA_Q:P_AB + (g + 1) * ADA_Q], ALU.add))
                do(dve.scalar_tensor_tensor(mod[:, g, 1, :], mod[:, g, 1, :], 1.0,
                                            par[:, P_NG + g * KC:P_NG + (g + 1) * KC],
                                            ALU.add, ALU.mult))
                if g != 1:
                    do(dve.tensor_scalar(mod[:, g, 2, :], mod[:, g, 2, :], 0.5, None, ALU.mult))

            def mean(which, bank, n, done):
                dst = stat[:, which, 0, :]
                do(dve.tensor_scalar(dst, ps[:, bank, 0:TC], 1.0 / n, EPS, ALU.mult, ALU.add))
                dve.reciprocal(dst, dst).then_inc(done.sem, 1)

            def norm(n):
                dve.wait_ge(n_sum.sem, n_sum.at(l, n + 1))
                mean(0, 6, DM, ms_done)
                dve.wait_ge(n_row.sem, n_row.at(l, n + 1))

                def lo(c):
                    dve.wait_ge(h_hi.sem, h_hi.at(l, n * KC + c + 1))
                    dve.scalar_tensor_tensor(hL[:, c, :], sq[:, c, :], mod[:, n, 0, c:c + 1],
                                             hH[:, c, :], ALU.add, ALU.subtract
                                             ).then_inc(h_lo.sem, 1)

                for c in range(KC):
                    dve.scalar_tensor_tensor(sq[:, c, :], x[:, c, :], mod[:, n, 1, c:c + 1],
                                             ps[:, 6, :], ALU.mult, ALU.mult).then_inc(u_done.sem, 1)
                    if c:
                        lo(c - 1)
                lo(KC - 1)

            def residual(d, gate, bank):
                dst = x[:, bass.ds(d, 1), :].rearrange("p a n -> p (a n)")
                dve.scalar_tensor_tensor(dst, ps[:, bank, :], gate, dst,
                                         ALU.mult, ALU.add).then_inc(x_new.sem, 1)

            def square(d, n, new):
                src = x[:, bass.ds(d, 1), :].rearrange("p a n -> p (a n)")
                dve.wait_ge(x_new.sem, x_new.at(l, new))
                dve.wait_ge(sq_add.sem, sq_add.at(l, d + n * KC))
                dve.tensor_tensor(tmp_a[:, :], src, src, ALU.mult).then_inc(sq_mul.sem, 1)
                dve.wait_ge(sq_mul.sem, sq_mul.at(l, d + (n * KC + 1)))
                dve.tensor_tensor(sqs[:, :], sqs[:, :], tmp_a[:, :], ALU.add).then_inc(sq_add.sem, 1)

            def up_chunks(i, j, first):
                for s in range(2):
                    dve.wait_ge(sg_done.sem, sg_done.at(l, i * 2 + (FC * j + s + 1)))
                    dve.wait_ge(w_used.sem, w_used.at(l, i * 4 + (first + 2 * s + 2)))
                    dve.wait_ge(ff_lo.sem, ff_lo.at(l, i * 2 + (FC * j + s - 1)))
                    dve.tensor_tensor(prod[s][:, :], sg[:, s, :], ps[:, 2 + s, :],
                                      ALU.mult).then_inc(prod_done.sem, 1)
                for s in range(2):
                    dve.wait_ge(ff_hi.sem, ff_hi.at(l, i * 2 + (FC * j + s + 1)))
                    ff = bass.ds(i * 2 + s, 1)
                    dve.tensor_tensor(ffL[:, ff, :].rearrange("p a n -> p (a n)"), prod[s][:, :],
                                      ffH[:, ff, :].rearrange("p a n -> p (a n)"),
                                      ALU.subtract).then_inc(ff_lo.sem, 1)

            def ffn(j, first):
                n = 2 * j
                if j == 0:
                    dve.wait_ge(par_land.sem, par_land.at(l, 16))
                    modulation(0)
                norm(n)
                dve.wait_ge(acc_zero.sem, acc_zero.at(l, [1, 3][j]))
                dve.sem_inc(passed["dve"].sem, 1)
                off = 2 * ADA_Q * j
                with dve.Fori(0, 8) as i:
                    for m in range(3):
                        ada_piece(m, csil[:, bass.ds(i, 1)],
                                  (ada_land[m], ada_land[m].at(l, i * 16 + 16 * (16 * j + 1))),
                                  (ada_done, ada_done.at(l, i * 3 + (off + m - 2))))
                    up_chunks(i, j, first)
                with dve.Fori(8, 11) as i:
                    up_chunks(i, j, first)
                if j == 0:
                    modulation(1)
                    dve.wait_ge(acc_zero.sem, acc_zero.at(l, 2))
                    dve.sem_inc(passed["dve"].sem, 1)
                gate = mod[:, n, 2, :]
                do(dve.memset(sqs[:, :], 0.0))
                dve.sem_inc(passed["dve"].sem, 1)
                with dve.Fori(0, KC // 2) as i:
                    for q in range(6):
                        if j == 0:
                            k2, m = divmod(q, 3)
                            ada_piece(m, csil[:, bass.ds(i * 2 + k2, 1)],
                                      (ada_land[m], ada_land[m].at(l, i * 32 + 16 * (8 + k2 + 1))),
                                      (ada_done, ada_done.at(l, i * 6 + (ADA_Q + q - 2))))
                        if q % 3 == 2:
                            d = i * 2 + q // 3
                            dve.wait_ge(w_used.sem,
                                        w_used.at(l, i * 6 + (first + UP_ITEMS + q + 1)))
                            residual(d, gate[:, bass.ds(d, 1)], 4 + q // 3)
                            square(d, n, d + (3 * KC * j + 1))

            ffn(0, 0)
            f = FF_ITEMS
            modulation(2)
            norm(1)

            def halves(t):
                return t.rearrange("p (d t h) -> p d t h", d=2, t=TC)

            dtv, adv, xrv = halves(dtt), halves(adt), halves(sxr)

            def softplus_start():
                dve.wait_ge(dt_tr.sem, dt_tr.at(l, 1))
                for d in range(2):
                    src = ps[:, 5, 0:P].rearrange("p (t d h) -> p d t h", d=2, t=TC)[:, d, :, :]
                    bias = par[:, P_DB + d * HEADS:P_DB + (d + 1) * HEADS]
                    do(dve.tensor_tensor(xrv[:, d, :, :], src,
                                         bias.unsqueeze(1).to_broadcast([P, TC, HEADS]), ALU.add))
                dve.scalar_tensor_tensor(sab, sxr, -1.0, sxr, ALU.mult, ALU.max).then_inc(d_abs.sem, 1)

            def softplus_end():
                dve.wait_ge(d_exp.sem, d_exp.at(l, 2))
                do(dve.tensor_scalar(sp1, sab, 2.0, None, ALU.add))
                do(dve.reciprocal(sp1, sp1))
                do(dve.tensor_tensor(sp1, sp1, sab, ALU.mult))
                do(dve.tensor_tensor(sp2, sp1, sp1, ALU.mult))
                do(dve.tensor_scalar(dtt, sp2, 1.0 / 15, None, ALU.mult))
                for odd in (13, 11, 9, 7, 5, 3):
                    do(dve.scalar_tensor_tensor(dtt, dtt, 1.0 / odd, sp2, ALU.add, ALU.mult))
                do(dve.scalar_tensor_tensor(dtt, dtt, 1.0, sp1, ALU.add, ALU.mult))
                do(dve.tensor_scalar(sxr, sxr, 0.0, None, ALU.max))
                do(dve.scalar_tensor_tensor(dtt, dtt, 2.0, sxr, ALU.mult, ALU.add))
                for d in range(2):
                    ea = sea[:, d * HEADS:(d + 1) * HEADS].unsqueeze(1).to_broadcast([P, TC, HEADS])
                    last = dve.scalar_tensor_tensor(adv[:, d, :, :], dtv[:, d, :, :], -1.0, ea,
                                                    ALU.mult, ALU.mult)
                    if d == 0:
                        do(last)
                last.then_inc(a_dt.sem, 1)

            for s in range(CCH):
                dve.wait_ge(cen.sem, cen.at(l, s + 1))
                for k in (0, 1, 3, 4):
                    sh = k - KSZ // 2
                    a, b = max(0, -sh), min(SEQ, SEQ - sh)
                    ins = dve.scalar_tensor_tensor(
                        cbuf[:, s % 2, a:b], ps[:, s % 2, a + sh:b + sh],
                        par[:, P_CW + s * KSZ + k:P_CW + s * KSZ + k + 1],
                        cbuf[:, s % 2, a:b], ALU.mult, ALU.add)
                    if k < 4:
                        do(ins)
                ins.then_inc(conv.sem, 1)
                if s == 2:
                    softplus_start()
                if s == 4:
                    softplus_end()
                if s == 8:
                    dve.wait_ge(cs_mm.sem, cs_mm.at(l, 1))
                    do(dve.tensor_copy(cs3[:, 1:3, :], ps[:, 5, 0:2 * P].rearrange("p (a n) -> p a n", a=2)))
                    do(dve.tensor_copy(sxr, cs3[:, 1, :]))
                    do(dve.tensor_tensor(cs3[:, 0, :], cs3[:, 2, :], cs3[:, 1, :], ALU.subtract))
                    dve.tensor_copy(csT[:, :, :], ps[0:HEADS, 6:8, :]).then_inc(cs_cp.sem, 1)

            dve.wait_ge(cb_mm.sem, cb_mm.at(l, 1))
            for d in range(2):
                for g in range(GRP):
                    tri = (triL if d else triU).unsqueeze(1).to_broadcast([P, TC, P])
                    ins = dve.tensor_tensor(cbm[:, d, :, g, :],
                                            ps[:, 2 + g, :].rearrange("p (t n) -> p t n", t=TC),
                                            tri, ALU.mult)
                    if d + g < 2:
                        do(ins)
            ins.then_inc(cb_ok.sem, 1)
            dve.wait_ge(cs_exp.sem, cs_exp.at(l, 1))
            to_end, vdec, cdec = (cs3[:, i, :] for i in range(3))
            do(dve.tensor_tensor(uu, dtt, to_end, ALU.mult))

            def weighted(d, c, n):
                if n:
                    dve.wait_ge(st_mm.sem, st_mm.at(l, n))
                dve.tensor_tensor(heads(xw[:, :]), heads(xtok[:, c, :]), per_head(uu, d, c),
                                  ALU.mult).then_inc(u_w.sem, 1)

            def bank2(b):
                return ps[:, b:b + 2, :].rearrange("p b n -> p (b n)")

            def add_state(dst, src, d, c, n):
                dve.wait_ge(st_mm.sem, st_mm.at(l, n + 1))
                if src is None:
                    dve.tensor_copy(dst, bank2(0)).then_inc(st_up.sem, 1)
                    return
                do(dve.tensor_tensor(heads(dst), heads(src), per_head(cdec, d, c), ALU.mult))
                dve.tensor_tensor(dst, dst, bank2(0), ALU.add).then_inc(st_up.sem, 1)

            for n, c in enumerate((3, 2, 1)):
                weighted(1, c, n)
                add_state(sbk[:, c - 1, :], sbk[:, c, :] if n else None, 1, c, n)

            def differences(c, d):
                dve.wait_ge(r_land[d].sem, r_land[d].at(l, 16 * (c + 1)))
                col = (d * TC + c) * HEADS
                at_s = sxr[:, col:col + HEADS].unsqueeze(2).to_broadcast([P, HEADS, P])
                do(dve.tensor_tensor(dec[:, d, :, :], dec[:, d, :, :], at_s, ALU.subtract))
                dve.tensor_scalar(dec[:, d, :, :], dec[:, d, :, :], 0.0, None,
                                  ALU.min).then_inc(d_dif.sem, 1)

            def masked(c, d):
                dve.wait_ge(d_ex.sem, d_ex.at(l, 2 * c + d + 1))
                view = dec[:, d, :, :].rearrange("p (g h) n -> p g h n", g=GRP)
                cb = cbm[:, d, c, :, :].unsqueeze(2).to_broadcast([P, GRP, HEADS // GRP, P])
                dve.tensor_tensor(view, view, cb, ALU.mult).then_inc(m_ok.sem, 1)

            for d in range(2):
                differences(0, d)
            for d in range(2):
                dve.tensor_tensor(heads(xdt[:, d, :]), heads(xtok[:, 0, :]), per_head(dtt, d, 0),
                                  ALU.mult).then_inc(x_dt.sem, 1)
            weighted(0, 0, 3)
            for d in range(2):
                masked(0, d)
            for c in range(TC - 1):
                if c:
                    weighted(0, c, 3 + c)
                add_state(sf[c][:, :], sf[c - 1][:, :] if c else None, 0, c, 3 + c)
            def off_parts(c):
                dve.wait_ge(off_mm.sem, off_mm.at(l, c + 1))
                if c:
                    dve.wait_ge(y_tr.sem, y_tr.at(l, 2 * c))
                dirs = [d for d in range(2) if c != (TC - 1 if d else 0)]
                for d, dst in zip(dirs, (yt2, yb)):
                    ins = dve.tensor_tensor(heads(dst[:, :]), heads(bank2(2 + 2 * d)),
                                            per_head(vdec, d, c), ALU.mult)
                    if len(dirs) == 2:
                        do(ins)
                if len(dirs) == 2:
                    ins = dve.tensor_tensor(yt2[:, :], yt2[:, :], yb[:, :], ALU.add)
                ins.then_inc(off_rd.sem, 1)
                dve.wait_ge(off_rd.sem, off_rd.at(l, c + 1))

            def y_features(c, b):
                dve.wait_ge(y_tr.sem, y_tr.at(l, 2 * c + b + 1))
                last = c == TC - 1 and b
                if 2 * c + b and not last:
                    dve.wait_ge(y_lo.sem, y_lo.at(l, 2 * c + b))
                gain = par[:, P_SG + 4 * b:P_SG + 4 * b + 4].unsqueeze(2).to_broadcast([P, 4, P])
                dst = ytl if last else yt
                dve.tensor_tensor(dst[:, :, :], ps[:, 6 + b, :].rearrange("p (k n) -> p k n", k=4),
                                  gain, ALU.mult).then_inc(y_f.sem, 1)

            off_parts(0)
            differences(1, 0)
            for c in range(TC):
                dve.wait_ge(yd_mm.sem, yd_mm.at(l, 2 * c + 2))
                dve.tensor_tensor(yb[:, :], bank2(0), yt2[:, :], ALU.add).then_inc(part_rd.sem, 1)
                dve.wait_ge(part_rd.sem, part_rd.at(l, c + 1))
                dve.tensor_tensor(yb[:, :], yb[:, :], zs[:, c, :], ALU.mult).then_inc(y_raw.sem, 1)
                if c + 1 < TC:
                    masked(c + 1, 0)
                dve.wait_ge(y_sq.sem, y_sq.at(l, 2 * c + 2))
                do(dve.tensor_scalar(ssq[:, 2:4], ssq[:, 0:2], 1.0 / SEQ, EPS, ALU.mult, ALU.add))
                dve.reciprocal(ssq[:, 2:4], ssq[:, 2:4]).then_inc(y_ms.sem, 1)
                if c + 1 < TC:
                    differences(c + 1, 1)
                if c + 1 < TC:
                    masked(c + 1, 1)
                y_features(c, 0)
                if c + 1 < TC:
                    off_parts(c + 1)
                y_features(c, 1)
                if c + 2 < TC:
                    differences(c + 2, 0)

            for b, src in ((0, yt), (1, ytl)):
                dve.wait_ge(y_hi.sem, y_hi.at(l, 2 * TC - 1 + b))
                put = (slice(None), slice(4 * b, 4 * b + 4), slice(SEQ - P, SEQ))
                dve.tensor_tensor(hL[put], src[:, :, :], hH[put], ALU.subtract).then_inc(y_lo.sem, 1)
            dve.wait_ge(l_sum.sem, l_sum.at(l, 1))
            mean(1, 5, KVL, l_ms)
            dve.wait_ge(l_sum.sem, l_sum.at(l, 2))
            mean(0, 4, QL, l_ms)

            def mix_residual(first, d, bank):
                dve.wait_ge(w_used.sem, w_used.at(l, f + first + d + 1))
                dve.scalar_tensor_tensor(x[:, d, :], ps[:, bank + d % 2, :], mod[:, 1, 2, d:d + 1],
                                         x[:, d, :], ALU.mult, ALU.add).then_inc(x_new.sem, 1)

            def scaled(src, gain, row, n, sig_u, sig_hi, sig_lo, dsts, count):
                def lo(c):
                    dve.wait_ge(sig_hi.sem, sig_hi.at(l, c + 1))
                    h, lo_ = dsts(c)
                    dve.tensor_tensor(lo_, src[:, c, :], h, ALU.subtract).then_inc(sig_lo.sem, 1)

                for c in range(n, n + count):
                    dve.scalar_tensor_tensor(src[:, c, :], src[:, c, :], gain(c), row,
                                             ALU.mult, ALU.mult).then_inc(sig_u.sem, 1)
                    if c > n:
                        lo(c - 1)
                lo(n + count - 1)

            def rope(r, dstH, dstL):
                dve.wait_ge(rp_mm.sem, rp_mm.at(l, r + 1))
                if r:
                    dve.wait_ge(rp_lo.sem, rp_lo.at(l, r))
                do(dve.tensor_tensor(rt[1][:, :], ps[:, 2, :], sinT[:, :], ALU.mult))
                do(dve.tensor_tensor(rt[0][:, :], rt[0][:, :], cosT[:, :], ALU.mult))
                dve.tensor_tensor(rt[0][:, :], rt[0][:, :], rt[1][:, :],
                                  ALU.add).then_inc(rp_out.sem, 1)
                dve.wait_ge(rp_hi.sem, rp_hi.at(l, r + 1))
                dve.tensor_tensor(dstL, rt[0][:, :], dstH, ALU.subtract).then_inc(rp_lo.sem, 1)

            for d in range(KC):
                mix_residual(I_OS, d, 6)
                if d in (1, 2):
                    dve.wait_ge(l_row.sem, l_row.at(l, 2))
                    scaled(rawq, lambda c: par[:, P_QG + c:P_QG + c + 1], ps[:, 4, :], 2 * d - 2,
                           l_u, l_hi, l_lo, lambda c: (qaH[:, c, :], qaL[:, c, :]), 2)
                if d == 3:
                    dve.wait_ge(l_row.sem, l_row.at(l, 2))
                    scaled(rawq, lambda c: par[:, P_KG + c - QC:P_KG + c - QC + 1], ps[:, 5, :], QC,
                           l_u, l_hi, l_lo, lambda c: (ckH[:, c - QC, :], ckL[:, c - QC, :]), KVC)
                if d == 5:
                    rope(0, krH[:, :], krL[:, :])
            for hg in range(2):
                for h in range(4):
                    dve.wait_ge(k_hi.sem, k_hi.at(l, 4 * hg + h + 1))
                    dve.tensor_tensor(kL[:, h, :], ps[:, h, :], kH[:, h, :],
                                      ALU.subtract).then_inc(k_lo.sem, 1)
                for t in range(TC):
                    dve.wait_ge(v_hi.sem, v_hi.at(l, 4 * hg + t + 1))
                    dve.tensor_tensor(vL[:, t, :], ps[:, 4 + t, :], vH[:, t, :],
                                      ALU.subtract).then_inc(v_lo.sem, 1)
                rope(1 + 2 * hg, qrH[:, 0, :], qrL[:, 0, :])
                for h in range(4):
                    dve.wait_ge(qn_hi.sem, qn_hi.at(l, 4 * hg + h + 1))
                    dve.tensor_tensor(qnL[:, h, :], ps[:, 3 + h, :], qnH[:, h, :],
                                      ALU.subtract).then_inc(qn_lo.sem, 1)
                rope(2 + 2 * hg, qrH[:, 1, :], qrL[:, 1, :])
                for s in range(SOFT + 4):
                    n = SOFT * hg + s
                    if s < SOFT:
                        st = sm[:, n % 4, :]
                        dve.wait_ge(s_mm.sem, s_mm.at(l, n + 1))
                        if n >= 4:
                            dve.wait_ge(s_nm.sem, s_nm.at(l, n - 3))
                        do(dve.reduce_max(st[:, 0:1], ps[:, 3 + n % 3, :], AXX))
                        dve.tensor_scalar(st[:, 1:2], st[:, 0:1], -ATT_SCALE, None,
                                          ALU.mult).then_inc(s_mx.sem, 1)
                    if n == 2 * SOFT + 3:
                        h = MH - 1
                        tile, i = o_place[h]
                        dve.wait_ge(a_hi.sem, a_hi.at(l, h + 1))
                        dve.scalar_tensor_tensor(oL[tile][:, i, :], ofm[:, h, :],
                                                 par[:, P_AG + h:P_AG + h + 1], oH[tile][:, i, :],
                                                 ALU.mult, ALU.subtract).then_inc(a_lo.sem, 1)
                    if 1 <= s < SOFT + 1:
                        m = n - 1
                        st = sm[:, m % 4, :]
                        dve.wait_ge(s_ex.sem, s_ex.at(l, m + 1))
                        do(dve.reciprocal(st[:, 3:4], st[:, 2:3]))
                        dve.tensor_scalar(pr[:, m % 4, :], pr[:, m % 4, :], st[:, 3:4], None,
                                          ALU.mult).then_inc(s_nm.sem, 1)
                    if 3 <= s < SOFT + 3:
                        m = n - 3
                        t = m % TC
                        put = (slice(None), slice(None), slice(t * P, (t + 1) * P))
                        dve.wait_ge(p_hi.sem, p_hi.at(l, m + 1))
                        dve.tensor_tensor(ptL[put],
                                          ps[:, 6 + m % 2, :].rearrange("p (k n) -> p k n", k=TC),
                                          ptH[put], ALU.subtract).then_inc(p_lo.sem, 1)
            dve.wait_ge(a_sum.sem, a_sum.at(l, 1))
            mean(0, 6, DM, a_ms)
            dve.wait_ge(a_row.sem, a_row.at(l, 1))
            do(dve.tensor_copy(pr[:, 2, :], ps[:, 6, :]))
            do(dve.memset(sqs[:, :], 0.0))
            for d in range(KC):
                dve.wait_ge(w_used.sem, w_used.at(l, f + I_OA + d + 1))
                do(dve.tensor_tensor(pr[:, d % 2, :], ps[:, 3 + d % 3, :], pr[:, 2, :], ALU.mult))
                dve.scalar_tensor_tensor(x[:, d, :], pr[:, d % 2, :], mod[:, 1, 2, d:d + 1], x[:, d, :],
                                         ALU.mult, ALU.add).then_inc(x_new.sem, 1)
                square(d, 1, 2 * KC + d + 1)
            ffn(1, FF_ITEMS + MX_ITEMS)
            assert do.n == DVE_STEPS, do.n

        dve.wait_ge(f_sum.sem, 1)
        dve.tensor_scalar(stat[:, 0, 0, :], ps[:, 6, 0:TC], 1.0 / DM, EPS,
                          ALU.mult, ALU.add).then_inc(p_step.sem, 1)
        dve.wait_ge(p_step.sem, PRO_ANGLES + 1)
        dve.reciprocal(stat[:, 0, 0, :], stat[:, 0, 0, :]).then_inc(f_ms.sem, 1)
        dve.wait_ge(f_row.sem, 1)
        for c in range(KC):
            dve.scalar_tensor_tensor(sq[:, c, :], x[:, c, :], fing[:, c:c + 1], ps[:, 6, :],
                                     ALU.mult, ALU.mult).then_inc(f_out.sem, 1)

    @block.tensor
    def _(pe):
        pe.sem_inc(w_used.sem, 2)
        pe.wait_ge(pos_land.sem, 64)

        def three(dst, aH, aL, bH, bL, first, last):
            pe.matmul(dst, aH, bH, start=first, stop=False)
            pe.matmul(dst, aH, bL, start=False, stop=False)
            return pe.matmul(dst, aL, bH, start=False, stop=last)

        def token_sums(bank, srcs):
            for t in range(TC):
                for k, src in enumerate(srcs):
                    last = pe.matmul(ps[:, bank, t:t + 1], src[:, t * P:(t + 1) * P], ones[:, 0:1],
                                     start=(k == 0), stop=(k == len(srcs) - 1))
            return last

        def token_row(bank, which):
            for t in range(TC):
                last = pe.matmul(ps[:, bank, t * P:(t + 1) * P],
                                 stat[:, which, 1, t:t + 1].to_broadcast([P, P]), ident,
                                 start=True, stop=True)
            return last

        with pe.Fori(0, DEPTH) as l:

            def mod_vectors(g):
                pe.wait_ge(ada_done.sem, ada_done.at(l, ADA_Q * g))
                for q in range(3 * KC):
                    m, c = divmod(q, KC)
                    last = pe.matmul(ps[:, 7, q:q + 1], acc[:, m, c * P:(c + 1) * P],
                                     ones[:, 0:1], start=True, stop=True)
                last.then_inc(mod_sum.sem, 1)

            def sum_squares(n):
                pe.wait_ge(sq_add.sem, sq_add.at(l, n * KC))
                token_sums(6, [sqs[:, :]]).then_inc(n_sum.sem, 1)
                pe.wait_ge(rstd_done.sem, rstd_done.at(l, n + 1))
                token_row(6, 0).then_inc(n_row.sem, 1)

            def blocks(dst, slot, n, rhsH, rhsL, k0=0, last=KC, width=P, off=0,
                       arrive=None):
                for b in range(n):
                    if arrive is not None:
                        pe.wait_ge(h_lo.sem, h_lo.at(l, arrive + b + 1))
                    w = slice(b * width + off, b * width + off + P)
                    k = k0 + b
                    end = three(dst, wH[slot][:, w], wL[slot][:, w], rhsH[:, k, :], rhsL[:, k, :],
                                k == 0, k == last - 1)
                return end

            def ffn(j, first):
                if j == 0:
                    mod_vectors(0)
                sum_squares(2 * j)
                pe.sem_inc(passed["pe"].sem, 1)
                with pe.Fori(0, FC // 2) as i:
                    for s in range(2):
                        for q in range(2):
                            free = sg_done if q == 0 else prod_done
                            pe.wait_ge(free.sem, free.at(l, i * 2 + (FC * j + s - 1)))
                            pe.wait_ge(w_lo.sem, w_lo.at(l, i * 4 + (first + 2 * s + q + 1)))
                            blocks(ps[:, 2 * q + s, :], q, KC, hH, hL,
                                   arrive=None if s or q else 2 * j * KC).then_inc(w_used.sem, 1)
                if j == 0:
                    mod_vectors(1)
                pe.sem_inc(passed["pe"].sem, 1)
                with pe.Fori(0, KC // 2) as i:
                    for q in range(6):
                        s, part = divmod(q, DN_PER)
                        if part == 0:
                            pe.wait_ge(x_new.sem, x_new.at(l, i * 2 + (3 * KC * j + s - 1)))
                        pe.wait_ge(w_lo.sem, w_lo.at(l, i * 6 + (first + UP_ITEMS + q + 1)))
                        n = min(8, FC - 8 * part)
                        pe.wait_ge(ff_lo.sem, ff_lo.at(l, FC * j + 8 * part + n))
                        blocks(ps[:, 4 + s, :], q % 2, n, ffH, ffL, 8 * part,
                               FC).then_inc(w_used.sem, 1)

            ffn(0, 0)
            f = FF_ITEMS

            def ready(n):
                pe.wait_ge(w_lo.sem, w_lo.at(l, f + n + 1))
                return n % 2

            mod_vectors(2)
            sum_squares(1)
            slot = ready(I_DT)
            for k in range(KC):
                pe.wait_ge(h_lo.sem, h_lo.at(l, KC + k + 1))
                w = slice(k * 2 * HEADS, (k + 1) * 2 * HEADS)
                last = three(ps[0:2 * HEADS, 4, :], wH[slot][:, w], wL[slot][:, w],
                             hH[:, k, :], hL[:, k, :], k == 0, k == KC - 1)
            last.then_inc(w_used.sem, 1)
            for s in range(CCH + 2):
                if s < CCH:
                    if s >= 2:
                        pe.wait_ge(conv.sem, conv.at(l, s - 1))
                    slot = ready(I_CONV + s)
                    blocks(ps[:, s % 2, :], slot, KC, hH, hL).then_inc(w_used.sem, 1)
                if s == 0:
                    pe.wait_ge(dt_cp.sem, dt_cp.at(l, 1))
                    pe.sem_inc(passed["pe"].sem, 1)
                    for t in range(TC):
                        last = pe.transpose(ps[:, 5, t * 2 * HEADS:(t + 1) * 2 * HEADS],
                                            dtf[:, t * P:(t + 1) * P],
                                            ident[0:2 * HEADS, 0:2 * HEADS])
                    last.then_inc(dt_tr.sem, 1)
                if s == 8:
                    pe.wait_ge(a_dt.sem, a_dt.at(l, 1))
                    half = HEADS * TC
                    for d, tri in ((0, triU), (1, triL)):
                        col = slice(d * half, (d + 1) * half)
                        pe.matmul(ps[:, 5, d * half:(d + 1) * half], tri, adt[:, col], start=True, stop=True)
                        pe.matmul(ps[:, 5, P + d * half:P + (d + 1) * half], ones, adt[:, col],
                                  start=True, stop=True)
                    for d, tri in ((0, triU), (1, triL)):
                        for t in range(TC):
                            col = (d * TC + t) * HEADS
                            last = pe.matmul(ps[0:HEADS, 6 + d, t * P:(t + 1) * P],
                                             adt[:, col:col + HEADS], tri, start=True, stop=True)
                    last.then_inc(cs_mm.sem, 1)
                if s - 2 in TR:
                    c = s - 2
                    n = TR.index(c)
                    pe.wait_ge(csilu.sem, csilu.at(l, c + 1))
                    if n >= 2:
                        pe.wait_ge(tev.sem, tev.at(l, n - 1))
                    src = bfm[:, c, :] if c < 2 else xs[:, c % 2, :]
                    for t in range(TC):
                        last = pe.transpose(ps[:, 2 + c % 2, t * P:(t + 1) * P],
                                            src[:, t * P:(t + 1) * P], ident)
                    last.then_inc(trx.sem, 1)
            pe.wait_ge(tev.sem, tev.at(l, len(TR)))
            for g in range(GRP):
                for t in range(TC):
                    tok = slice(t * P, (t + 1) * P)
                    last = pe.matmul(ps[:, 2 + g, tok], bfm[:, g, tok], cfm[:, g, tok],
                                     start=True, stop=True)
            last.then_inc(cb_mm.sem, 1)

            def state(c, n):
                pe.wait_ge(u_w.sem, u_w.at(l, n + 1))
                for g in range(GRP):
                    last = pe.matmul(ps[:, g, :], btok[:, c, g * NST:(g + 1) * NST],
                                     xw[:, g * SEQ:(g + 1) * SEQ], start=True, stop=True)
                last.then_inc(st_mm.sem, 1)

            pe.wait_ge(cs_cp.sem, cs_cp.at(l, 1))
            for z in range(2):
                for q in range(4):
                    slot = ready(I_Z + 4 * z + q)
                    for t in range(TC):
                        tok = slice(t * P, (t + 1) * P)
                        if z and q == 0:
                            pe.wait_ge(z_ev.sem, z_ev.at(l, t + 1))
                        for b in range(2):
                            k = 2 * q + b
                            w = slice(b * SEQ, (b + 1) * SEQ)
                            last = three(ps[:, 4 + t, :], hH[:, k, tok], hL[:, k, tok],
                                         wH[slot][:, w], wL[slot][:, w], k == 0, k == KC - 1)
                    last.then_inc(w_used.sem, 1)
                    n = 4 * z + q - 2
                    if n in (0, 2, 4):
                        if n:
                            pe.wait_ge(st_up.sem, st_up.at(l, n // 2))
                        state(3 - n // 2, n // 2)

            def off_diagonal(c):
                tok = slice(c * P, (c + 1) * P)
                if c:
                    pe.wait_ge(off_rd.sem, off_rd.at(l, c))
                for d in range(2):
                    if c == (TC - 1 if d else 0):
                        continue
                    src = sbk[:, c, :] if d else sf[c - 1][:, :]
                    for g in range(GRP):
                        last = pe.matmul(ps[:, 2 + 2 * d + g, :], cfm[:, g, tok],
                                         src[:, g * SEQ:(g + 1) * SEQ], start=True, stop=True)
                last.then_inc(off_mm.sem, 1)
                if c:
                    pe.wait_ge(part_rd.sem, part_rd.at(l, c))
                pe.wait_ge(skip_x.sem, skip_x.at(l, c + 1))
                for g in range(GRP):
                    pe.matmul(ps[:, g, :], ident, xw[:, g * SEQ:(g + 1) * SEQ],
                              start=True, stop=False)

            def diagonal(c, d):
                pe.wait_ge(x_dt.sem, x_dt.at(l, 2 * c + d + 1))
                pe.wait_ge(m_ok.sem, m_ok.at(l, 2 * c + d + 1))
                for h in range(HEADS):
                    g, col = divmod(h * HD, SEQ)
                    last = pe.matmul(ps[:, g, col:col + HD], dec[:, d, h, :],
                                     xdt[:, d, h * HD:(h + 1) * HD],
                                     start=False, stop=(h % 8 == 7 and d == 1))
                last.then_inc(yd_mm.sem, 1)

            def transposed(c):
                pe.wait_ge(y_nm.sem, y_nm.at(l, 2 * c + 2))
                if c:
                    pe.wait_ge(y_f.sem, y_f.at(l, 2 * c))
                for b in range(2):
                    for k in range(4):
                        col = (4 * b + k) * P
                        last = pe.transpose(ps[:, 6 + b, k * P:(k + 1) * P], yb[:, col:col + P],
                                            ident)
                    last.then_inc(y_tr.sem, 1)

            pe.wait_ge(cb_ok.sem, cb_ok.at(l, 1))
            for q in range(7):
                if q >= 2:
                    pe.wait_ge(q_ev.sem, q_ev.at(l, q - 1))
                slot = ready(I_QA + q)
                blocks(ps[:, 2 + q % 2, :], slot, KC, hH, hL).then_inc(w_used.sem, 1)
                if q < 3:
                    pe.wait_ge(st_up.sem, st_up.at(l, 3 + q))
                    state(q, 3 + q)
                if q == 4:
                    pe.wait_ge(st_up.sem, st_up.at(l, 6))
                    pe.wait_ge(z_ev.sem, z_ev.at(l, 2 * TC))
                    off_diagonal(0)
                    diagonal(0, 0)
                    diagonal(0, 1)
            pe.wait_ge(q_ev.sem, q_ev.at(l, 7))
            for c in range(TC - 1):
                off_diagonal(c + 1)
                diagonal(c + 1, 0)
                transposed(c)
                diagonal(c + 1, 1)
            pe.wait_ge(l_sq.sem, l_sq.at(l, 6))
            token_sums(5, [lsq[:, QC + q, :] for q in range(KVC)]).then_inc(l_sum.sem, 1)
            transposed(TC - 1)
            token_sums(4, [lsq[:, q, :] for q in range(QC)]).then_inc(l_sum.sem, 1)

            def rotate(r):
                pe.wait_ge(rp_in.sem, rp_in.at(l, r + 1))
                pe.matmul(ps[:, 2, :], perm, rt[0][:, :], start=True, stop=True
                          ).then_inc(rp_mm.sem, 1)

            pe.wait_ge(y_lo.sem, y_lo.at(l, 2 * TC))
            for d in range(KC):
                pe.wait_ge(x_new.sem, x_new.at(l, KC + d - 1))
                slot = ready(I_OS + d)
                blocks(ps[:, 6 + d % 2, :], slot, KC, hH, hL).then_inc(w_used.sem, 1)
                if d == 0:
                    for q in range(2):
                        pe.wait_ge(l_rs.sem, l_rs.at(l, q + 1))
                        token_row(5 - q, 1 - q).then_inc(l_row.sem, 1)
                if d == 5:
                    rotate(0)

            pe.wait_ge(l_lo.sem, l_lo.at(l, 6))
            pe.wait_ge(rp_lo.sem, rp_lo.at(l, 1))
            def out_heads(d, h0, h1):
                slot = (I_OA + d) % 2
                for h in range(h0, h1):
                    tile, i = o_place[h]
                    w = slice(h * P, (h + 1) * P)
                    last = three(ps[:, 3 + d % 3, :], wH[slot][:, w], wL[slot][:, w],
                                 oH[tile][:, i, :], oL[tile][:, i, :], h == 0, h == MH - 1)
                return last

            def keys(hg, h):
                slot = (I_MLA + 5 * hg) % 2
                for k in range(KVC):
                    w = slice((k * 4 + h) * P, (k * 4 + h + 1) * P)
                    last = three(ps[:, h, :], wH[slot][:, w], wL[slot][:, w],
                                 ckH[:, k, :], ckL[:, k, :], k == 0, k == KVC - 1)
                return last

            for hg in range(2):
                i0 = I_MLA + 5 * hg
                if hg:
                    pe.wait_ge(a_hi.sem, a_hi.at(l, 4))
                    pe.wait_ge(p_lo.sem, p_lo.at(l, SOFT))
                    last = keys(1, 2)
                else:
                    ready(i0)
                    for h in range(4):
                        last = keys(0, h)
                last.then_inc(w_used.sem, 1)
                slot = ready(i0 + 1)
                if hg == 0:
                    pe.wait_ge(x_new.sem, x_new.at(l, 2 * KC))
                for t in range(TC):
                    tok = slice(t * P, (t + 1) * P)
                    for k in range(KVC):
                        w = slice(k * SEQ, (k + 1) * SEQ)
                        last = three(ps[:, 4 + t, :], ckH[:, k, tok], ckL[:, k, tok],
                                     wH[slot][:, w], wL[slot][:, w], k == 0, k == KVC - 1)
                last.then_inc(w_used.sem, 1)
                pe.wait_ge(k_lo.sem, k_lo.at(l, 4 * hg + 4))
                slot = ready(i0 + 2)
                for p in range(2):
                    last = blocks(ps[:, p, :], slot, QC, qaH, qaL, last=QC, width=2 * P, off=p * P)
                last.then_inc(w_used.sem, 1)
                pe.wait_ge(v_lo.sem, v_lo.at(l, 4 * hg + 4))
                for p in range(2):
                    slot = ready(i0 + 3 + p)
                    for h in range(2):
                        last = blocks(ps[:, 3 + 2 * p + h, :], slot, QC, qaH, qaL, last=QC,
                                      width=2 * P, off=h * P)
                    last.then_inc(w_used.sem, 1)
                    rotate(1 + 2 * hg + p)
                pe.wait_ge(rp_lo.sem, rp_lo.at(l, 2 + 2 * hg))
                pe.wait_ge(qn_lo.sem, qn_lo.at(l, 4 * hg + 4))
                for s in range(SOFT + 4):
                    n = SOFT * hg + s
                    if s == 2:
                        pe.wait_ge(rp_lo.sem, rp_lo.at(l, 3 + 2 * hg))
                    if hg == 0 and s == SOFT:
                        ready(i0 + 5)
                        for h in range(2):
                            keys(1, h)
                    if hg == 0 and s == SOFT + 1:
                        pe.wait_ge(s_ex.sem, s_ex.at(l, SOFT))
                        keys(1, 3)
                    if s < SOFT:
                        h, t = divmod(s, TC)
                        tok = slice(t * P, (t + 1) * P)
                        bank = ps[:, 3 + n % 3, :]
                        if n >= 3:
                            pe.wait_ge(s_ex.sem, s_ex.at(l, n - 2))
                        three(bank, qnH[:, h, tok], qnL[:, h, tok], kH[:, h, :], kL[:, h, :],
                              True, False)
                        r = slice((h % 2) * ROPE, (h % 2 + 1) * ROPE)
                        three(bank, qrH[r, h // 2, tok], qrL[r, h // 2, tok], krH[r, :],
                              krL[r, :], False, True).then_inc(s_mm.sem, 1)
                    if hg and s == SOFT + 3:
                        pe.wait_ge(a_lo.sem, a_lo.at(l, MH - 1))
                        pe.wait_ge(s_ex.sem, s_ex.at(l, 2 * SOFT))
                        ready(I_OA)
                        out_heads(0, 0, MH - 1)
                    if s > 3 and (s - 3) % TC == 0:
                        h = (n - 3) // TC - 1
                        pe.wait_ge(p_lo.sem, p_lo.at(l, n - 3))
                        if h:
                            pe.wait_ge(a_hi.sem, a_hi.at(l, h))
                        col = slice((h % 4) * VD, (h % 4 + 1) * VD)
                        for k in range(TC):
                            last = three(ps[:, 2, :], vH[:, k, col], vL[:, k, col],
                                         ptH[:, k, :], ptL[:, k, :], k == 0, k == TC - 1)
                        last.then_inc(o_mm.sem, 1)
                    if 3 <= s < SOFT + 3:
                        m = n - 3
                        pe.wait_ge(s_nm.sem, s_nm.at(l, m + 1))
                        if m >= 2:
                            pe.wait_ge(p_lo.sem, p_lo.at(l, m - 1))
                        for k in range(TC):
                            last = pe.transpose(ps[:, 6 + m % 2, k * P:(k + 1) * P],
                                                pr[:, m % 4, k * P:(k + 1) * P], ident)
                        last.then_inc(p_tr.sem, 1)
            for d in range(KC):
                if d:
                    ready(I_OA + d)
                if d >= 3:
                    pe.wait_ge(x_new.sem, x_new.at(l, 2 * KC + d - 2))
                pe.wait_ge(a_lo.sem, a_lo.at(l, MH))
                out_heads(d, 0 if d else MH - 1, MH).then_inc(w_used.sem, 1)
                if d == 0:
                    pe.wait_ge(a_add.sem, a_add.at(l, MH - 1))
                    token_sums(6, [asum[:, :]]).then_inc(a_sum.sem, 1)
                if d == 1:
                    pe.wait_ge(a_rs.sem, a_rs.at(l, 1))
                    token_row(6, 0).then_inc(a_row.sem, 1)
            ffn(1, FF_ITEMS + MX_ITEMS)

        pe.wait_ge(sq_add.sem, sq_add.at(DEPTH, 0))
        token_sums(6, [sqs[:, :]]).then_inc(f_sum.sem, 1)
        pe.wait_ge(f_rs.sem, 1)
        token_row(6, 0).then_inc(f_row.sem, 1)



def chunks(v, n):
    return np.swapaxes(v.reshape(v.shape[:-1] + (n, P)), -1, -2)


def blocks_of(w, cols):
    w = w[:, cols]
    return np.transpose(w.reshape(-1, P, w.shape[1]), (1, 0, 2)).reshape(P, -1)


def padded(a):
    out = np.zeros((P, ITEM), a.dtype)
    out[:, :a.shape[1]] = a
    return out


def up_items(g, u):
    out = []
    for f in range(FC):
        for w in (g, u):
            out.append(blocks_of(w, slice(f * P, (f + 1) * P)))
    return out


def down_items(w):
    out = []
    for d in range(KC):
        b = blocks_of(w, slice(d * P, (d + 1) * P))
        out += [padded(b[:, q * ITEM:(q + 1) * ITEM]) for q in range(DN_PER)]
    return out


def mixer_items(w_in, w_q, w_kv, w_out):
    xbc0 = DM
    dt0 = xbc0 + DM + 2 * GRP * NST
    qa0 = dt0 + 2 * HEADS
    kv0 = qa0 + QL
    items = [padded(blocks_of(w_in, slice(dt0, dt0 + 2 * HEADS)))]
    for c in list(range(KC, CCH)) + list(range(KC)):
        items.append(blocks_of(w_in, slice(xbc0 + c * P, xbc0 + (c + 1) * P)))
    for z in range(2):
        b = blocks_of(w_in, slice(z * SEQ, (z + 1) * SEQ))
        items += [b[:, q * ITEM:(q + 1) * ITEM] for q in range(4)]
    for c in range(QC):
        items.append(blocks_of(w_in, slice(qa0 + c * P, qa0 + (c + 1) * P)))
    for c in range(KVC):
        items.append(blocks_of(w_in, slice(kv0 + c * P, kv0 + (c + 1) * P)))
    kr = np.arange(kv0 + KVL, kv0 + KVL + ROPE)
    items.append(blocks_of(w_in, np.concatenate([kr, kr])))
    for d in range(KC):
        items.append(blocks_of(w_out[:DM], slice(d * P, (d + 1) * P)))
    for hg in range(2):
        hs = range(4 * hg, 4 * hg + 4)
        k = np.concatenate([np.arange(h * 256, h * 256 + NOPE) for h in hs])
        q = np.concatenate([np.arange(h * 192, h * 192 + NOPE) for h in hs])
        r = np.concatenate([np.arange(h * 192 + NOPE, (h + 1) * 192) for h in hs])
        items.append(blocks_of(w_kv, k))
        items.append(blocks_of(w_kv, k + NOPE))
        items.append(blocks_of(w_q, r))
        items += [blocks_of(w_q, q[:2 * P]), blocks_of(w_q, q[2 * P:])]
    for d in range(KC):
        items.append(blocks_of(w_out[DM:], slice(d * P, (d + 1) * P)))
    assert len(items) == MX_ITEMS
    return items


def kernel(**inputs):
    import concourse.bacc as _bacc
    from concourse.bass_utils import run_bass_kernel_spmd as _run

    a = {k: np.asarray(v) for k, v in inputs.items()}
    row = np.arange(P)
    le = (row[:, None] <= row[None, :]).astype(np.float32)
    turn = np.zeros((P, P), np.float32)
    for m in range(P):
        first = m % ROPE < ROPE // 2
        turn[m + (ROPE // 2 if first else -(ROPE // 2)), m] = -1.0 if first else 1.0
    consts = np.stack([le, le.T, np.ones((P, P), np.float32), np.eye(P, dtype=np.float32), turn], 1)
    power = (np.arange(0, ROPE, 2, dtype=np.float32) / ROPE).astype(np.float32)
    inv = (np.float32(1.0) / np.power(np.float32(THETA), power)).astype(np.float32)
    invf = inv[row % (ROPE // 2)][:, None]

    def wide(v):
        return np.broadcast_to(v.reshape(1, -1), (P, v.size))

    params = []
    order = list(range(KC, CCH)) + list(range(KC))
    for l in range(DEPTH):
        cw = np.transpose(a["conv_w"][l].reshape(KSZ, CCH, P)[:, order], (2, 1, 0)).reshape(P, -1)
        params.append(np.concatenate([
            cw, chunks(a["conv_b"][l], CCH)[:, order],
            np.transpose(chunks(a["norm_g"][l], KC), (1, 0, 2)).reshape(P, -1),
            chunks(a["ssd_norm_g"][l], KC), chunks(a["q_norm_g"][l], QC),
            chunks(a["kv_norm_g"][l], KVC), chunks(a["attn_norm_g"][l], KC),
            chunks(a["ada_b"][l], 72),
            wide(a["dt_bias"][l]), wide(a["a_log"][l]), wide(a["d_skip"][l])], axis=1))
    w_up, w_dn, w_mx = [], [], []
    for l in range(DEPTH):
        for j in range(2):
            w_up += up_items(a["ffn_w_gate"][l, j], a["ffn_w_up"][l, j])
            w_dn += down_items(a["ffn_w_down"][l, j])
        w_mx += mixer_items(a["w_in"][l], a["w_q_b"][l], a["w_kv_b"][l], a["w_out"][l])
    ada = a["ada_w"].reshape(DEPTH, KC, P, 3, 3, DM).transpose(0, 3, 1, 4, 2, 5)
    arrays = {
        "xT": np.transpose(a["x"][0].reshape(SEQ, KC, P), (2, 1, 0)),
        "cT": chunks(a["c"][0], KC),
        "pos": a["positions"].astype(np.int32, copy=False).reshape(1, SEQ),
        "invf": invf, "consts": consts, "params": np.stack(params),
        "finalg": chunks(a["final_norm_g"], KC),
        "w_up": np.stack(w_up), "w_dn": np.stack(w_dn), "w_mx": np.stack(w_mx),
        "w_ada": ada.reshape(DEPTH * 3 * ADA_Q, P, DM),
    }
    arrays = {k: np.ascontiguousarray(v) for k, v in arrays.items()}
    nc = _bacc.Bacc("TRN2", target_bir_lowering=False, num_devices=1)
    args = [nc.dram_tensor(n, v.shape, mybir.dt.from_np(v.dtype), kind="ExternalInput").ap()
            for n, v in arrays.items()]
    out = nc.dram_tensor("out", (P, KC, SEQ), F32, kind="ExternalOutput").ap()
    build_trunk(nc, *args, out)
    r = _run(nc, [arrays], core_ids=[0])
    got = r.results[0]["out"]
    return np.ascontiguousarray(np.transpose(got, (2, 1, 0)).reshape(1, SEQ, DM))
```
